# Optimizing a Trainium2 kernel written in Bass

```python
import jax, jax.numpy as jnp
from jax import lax
import numpy as np

D_MODEL = 1024
BATCH = 1
SEQ = 256
DEPTH = 2

N_MIXERS = 2
CHUNK = 64
EPS = 1e-6

ML_HEADS = 4
ML_DQK = 128
ML_DV = 256
ML_QK_W = ML_HEADS * ML_DQK
ML_V_W = ML_HEADS * ML_DV
ML_IN_W = 2 * ML_QK_W + 2 * ML_V_W + 2 * ML_HEADS

GD_HEADS = 8
GD_DK = 128
GD_DV = 128
GD_K_W = GD_HEADS * GD_DK
GD_V_W = GD_HEADS * GD_DV
GD_CONV_C = 2 * GD_K_W + GD_V_W
GD_CONV_K = 4
GD_IN_W = GD_CONV_C + GD_V_W + 2 * GD_HEADS

D_FF = 3584
N_EXPERTS = 8
TOP_K = 2
D_FF_EXPERT = 3584

kernel_name = 'hybrid_mlstm_gdn_moe_trunk'

def rms_norm(x, g):
    xf = x.astype(jnp.float32)
    y = xf * lax.rsqrt(jnp.mean(xf * xf, axis=-1, keepdims=True) + EPS)
    return (y * g.astype(jnp.float32)).astype(x.dtype)

def to_chunks(t):
    b, h, s = t.shape[:3]
    t = t.reshape(b, h, s // CHUNK, CHUNK, *t.shape[3:])
    return jnp.moveaxis(t, 2, 0)

def from_chunks(t):
    t = jnp.moveaxis(t, 0, 2)
    return t.reshape(t.shape[0], t.shape[1], -1, *t.shape[4:])

def mlstm_mixer(h, w_in, b_if, head_gain, w_out):
    bsz, s, _ = h.shape
    f32 = jnp.float32
    p = (h @ w_in).astype(f32)
    q, k, v, o, gates = jnp.split(
        p, [ML_QK_W, 2 * ML_QK_W, 2 * ML_QK_W + ML_V_W, 2 * ML_QK_W + 2 * ML_V_W], axis=-1)
    heads = lambda t, d: t.reshape(bsz, s, ML_HEADS, d).transpose(0, 2, 1, 3)
    q = heads(q, ML_DQK)
    k = heads(k, ML_DQK) * (ML_DQK ** -0.5)
    v = heads(v, ML_DV)
    gates = (gates + b_if.astype(f32)).transpose(0, 2, 1)
    log_i = gates[:, :ML_HEADS]
    log_f = jax.nn.log_sigmoid(gates[:, ML_HEADS:])
    causal = jnp.tril(jnp.ones((CHUNK, CHUNK), dtype=bool))

    def step(carry, inp):
        C, n, m = carry
        qc, kc, vc, ic, fc = inp
        b = jnp.cumsum(fc, axis=-1)
        d = jnp.where(causal, b[..., :, None] - b[..., None, :] + ic[..., None, :], -jnp.inf)
        m_inter = b + m[..., None]
        m_t = jnp.maximum(jnp.max(d, axis=-1), m_inter)
        w = jnp.exp(d - m_t[..., None])
        sc = jnp.einsum('bhtd,bhsd->bhts', qc, kc) * w
        a = jnp.exp(m_inter - m_t)
        num = jnp.einsum('bhts,bhsv->bhtv', sc, vc) + a[..., None] * jnp.einsum('bhtd,bhdv->bhtv', qc, C)
        den = jnp.sum(sc, axis=-1) + a * jnp.einsum('bhtd,bhd->bht', qc, n)
        hc = num / jnp.maximum(jnp.abs(den), jnp.exp(-m_t))[..., None]
        b_last = b[..., -1]
        d_last = b_last[..., None] - b + ic
        m_new = jnp.maximum(b_last + m, jnp.max(d_last, axis=-1))
        ws = jnp.exp(d_last - m_new[..., None])
        decay = jnp.exp(b_last + m - m_new)
        C = decay[..., None, None] * C + jnp.einsum('bhs,bhsd,bhsv->bhdv', ws, kc, vc)
        n = decay[..., None] * n + jnp.einsum('bhs,bhsd->bhd', ws, kc)
        return (C, n, m_new), hc

    init = (jnp.zeros((bsz, ML_HEADS, ML_DQK, ML_DV), f32),
            jnp.zeros((bsz, ML_HEADS, ML_DQK), f32),
            jnp.zeros((bsz, ML_HEADS), f32))
    _, hs = lax.scan(step, init, (to_chunks(q), to_chunks(k), to_chunks(v),
                                  to_chunks(log_i), to_chunks(log_f)))
    hs = from_chunks(hs)
    hs = hs * lax.rsqrt(jnp.mean(hs * hs, axis=-1, keepdims=True) + EPS)
    hs = hs * head_gain.astype(f32).reshape(ML_HEADS, 1, ML_DV)
    hs = hs.transpose(0, 2, 1, 3).reshape(bsz, s, ML_V_W) * jax.nn.sigmoid(o)
    return hs.astype(h.dtype) @ w_out

def l2_normalize(t):
    return t * lax.rsqrt(jnp.sum(t * t, axis=-1, keepdims=True) + EPS)

def gdn_mixer(h, w_in, conv_w, a_log, dt_bias, out_gain, w_out):
    bsz, s, _ = h.shape
    f32 = jnp.float32
    p = h @ w_in
    qkv, z, b_raw, a_raw = jnp.split(
        p, [GD_CONV_C, GD_CONV_C + GD_V_W, GD_CONV_C + GD_V_W + GD_HEADS], axis=-1)
    qkv = lax.conv_general_dilated(
        qkv, conv_w[:, None, :].astype(qkv.dtype), window_strides=(1,),
        padding=[(GD_CONV_K - 1, 0)], dimension_numbers=('NWC', 'WIO', 'NWC'),
        feature_group_count=GD_CONV_C)
    qkv = jax.nn.silu(qkv.astype(f32))
    q, k, v = jnp.split(qkv, [GD_K_W, 2 * GD_K_W], axis=-1)
    heads = lambda t, d: t.reshape(bsz, s, GD_HEADS, d).transpose(0, 2, 1, 3)
    q = l2_normalize(heads(q, GD_DK)) * (GD_DK ** -0.5)
    k = l2_normalize(heads(k, GD_DK))
    v = heads(v, GD_DV)
    beta = jax.nn.sigmoid(b_raw.astype(f32)).transpose(0, 2, 1)
    g = -(jnp.exp(a_log.astype(f32)) *
          jax.nn.softplus(a_raw.astype(f32) + dt_bias.astype(f32))).transpose(0, 2, 1)

    qc, kc, vc = to_chunks(q), to_chunks(k), to_chunks(v)
    betac = to_chunks(beta)[..., None]
    gc = jnp.cumsum(to_chunks(g), axis=-1)
    causal = jnp.tril(jnp.ones((CHUNK, CHUNK), dtype=bool))
    strict = jnp.tril(jnp.ones((CHUNK, CHUNK), dtype=bool), -1)
    diff = gc[..., :, None] - gc[..., None, :]
    gamma = jnp.where(causal, jnp.exp(jnp.where(causal, diff, 0.0)), 0.0)
    kb = kc * betac
    A = jnp.where(strict, jnp.einsum('nbhtd,nbhsd->nbhts', kb, kc) * gamma, 0.0)
    u = lax.linalg.triangular_solve(A, vc * betac, left_side=True, lower=True, unit_diagonal=True)
    w = lax.linalg.triangular_solve(A, kb * jnp.exp(gc)[..., None], left_side=True, lower=True,
                                    unit_diagonal=True)
    attn = jnp.einsum('nbhtd,nbhsd->nbhts', qc, kc) * gamma
    qg = qc * jnp.exp(gc)[..., None]
    g_last = gc[..., -1]
    kdec = kc * jnp.exp(g_last[..., None] - gc)[..., None]

    def step(state, inp):
        qg_, attn_, u_, w_, kdec_, gl_ = inp
        v_new = u_ - jnp.einsum('bhtk,bhkv->bhtv', w_, state)
        o = jnp.einsum('bhtk,bhkv->bhtv', qg_, state) + jnp.einsum('bhts,bhsv->bhtv', attn_, v_new)
        state = jnp.exp(gl_)[..., None, None] * state + jnp.einsum('bhsk,bhsv->bhkv', kdec_, v_new)
        return state, o

    init = jnp.zeros((bsz, GD_HEADS, GD_DK, GD_DV), f32)
    _, os_ = lax.scan(step, init, (qg, attn, u, w, kdec, g_last))
    o = from_chunks(os_)
    o = o * lax.rsqrt(jnp.mean(o * o, axis=-1, keepdims=True) + EPS) * out_gain.astype(f32)
    o = o.transpose(0, 2, 1, 3).reshape(bsz, s, GD_V_W) * jax.nn.silu(z.astype(f32))
    return o.astype(h.dtype) @ w_out

def swiglu(h, w_gate, w_up, w_down):
    return (jax.nn.silu(h @ w_gate) * (h @ w_up)) @ w_down

def moe_ffn(h, router, w_gate, w_up, w_down):
    bsz, s, d = h.shape
    t = h.reshape(-1, d)
    logits = (t @ router).astype(jnp.float32)
    top_v, top_i = lax.top_k(logits, TOP_K)
    top_w = jax.nn.softmax(top_v, axis=-1)
    gates = jnp.sum(jax.nn.one_hot(top_i, N_EXPERTS, dtype=jnp.float32) * top_w[..., None], axis=1)
    y = jnp.zeros(t.shape, jnp.float32)
    for e in range(N_EXPERTS):
        y = y + gates[:, e:e + 1] * swiglu(t, w_gate[e], w_up[e], w_down[e]).astype(jnp.float32)
    return y.astype(h.dtype).reshape(bsz, s, d)

def setup_inputs(seed: int = 0) -> dict:
    key = jax.random.key(seed)
    ks = list(jax.random.split(key, 32))
    nrm = lambda k, shape, fan_in: jax.random.normal(k, shape, jnp.float32) * (fan_in ** -0.5)
    gain = lambda k, n: 1.0 + 0.02 * jax.random.normal(k, (n,), jnp.float32)
    b_if = jnp.concatenate([
        0.1 * jax.random.normal(ks[3], (ML_HEADS,), jnp.float32),
        3.0 + 0.5 * jax.random.normal(ks[4], (ML_HEADS,), jnp.float32)])
    a_log = jnp.log(jax.random.uniform(ks[14], (GD_HEADS,), jnp.float32, 1.0, 16.0))
    dt = jnp.exp(jax.random.uniform(ks[15], (GD_HEADS,), jnp.float32, np.log(1e-3), np.log(1e-1)))
    dt_bias = dt + jnp.log(-jnp.expm1(-dt))
    return {
        'x': jax.random.normal(ks[0], (BATCH, SEQ, D_MODEL), jnp.float32),
        'l0_norm_mix': gain(ks[1], D_MODEL),
        'l0_ml_w_in': nrm(ks[2], (D_MODEL, ML_IN_W), D_MODEL),
        'l0_ml_b_if': b_if,
        'l0_ml_head_gain': gain(ks[5], ML_V_W),
        'l0_ml_w_out': nrm(ks[6], (ML_V_W, D_MODEL), ML_V_W),
        'l0_norm_ffn': gain(ks[7], D_MODEL),
        'l0_ffn_w_gate': nrm(ks[8], (D_MODEL, D_FF), D_MODEL),
        'l0_ffn_w_up': nrm(ks[9], (D_MODEL, D_FF), D_MODEL),
        'l0_ffn_w_down': nrm(ks[10], (D_FF, D_MODEL), D_FF),
        'l1_norm_mix': gain(ks[11], D_MODEL),
        'l1_gdn_w_in': nrm(ks[12], (D_MODEL, GD_IN_W), D_MODEL),
        'l1_gdn_conv': nrm(ks[13], (GD_CONV_K, GD_CONV_C), GD_CONV_K),
        'l1_gdn_a_log': a_log,
        'l1_gdn_dt_bias': dt_bias,
        'l1_gdn_out_gain': gain(ks[16], GD_DV),
        'l1_gdn_w_out': nrm(ks[17], (GD_V_W, D_MODEL), GD_V_W),
        'l1_norm_ffn': gain(ks[18], D_MODEL),
        'l1_moe_router': nrm(ks[19], (D_MODEL, N_EXPERTS), D_MODEL),
        'l1_moe_w_gate': nrm(ks[20], (N_EXPERTS, D_MODEL, D_FF_EXPERT), D_MODEL),
        'l1_moe_w_up': nrm(ks[21], (N_EXPERTS, D_MODEL, D_FF_EXPERT), D_MODEL),
        'l1_moe_w_down': nrm(ks[22], (N_EXPERTS, D_FF_EXPERT, D_MODEL), D_FF_EXPERT),
        'final_norm': gain(ks[23], D_MODEL),
    }

def reference(x, l0_norm_mix, l0_ml_w_in, l0_ml_b_if, l0_ml_head_gain, l0_ml_w_out,
              l0_norm_ffn, l0_ffn_w_gate, l0_ffn_w_up, l0_ffn_w_down,
              l1_norm_mix, l1_gdn_w_in, l1_gdn_conv, l1_gdn_a_log, l1_gdn_dt_bias,
              l1_gdn_out_gain, l1_gdn_w_out, l1_norm_ffn, l1_moe_router,
              l1_moe_w_gate, l1_moe_w_up, l1_moe_w_down, final_norm):
    mixers = [
        lambda h: mlstm_mixer(h, l0_ml_w_in, l0_ml_b_if, l0_ml_head_gain, l0_ml_w_out),
        lambda h: gdn_mixer(h, l1_gdn_w_in, l1_gdn_conv, l1_gdn_a_log, l1_gdn_dt_bias,
                            l1_gdn_out_gain, l1_gdn_w_out),
    ]
    ffns = [
        lambda h: swiglu(h, l0_ffn_w_gate, l0_ffn_w_up, l0_ffn_w_down),
        lambda h: moe_ffn(h, l1_moe_router, l1_moe_w_gate, l1_moe_w_up, l1_moe_w_down),
    ]
    norms_mix = [l0_norm_mix, l1_norm_mix]
    norms_ffn = [l0_norm_ffn, l1_norm_ffn]
    for i in range(DEPTH):
        x = x + mixers[i % N_MIXERS](rms_norm(x, norms_mix[i]))
        x = x + ffns[i % 2](rms_norm(x, norms_ffn[i]))
    return rms_norm(x, final_norm)


_drawn_inputs = setup_inputs


def setup_inputs(seed=0):
    import zlib

    import numpy as np

    out = dict(_drawn_inputs(seed))
    spreads = {}
    factors = {'l1_gdn_out_gain': 2.903, 'final_norm': 8.454, 'l1_norm_ffn': 2.936}
    for name, (base, spread) in spreads.items():
        noise = np.random.default_rng([zlib.crc32(name.encode()), seed]).standard_normal(out[name].shape)
        drawn = base * np.exp(spread * noise) if base else spread * noise
        out[name] = __import__('jax').numpy.asarray(drawn.astype(out[name].dtype))
    for name, factor in factors.items():
        out[name] = (out[name] * factor).astype(out[name].dtype)
    return out
```

```python
from contextlib import ExitStack

import concourse.bass as bass
from concourse import mybir

P = 128
S = 256
TC = S // P
D = 1024
DC = D // P
EPS = 1e-6

ML_H, ML_DQK, ML_DV = 4, 128, 256
GD_H, GD_DK, GD_DV, GD_K = 8, 128, 128, 4
FF = 3584
NE = 8
CAP = 96
ROUNDS = -(-S // CAP)

SLAB = 512
SLOTS = 7
FJ = FF // SLAB
FC = SLAB // P
NEG = -1e30

F32 = mybir.dt.float32
I32 = mybir.dt.int32
U8 = mybir.dt.uint8
ALU = mybir.AluOpType
ACT = mybir.ActivationFunctionType
AX = mybir.AxisListType


def bass_hybrid_trunk(nc, out, w):
    ctx = ExitStack()
    with ctx:
        def sb(name, shape, dt=F32):
            return ctx.enter_context(nc.sbuf_tensor(name, shape, dt))

        def sem(name):
            return ctx.enter_context(nc.semaphore(name))

        ring = sb("ring", [P, SLOTS, DC * SLAB])
        x = sb("x", [P, TC, D])
        xn = sb("xn", [P, TC, D])
        hT = sb("hT", [P, DC, S])
        area = sb("area", [P, 15424])

        ident = sb("ident", [P, P])
        ones = sb("ones", [P, P])
        incl = sb("incl", [P, P])
        strict = sb("strict", [P, P])
        neg = sb("neg", [P, 2, TC, P])
        low = sb("low", [P, 7, P], U8)
        upp = sb("upp", [P, 7, P], U8)
        iot = sb("iot", [P, P])
        mhalf = sb("mhalf", [P, 16])
        gains = sb("gains", [P, 5 * DC + 1])
        taps = sb("taps", [P, GD_K, 24])
        w_if = sb("w_if", [P, DC, 2 * ML_H])
        w_ba = sb("w_ba", [P, DC, 2 * GD_H])
        w_rt = sb("w_rt", [P, DC, NE])
        bif = sb("bif", [P, 2 * ML_H])
        dtb = sb("dtb", [P, GD_H])
        alog = sb("alog", [P, GD_H])
        ss = sb("ss", [P, 8, 16])
        va = sb("va", [P, 8, 16])
        rs = sb("rs", [P, 8, 16])
        sm = sb("sm", [P, 24, 16])
        den = sb("den", [P, 2, 8])
        nrounds = sb("nrounds", [1, 1], I32)

        def view(at, n, pat=None, **kw):
            v = area[:, at:at + n]
            return v.rearrange(pat, **kw) if pat else v

        packG = view(0, 128)
        packT = view(128, 128)
        xorI = view(256, 3 * 128).bitcast(I32).rearrange("p (a n) -> p a n", a=3)
        xorF = view(640, 4 * 128, "p (a n) -> p a n", a=4)
        mq = view(0, 1024, "p (h t) -> p h t", h=ML_H)
        mk = view(1024, 1024, "p (h t) -> p h t", h=ML_H)
        mv = view(2048, TC * ML_H * 257, "p (c h n) -> p c h n", c=TC, h=ML_H)
        mog = view(4104, 2048, "p (c n) -> p c n", c=TC)
        mw = view(6152, 2 * 384, "p (b n) -> p b n", b=2)
        msc = view(6920, 2 * 384, "p (b n) -> p b n", b=2)
        mrow = view(7688, 3 * S, "p (a n) -> p a n", a=3)
        msq = view(8456, 256)
        fsg = view(0, 1024, "p (a t) -> p a t", a=FC)
        fhh = view(1024, 2048, "p (b a t) -> p b a t", b=2, a=FC)
        gq = view(0, 2048, "p (h t) -> p h t", h=GD_H)
        gk = view(2048, 2048, "p (h t) -> p h t", h=GD_H)
        gv = view(4096, 2048, "p (h t) -> p h t", h=GD_H)
        gz = view(6144, 2048, "p (c n) -> p c n", c=TC)
        RW = S + GD_K - 1
        graw = view(8192, 8 * RW, "p (b a n) -> p b a n", b=2, a=4)
        kbg = view(8192, 1024, "p (h d) -> p h d", h=GD_H)
        kdec = view(9216, 1024, "p (h d) -> p h d", h=GD_H)
        nAT = view(10304, 2048, "p (c h t) -> p c h t", c=TC, h=GD_H)
        attT = view(12352, 2048, "p (c h t) -> p c h t", c=TC, h=GD_H)
        rsq = view(10304, 4096, "p (h t) -> p h t", h=2 * GD_H)
        gam = view(14400, 1024, "p (b a c t) -> p b a c t", b=2, a=2, c=TC)
        vb = view(4096, 2048, "p (c h d) -> p c h d", c=TC, h=GD_H)
        xs = view(2048, 2048, "p (g h t) -> p g h t", g=4, h=4)
        nwT = view(2048, 1024, "p (h t) -> p h t", h=GD_H)
        st1 = view(3072, 1024, "p (h t) -> p h t", h=GD_H)
        vn = view(10304, 2048, "p (c h d) -> p c h d", c=TC, h=GD_H)
        osq = view(12352, 2048, "p (g d) -> p g d", g=16)
        grow = view(14400, 512, "p (a t) -> p a t", a=2)
        rows2 = sb("rows2", [GD_H, 2, S])
        sqb = xn[:, :, :].rearrange("p b (h t) -> p b h t", h=4)
        Tn = xn[:, :, :].rearrange("p c (h t) -> p c h t", h=GD_H)
        Tt = hT[:, :, :].rearrange("p a b -> p (a b)").rearrange("p (c h t) -> p c h t", c=TC, h=GD_H)
        eP = view(0, TC * CAP, "p (c n) -> p c n", c=TC)
        ePG = view(256, TC * CAP, "p (c n) -> p c n", c=TC)
        eGT = view(512, S)
        exg = view(768, DC * CAP, "p (c n) -> p c n", c=DC)
        esg = view(1792, 2 * FC * CAP, "p (b a n) -> p b a n", b=2, a=FC)
        ehh = view(2816, 2 * FC * CAP, "p (b a n) -> p b a n", b=2, a=FC)
        eyT = view(3840, DC * CAP, "p (c n) -> p c n", c=DC)
        eyg = view(4864, D)
        fgain = view(6144, D)
        fout = view(7168, 2 * D, "p (c n) -> p c n", c=TC)
        tok9 = view(9216, 2 * TC * 9, "p (a c n) -> p a c n", a=2, c=TC)
        posm, gate9 = tok9[:, 0], tok9[:, 1]
        rt = view(9280, 16 * 16, "p (a n) -> p a n", a=16)

        bank = [ctx.enter_context(nc.psum_tensor(f"bank{i}", [P, 512], F32)) for i in range(8)]

        def b2(i, n=2):
            return bank[i][:, :].rearrange("p (a t) -> p a t", a=n)

        x_in = sem("x_in")
        par_in = sem("par_in")
        landed = [sem(f"landed{i}") for i in range(SLOTS)]
        slab_half = sem("slab_half")
        slab_used = sem("slab_used")
        pool_step = sem("pool_step")
        consts = sem("consts")
        dve_step = sem("dve_step")
        act_step = sem("act_step")
        masks = sem("masks")
        pack_t = sem("pack_t")
        pack_e = sem("pack_e")
        sq_sum = [sem(f"sq_sum{i}") for i in range(7)]
        var_ok = [sem(f"var_ok{i}") for i in range(7)]
        rs_ok = [sem(f"rs_ok{i}") for i in range(7)]
        xn_ok = [sem(f"xn_ok{i}") for i in range(6)]
        tr_ok = [sem(f"tr_ok{i}") for i in range(6)]
        hT_ok = [sem(f"hT_ok{i}") for i in range(6)]
        ev0, ev0v = sem("ev0"), sem("ev0v")
        g0_pe, g0_dve, g0_act = sem("g0_pe"), sem("g0_dve"), sem("g0_act")
        h_bc, h_w, h_qk, h_sc, h_num, h_hs = [sem(n) for n in ("h_bc", "h_w", "h_qk", "h_sc", "h_num", "h_hs")]
        res = [sem(f"res{i}") for i in range(3)]
        f_silu, f_hh = sem("f_silu"), sem("f_hh")
        ev1 = sem("ev1")
        conv_ok, silu_ok, sqr_ok, ssq_pe, ssq_ev, ln_ok, qk_ok = [sem(n) for n in (
            "conv_ok", "silu_ok", "sqr_ok", "ssq_pe", "ssq_ev", "ln_ok", "qk_ok")]
        g1_pe, g1_dve, g1_act = sem("g1_pe"), sem("g1_dve"), sem("g1_act")
        kv_t, kv_ev = sem("kv_t"), sem("kv_ev")
        bc_ok, gam_ok, kq_ok, att_ok = sem("bc_ok"), sem("gam_ok"), sem("kq_ok"), sem("att_ok")
        inv_x, inv_xs, inv_d, inv_t = sem("inv_x"), sem("inv_xs"), sem("inv_d"), sem("inv_t")
        s_pe, s_act, s_dve = sem("s_pe"), sem("s_act"), sem("s_dve")
        r_pe, r_dve, r_act, routed = sem("r_pe"), sem("r_dve"), sem("r_act"), sem("routed")
        e_sel, e_gather, e_xg, e_gt, e_silu, e_hh, e_yT, e_tr, e_yg, e_sc, e_x = [sem(n) for n in (
            "e_sel", "e_gather", "e_xg", "e_gt", "e_silu", "e_hh", "e_yT", "e_tr", "e_yg", "e_sc", "e_x")]
        e_own = sem("e_own")
        fin_ok = sem("fin_ok")
        stored = sem("stored")

        def cols(m, a):
            return m[:, a:a + SLAB].rearrange("(c p) n -> p c n", p=P)

        def rows(m, a):
            return m[a:a + SLAB, :].rearrange("(c p) n -> p c n", p=P)

        slabs = [cols(w["l0_ml_w_in"], SLAB * i) for i in range(6)]
        slabs += [cols(w["l0_ml_w_out"], SLAB * i) for i in range(2)]
        FFN0 = len(slabs)
        for j in range(FJ):
            slabs += [cols(w["l0_ffn_w_gate"], SLAB * j), cols(w["l0_ffn_w_up"], SLAB * j),
                      rows(w["l0_ffn_w_down"], SLAB * j)]
        GDN0 = len(slabs)
        slabs += [cols(w["l1_gdn_w_in"], SLAB * i) for i in range(8)]
        slabs += [cols(w["l1_gdn_w_out"], SLAB * i) for i in range(2)]
        MOE0 = len(slabs)
        PER = 3 * FJ
        order = []
        for j in range(FJ + 1):
            if j < FJ:
                order += [("gate", j), ("up", j)]
            if j > 0:
                order += [("down", j - 1)]
        place = {key: m for m, key in enumerate(order)}

        def slab_at(k):
            s = ring[:, k % SLOTS, :]
            return s.rearrange("p (c n) -> p c n", c=DC), s.rearrange("p (c n) -> p c n", c=FC)

        ffn_slab = {key: FFN0 + m for key, m in place.items()}
        by_kind = {"gate": "l0_ffn_w_gate", "up": "l0_ffn_w_up", "down": "l0_ffn_w_down"}
        for (kind, j), k in ffn_slab.items():
            slabs[k] = (rows if kind == "down" else cols)(w[by_kind[kind]], SLAB * j)

        def products(eng, k, half, item=0):
            eng.wait_ge(slab_used if half else slab_half, item * PER + (k + 1))

        N_PAR = 16

        block = ctx.enter_context(nc.Block())

        @block.sync
        def _(sp):
            xv = w["x"].rearrange("b (c p) d -> p (b c) d", p=P)
            sp.dma_start(x[:, :, :], xv).then_inc(x_in, 16)
            for k, src in enumerate(slabs):
                if k >= SLOTS:
                    sp.wait_ge(slab_used, k - SLOTS + 1)
                shape = slab_at(k)[1 if src.shape[1] == FC else 0]
                sp.dma_start(shape, src).then_inc(landed[k % SLOTS], 16)
            moe = {"gate": "l1_moe_w_gate", "up": "l1_moe_w_up", "down": "l1_moe_w_down"}

            def load_round(b):
                with sp.Fori(0, NE) as e:
                    it = sp.snap(b * NE + e)
                    for m, (kind, j) in enumerate(order):
                        k = MOE0 + m
                        sp.wait_ge(slab_used, it * PER + (k - SLOTS + 1))
                        wm = w[moe[kind]]
                        part = slice(SLAB * j, SLAB * (j + 1))
                        src = wm[bass.ds(e, 1), part, :] if kind == "down" else wm[bass.ds(e, 1), :, part]
                        dst = slab_at(k)[1 if kind == "down" else 0]
                        sp.dma_start(dst, src.rearrange("a (c p) n -> p (a c) n", p=P)) \
                          .then_inc(landed[k % SLOTS], 16)

            load_round(0)
            sp.wait_ge(routed, 1)
            nr = sp.value_load(nrounds[0:1, 0:1], min_val=1, max_val=ROUNDS)
            with sp.If(nr > 1):
                with sp.Fori(1, nr) as b:
                    load_round(b)
            ov = out.rearrange("b (c p) d -> p (b c) d", p=P)
            for c in range(TC):
                sp.wait_ge(fin_ok, c + 1)
                sp.dma_start(ov[:, c, :], fout[:, c, :]).then_inc(stored, 16)
            sp.wait_ge(stored, 16 * TC)

        @block.gpsimd
        def _(pool):
            n = [0]

            def own(ins):
                n[0] += 1
                ins.then_inc(pool_step, 1)

            def settled():
                pool.wait_ge(pool_step, n[0])

            own(pool.memset(ident[:, :], 0.0))
            own(pool.memset(ones[:, :], 1.0))
            own(pool.memset(neg[:, :, :, :], 0.0))
            own(pool.memset(mhalf[:, :], -0.5))
            own(pool.iota(xorI[:, 0, :], pattern=[[1, P]], base=0, channel_multiplier=0))
            own(pool.iota(xorI[:, 1, :], pattern=[[0, P]], base=0, channel_multiplier=1))
            own(pool.iota(iot[:, :], pattern=[[1, P]], base=0, channel_multiplier=0,
                          allow_small_or_imprecise_dtypes=True))
            settled()
            own(pool.affine_select(out=ident[:, :], in_=ident[:, :], compare_op=ALU.not_equal, fill=1.0, base=0,
                                   pattern=[[-1, P]], channel_multiplier=1))
            own(pool.affine_select(out=incl[:, :], in_=ones[:, :], compare_op=ALU.is_ge, fill=0.0, base=0,
                                   pattern=[[1, P]], channel_multiplier=-1))
            own(pool.affine_select(out=strict[:, :], in_=ones[:, :], compare_op=ALU.is_gt, fill=0.0, base=0,
                                   pattern=[[1, P]], channel_multiplier=-1))
            for a, op in ((0, ALU.is_gt), (1, ALU.is_ge)):
                own(pool.affine_select(out=neg[:, a, :, :], in_=neg[:, a, :, :], compare_op=op, fill=NEG, base=0,
                                       pattern=[[0, TC], [1, P]], channel_multiplier=-1))
            settled()
            pool.memset(mv[:, :, :, 256:257], 1.0).then_inc(consts, 1)

            def root(i, m):
                pool.wait_ge(var_ok[i], 1)
                pool.tensor_tensor(rs[:, i, 0:m], va[:, i, 0:m], mhalf[:, 0:m], ALU.pow).then_inc(rs_ok[i], 1)

            root(0, TC)
            root(1, TC * ML_H)
            root(2, TC)
            pool.wait_ge(res[1], 4)
            pool.memset(graw[:, :, :, 0:GD_K - 1], 0.0).then_inc(consts, 1)
            root(3, TC)
            root(4, TC * GD_H)
            root(5, TC)
            root(6, TC)

        @block.scalar
        def _(act):
            g = [w["l0_norm_mix"], w["l0_ml_head_gain"], w["l0_norm_ffn"], w["l1_norm_mix"], w["l1_norm_ffn"]]
            for i, a in enumerate(g):
                act.dma_start(packG[DC * i:DC * (i + 1), :], a.rearrange("(c p) -> c p", p=P)).then_inc(par_in, 16)
            act.dma_start(packG[5 * DC:5 * DC + 1, :], w["l1_gdn_out_gain"].rearrange("(c p) -> c p", p=P)) \
               .then_inc(par_in, 16)
            for k in range(GD_K):
                act.dma_start(packT[24 * k:24 * (k + 1), :],
                              w["l1_gdn_conv"][k, :].rearrange("(c p) -> c p", p=P)).then_inc(par_in, 16)
            for dst, name, a, m in ((w_if, "l0_ml_w_in", 3072, 2 * ML_H), (w_ba, "l1_gdn_w_in", 4096, 2 * GD_H),
                                    (w_rt, "l1_moe_router", 0, NE)):
                act.dma_start(dst[:, :, :], w[name][:, a:a + m].rearrange("(c p) n -> p c n", p=P)) \
                   .then_inc(par_in, 16)
            for dst, name in ((bif, "l0_ml_b_if"), (dtb, "l1_gdn_dt_bias"), (alog, "l1_gdn_a_log")):
                act.dma_start(dst[:, :], w[name].partition_broadcast(P)).then_inc(par_in, 16)

            n = [0]

            def own(ins):
                n[0] += 1
                ins.then_inc(act_step, 1)
                act.wait_ge(act_step, n[0])

            def sum_squares(i):
                for c in range(TC):
                    act.activation(xn[:, c, :], x[:, c, :], ACT.Square,
                                   accum_out=ss[:, i, c:c + 1]).then_inc(sq_sum[i], 1)

            def turned(i, gcol):
                for k in (2, 3):
                    act.wait_ge(tr_ok[i], k + 1)
                    for a in range(2):
                        c = 2 * k + a
                        ins = act.activation(hT[:, c, :], b2(k)[:, a, :], ACT.Copy, scale=gcol(c))
                    ins.then_inc(hT_ok[i], 1)

            act.wait_ge(x_in, 16)
            sum_squares(0)
            act.wait_ge(pack_e, 1)
            turned(0, lambda c: gains[:, c:c + 1])

            act.wait_ge(g0_dve, 2)
            act.activation(sm[:, 2, 0:8], sm[:, 1, 0:8], ACT.Exp, scale=-1.0).then_inc(g0_act, 1)
            act.wait_ge(g0_act, 1)
            act.activation(sm[:, 3, 0:8], sm[:, 2, 0:8], ACT.Ln, bias=1.0).then_inc(g0_act, 1)

            for s, dst, scale in ((0, mq, 1.0), (1, mk, ML_DQK ** -0.5)):
                for a in range(2):
                    products(act, s, a)
                    act.activation(dst[:, 2 * a:2 * a + 2, :], b2([6, 0][s] + a), ACT.Copy, scale=scale) \
                       .then_inc(ev0, 1)
            act.wait_ge(g0_dve, 8)
            act.activation(sm[:, 8, 0:8], sm[:, 7, 0:8], ACT.Exp, scale=-1.0).then_inc(g0_act, 1)
            for s, at in ((4, 6), (5, 0)):
                for c in range(TC):
                    products(act, s, c)
                    act.activation(mog[:, c, SLAB * (s - 4):SLAB * (s - 3)], bank[at + c][:, :], ACT.Sigmoid) \
                       .then_inc(ev0, 1)
            for h in range(ML_H):
                act.wait_ge(h_bc, h + 1)
                if h >= 2:
                    act.wait_ge(h_sc, h - 1)
                D0 = bank[2 + 4 * (h % 2)]
                act.activation(mw[:, h % 2, 0:256], D0[:, 0:256], ACT.Exp, bias=sm[:, 5, h:h + 1])
                act.activation(mw[:, h % 2, 256:384], D0[:, 256:384], ACT.Exp,
                               bias=sm[:, 5, 4 + h:5 + h]).then_inc(h_w, 1)
            for h in range(ML_H):
                for c in range(TC):
                    act.wait_ge(h_hs, TC * h + c + 1)
                    if h or c:
                        act.wait_ge(sq_sum[1], TC * h + c)
                    act.activation(msq[:, :], xn[:, c, ML_DV * h:ML_DV * (h + 1)], ACT.Square,
                                   accum_out=ss[:, 1, 4 * c + h:4 * c + h + 1]).then_inc(sq_sum[1], 1)
            turned(1, lambda c: gains[:, DC + c:DC + c + 1])

            act.wait_ge(res[0], 4)
            sum_squares(2)
            turned(2, lambda c: gains[:, 2 * DC + c:2 * DC + c + 1])
            for j in range(FJ):
                for a in range(2):
                    products(act, ffn_slab[("gate", j)], a)
                    if j >= 1:
                        act.wait_ge(f_hh, 2 * (j - 1) + a + 1)
                    act.activation(fsg[:, 2 * a:2 * a + 2, :], b2(a), ACT.Silu).then_inc(f_silu, 1)

            act.wait_ge(res[1], 4)
            sum_squares(3)
            turned(3, lambda c: gains[:, 3 * DC + c:3 * DC + c + 1])
            act.wait_ge(par_in, 16 * N_PAR)
            act.activation(sm[:, 10, 0:8], alog[:, :], ACT.Exp).then_inc(g1_act, 1)
            act.wait_ge(g1_dve, 3)
            act.activation(sm[:, 14:16, :], sm[:, 12:14, :], ACT.Exp, scale=-1.0).then_inc(g1_act, 1)
            act.wait_ge(g1_act, 2)
            act.activation(sm[:, 16:18, :], sm[:, 14:16, :], ACT.Ln, bias=1.0).then_inc(g1_act, 1)
            act.wait_ge(g1_dve, 8)
            act.activation(sm[:, 18, :], sm[:, 19, :], ACT.Exp)
            act.activation(sm[:, 20, 0:8], sm[:, 21, 8:16], ACT.Exp)
            act.activation(sm[:, 20, 8:16], sm[:, 22, 8:16], ACT.Exp)
            act.activation(sm[:, 23, 8:16], sm[:, 23, 0:8], ACT.Exp).then_inc(g1_act, 1)
            act.wait_ge(consts, 2)

            def conv_in(s):
                if s >= 2:
                    act.wait_ge(conv_ok, s - 1)
                for a in range(2):
                    products(act, GDN0 + s, a)
                    act.activation(graw[:, s % 2, 2 * a:2 * a + 2, GD_K - 1:RW], b2(2 * ((s + 3) % 4) + a),
                                   ACT.Copy).then_inc(ev1, 1)

            def conv_act(s):
                dst = (gq, gk, gv)[s // 2][:, 4 * (s % 2):4 * (s % 2) + 4, :]
                act.wait_ge(conv_ok, s + 1)
                ins = act.activation(dst, dst, ACT.Silu)
                if s < 4:
                    own(ins)
                    if s >= 2:
                        act.wait_ge(ssq_pe, 2 * (s - 1))
                    act.activation(sqb[:, s % 2, :, :], dst, ACT.Square).then_inc(sqr_ok, 1)
                else:
                    ins.then_inc(silu_ok, 1)

            conv_in(0)
            for s in range(1, 6):
                conv_in(s)
                conv_act(s - 1)
            conv_act(5)
            for s in range(4):
                act.wait_ge(ssq_ev, 2 * s + 2)
                r = rsq[:, 4 * s:4 * s + 4, :]
                own(act.activation(r, r, ACT.Ln))
                act.activation(r, r, ACT.Exp, scale=-0.5).then_inc(ln_ok, 1)
            for s in (6, 7):
                for c in range(TC):
                    products(act, GDN0 + s, c)
                    act.activation(gz[:, c, SLAB * (s - 6):SLAB * (s - 5)], bank[2 * ((s + 3) % 4) + c][:, :],
                                   ACT.Silu).then_inc(ev1, 1)
            for h in range(GD_H):
                act.wait_ge(bc_ok, h + 1)
                if h >= 2:
                    act.wait_ge(att_ok, h - 1)
                Db = bank[4 + h % 2][:, :].rearrange("p (a c t) -> p a c t", a=2, c=TC)
                for c in range(TC):
                    ins = act.activation(gam[:, h % 2, :, c, :], Db[:, :, c, :], ACT.Exp,
                                         bias=sm[:, 11, 8 * c + h:8 * c + h + 1])
                ins.then_inc(gam_ok, 1)
            for l in range(1, 7):
                for gi in range(4):
                    act.wait_ge(inv_x, 4 * l + gi + 1)
                    act.activation(xs[:, gi, :, :], b2(2 * gi, 4), ACT.Copy).then_inc(inv_xs, 1)
            for gi in range(2):
                hs = slice(4 * gi, 4 * gi + 4)
                act.wait_ge(s_pe, 2 * gi + 1)
                act.activation(vn[:, 0, hs, :], b2(2 * gi, 4), ACT.Copy).then_inc(s_act, 1)
                act.wait_ge(s_pe, 2 * gi + 2)
                act.activation(nwT[:, hs, :], b2(2 * gi + 1, 4), ACT.Copy, scale=-1.0).then_inc(s_act, 1)
            for gi in range(2):
                hs = slice(4 * gi, 4 * gi + 4)
                act.wait_ge(s_pe, 4 + 3 * gi + 1)
                act.activation(st1[:, hs, :], b2(4 + 2 * gi, 4), ACT.Copy).then_inc(s_act, 1)
            for gi in range(2):
                hs = slice(4 * gi, 4 * gi + 4)
                act.wait_ge(s_pe, 10 + 2 * gi + 1)
                act.activation(vn[:, 1, hs, :], b2(2 * gi, 4), ACT.Copy).then_inc(s_act, 1)
            turned(4, lambda c: gains[:, 5 * DC:5 * DC + 1])

            act.wait_ge(res[2], 4)
            sum_squares(5)
            turned(5, lambda c: gains[:, 4 * DC + c:4 * DC + c + 1])
            act.dma_start(fgain[:, :], w["final_norm"].partition_broadcast(P)).then_inc(par_in, 16)
            act.wait_ge(r_dve, 1)
            act.activation(rt[:, 6, 0:TC], rt[:, 5, 0:TC], ACT.Exp).then_inc(r_act, 1)
            act.wait_ge(routed, 1)
            nr = act.value_load(nrounds[0:1, 0:1], min_val=1, max_val=ROUNDS)
            with act.Fori(0, nr) as b:
                with act.Fori(0, NE) as e:
                    it = act.snap(b * NE + e)
                    act.wait_ge(e_gather, it * 3 + 3)
                    act.activation(eGT[0:CAP, :], bank[6][0:CAP, 0:S], ACT.Copy).then_inc(e_gt, 1)
                    for j in range(FJ):
                        products(act, MOE0 + place[("gate", j)], 1, it)
                        act.activation(esg[:, j % 2, :, :],
                                       bank[j % 2][:, 0:FC * CAP].rearrange("p (a n) -> p a n", a=FC),
                                       ACT.Silu).then_inc(e_silu, 1)
                    products(act, MOE0 + PER - 1, 1, it)
                    act.activation(eyT[:, 0:4, :], bank[6][:, 0:4 * CAP].rearrange("p (a n) -> p a n", a=4),
                                   ACT.Copy).then_inc(e_yT, 1)
                    act.wait_ge(e_tr, it * 2 + 1)
                    act.activation(eyg[0:CAP, 0:512], bank[4][0:CAP, :], ACT.Copy).then_inc(e_yg, 1)
            act.wait_ge(e_x, nr * (4 * NE) + 1)
            sum_squares(6)

        @block.vector
        def _(dve):
            n = [0]

            def own(ins):
                n[0] += 1
                ins.then_inc(dve_step, 1)

            def settled():
                dve.wait_ge(dve_step, n[0])

            def step(ins):
                own(ins)
                settled()

            dve.wait_ge(consts, 1)
            step(dve.tensor_tensor(xorI[:, 2, :], xorI[:, 0, :], xorI[:, 1, :], ALU.bitwise_xor))
            step(dve.tensor_copy(xorF[:, 0, :], xorI[:, 2, :]))
            step(dve.tensor_tensor(xorF[:, 2, :], xorF[:, 0, :], strict[:, :], ALU.mult))
            step(dve.tensor_tensor(xorF[:, 3, :], xorF[:, 0, :], incl[:, :], ALU.mult))
            step(dve.tensor_tensor(xorF[:, 1, :], xorF[:, 0, :], xorF[:, 3, :], ALU.subtract))
            for l in range(7):
                for dst, src in ((low, xorF[:, 1, :]), (upp, xorF[:, 2, :])):
                    step(dve.tensor_scalar(xorF[:, 0, :], src, float(2 ** l), None, ALU.is_ge))
                    step(dve.scalar_tensor_tensor(out=dst[:, l, :], in0=src, scalar=float(2 ** (l + 1)),
                                                  in1=xorF[:, 0, :], op0=ALU.is_lt, op1=ALU.mult))
            dve.wait_ge(pack_t, 1)
            own(dve.tensor_copy(gains[:, :], bank[4][:, 0:5 * DC + 1]))
            dve.tensor_copy(taps[:, :, :].rearrange("p a b -> p (a b)"), bank[4][:, 128:128 + 96]).then_inc(pack_e, 1)

            def normed(i, m, slot, width, last=False):
                dve.tensor_scalar(va[:, i, 0:m], ss[:, i, 0:m], 1.0 / width, EPS, ALU.mult, ALU.add) \
                   .then_inc(var_ok[i], 1)
                dve.wait_ge(rs_ok[i], 1)

            def norm(i, k):
                dve.wait_ge(sq_sum[i], TC)
                normed(i, TC, i, D)
                for c in range(TC):
                    dve.tensor_scalar(xn[:, c, :], x[:, c, :], rs[:, i, c:c + 1], None, ALU.mult) \
                       .then_inc(xn_ok[k], 1)

            def turned(i, g):
                for k in (0, 1):
                    dve.wait_ge(tr_ok[i], k + 1)
                    dve.tensor_tensor(hT[:, 2 * k:2 * k + 2, :], b2(k), g(k).to_broadcast([P, 2, S]), ALU.mult) \
                       .then_inc(hT_ok[i], 1)

            def gcol(i):
                return lambda k: gains[:, DC * i + 2 * k:DC * i + 2 * k + 2].unsqueeze(2)

            norm(0, 0)
            turned(0, gcol(0))
            G = sm[:, 0, :].rearrange("p (c n) -> p c n", c=TC)
            dve.wait_ge(g0_pe, 1)
            dve.wait_ge(par_in, 16 * N_PAR)
            dve.tensor_tensor(G, bank[4][:, 0:16].rearrange("p (c n) -> p c n", c=TC),
                              bif[:, :].unsqueeze(1).to_broadcast([P, TC, 8]), ALU.add).then_inc(g0_dve, 1)
            dve.wait_ge(g0_dve, 1)
            four = "p (c n) -> p c n"
            dve.scalar_tensor_tensor(out=sm[:, 1, 0:8].rearrange(four, c=TC), in0=G[:, :, 4:8], scalar=-1.0,
                                     in1=G[:, :, 4:8], op0=ALU.mult, op1=ALU.max).then_inc(g0_dve, 1)
            dve.wait_ge(g0_act, 2)
            dve.scalar_tensor_tensor(out=sm[:, 4, 0:8].rearrange(four, c=TC), in0=G[:, :, 4:8], scalar=0.0,
                                     in1=sm[:, 3, 0:8].rearrange(four, c=TC), op0=ALU.min,
                                     op1=ALU.subtract).then_inc(g0_dve, 1)
            dve.wait_ge(g0_pe, 2)
            own(dve.tensor_copy(sm[:, 6, 0:8], bank[5][:, 0:8]))
            dve.tensor_tensor(sm[:, 5, 0:8].rearrange(four, c=TC), G[:, :, 0:4],
                              bank[5][:, 0:8].rearrange(four, c=TC), ALU.subtract).then_inc(g0_dve, 1)
            dve.wait_ge(g0_pe, 3)
            dve.tensor_copy(mrow[0:4, 0, :], bank[5][0:4, 256:512]).then_inc(g0_dve, 1)
            dve.wait_ge(g0_dve, 5)
            dve.tensor_tensor_scan(mrow[0:4, 1, :], mrow[0:4, 0, :], mrow[0:4, 0, :], 0.0, ALU.max, ALU.max) \
               .then_inc(g0_dve, 1)
            dve.wait_ge(g0_dve, 6)
            dve.tensor_scalar(mrow[0:4, 2, :], mrow[0:4, 1, :], -1.0, None, ALU.mult).then_inc(g0_dve, 1)
            dve.wait_ge(g0_pe, 4)
            dve.tensor_tensor(sm[:, 7, 0:8], sm[:, 6, 0:8], bank[5][:, 16:24], ALU.add).then_inc(g0_dve, 1)
            for s, at in ((2, 2), (3, 4)):
                for c in range(TC):
                    products(dve, s, c)
                    dve.tensor_copy(mv[:, c, 2 * (s - 2):2 * (s - 2) + 2, 0:256], b2(at + c)).then_inc(ev0v, 1)

            def head_scores(h):
                dve.wait_ge(h_w, h + 1)
                dve.wait_ge(h_qk, h + 1)
                dve.tensor_tensor(msc[:, h % 2, :], bank[3 + 4 * (h % 2)][:, 0:384], mw[:, h % 2, :], ALU.mult) \
                   .then_inc(h_sc, 1)

            def head_out(h):
                dve.wait_ge(h_num, h + 1)
                for c in range(TC):
                    nb = bank[(0, 4)[h % 2] + c]
                    e_m = sm[:, 8, 4 * c + h:4 * c + h + 1]
                    step(dve.tensor_tensor(den[:, 0, c:c + 1], nb[:, 256:257], e_m, ALU.max))
                    step(dve.scalar_tensor_tensor(out=den[:, 0, c:c + 1], in0=nb[:, 256:257], scalar=-1.0,
                                                  in1=den[:, 0, c:c + 1], op0=ALU.mult, op1=ALU.max))
                    step(dve.reciprocal(den[:, 1, c:c + 1], den[:, 0, c:c + 1]))
                    dve.tensor_scalar(xn[:, c, ML_DV * h:ML_DV * (h + 1)], nb[:, 0:256], den[:, 1, c:c + 1], None,
                                      ALU.mult).then_inc(h_hs, 1)

            dve.wait_ge(g0_act, 3)
            for h in range(ML_H):
                head_scores(h)
                if h >= 1:
                    head_out(h - 1)
            head_out(ML_H - 1)
            dve.wait_ge(sq_sum[1], TC * ML_H)
            normed(1, TC * ML_H, 1, ML_DV)
            for c in range(TC):
                for h in range(ML_H):
                    v = xn[:, c, ML_DV * h:ML_DV * (h + 1)]
                    ins = dve.scalar_tensor_tensor(out=v, in0=v, scalar=rs[:, 1, 4 * c + h:4 * c + h + 1],
                                                   in1=mog[:, c, ML_DV * h:ML_DV * (h + 1)],
                                                   op0=ALU.mult, op1=ALU.mult)
                ins.then_inc(xn_ok[1], 1)
            turned(1, gcol(1))

            def residual(i, ready, banks):
                for m, (c, half, at) in enumerate(banks):
                    if len(ready) == 2:
                        products(dve, ready[m // 2], m % 2)
                    v = x[:, c, 512 * half:512 * (half + 1)]
                    dve.tensor_tensor(v, v, bank[at][:, :], ALU.add).then_inc(res[i], 1)

            proj_banks = [(c, half, 4 + 2 * half + c) for half in range(2) for c in range(TC)]
            residual(0, (6, 7), proj_banks)

            dve.wait_ge(res[0], 4)
            norm(2, 2)
            turned(2, gcol(2))
            for j in range(FJ):
                for a in range(2):
                    products(dve, ffn_slab[("up", j)], a)
                    dve.wait_ge(f_silu, 2 * j + a + 1)
                    dve.tensor_tensor(fhh[:, j % 2, 2 * a:2 * a + 2, :], b2(2 + a), fsg[:, 2 * a:2 * a + 2, :],
                                      ALU.mult).then_inc(f_hh, 1)
            products(dve, ffn_slab[("down", FJ - 1)], 1)
            residual(1, (), [(c, half, 4 + 2 * c + half) for c in range(TC) for half in range(2)])

            dve.wait_ge(res[1], 4)
            norm(3, 3)
            turned(3, gcol(3))
            SB = sm[:, 0:2, :]
            dve.wait_ge(g1_pe, 1)
            bk = bank[4][:, 0:32].rearrange("p (c n) -> p c n", c=TC)
            own(dve.tensor_copy(SB[:, :, 0:8], bk[:, :, 0:8]))
            own(dve.tensor_tensor(SB[:, :, 8:16], bk[:, :, 8:16], dtb[:, :].unsqueeze(1).to_broadcast([P, TC, 8]),
                                  ALU.add))
            settled()
            dve.scalar_tensor_tensor(out=sm[:, 12:14, :], in0=SB, scalar=-1.0, in1=SB, op0=ALU.mult,
                                     op1=ALU.max).then_inc(g1_dve, 3)
            dve.wait_ge(g1_act, 3)
            lnb = sm[:, 19, :].rearrange("p (c n) -> p c n", c=TC)
            gg = sm[:, 4, :].rearrange("p (c n) -> p c n", c=TC)
            own(dve.scalar_tensor_tensor(out=lnb, in0=SB[:, :, 0:8], scalar=0.0, in1=sm[:, 16:18, 0:8], op0=ALU.min,
                                         op1=ALU.subtract))
            step(dve.scalar_tensor_tensor(out=sm[:, 2:4, 0:8], in0=SB[:, :, 8:16], scalar=0.0,
                                          in1=sm[:, 16:18, 8:16], op0=ALU.max, op1=ALU.add))
            dve.scalar_tensor_tensor(out=gg, in0=sm[:, 2:4, 0:8], scalar=-1.0,
                                     in1=sm[:, 10, 0:8].unsqueeze(1).to_broadcast([P, TC, 8]),
                                     op0=ALU.mult, op1=ALU.mult).then_inc(g1_dve, 1)
            dve.wait_ge(g1_pe, 2)
            own(dve.tensor_scalar(sm[:, 11, :], bank[5][:, 0:16], -1.0, None, ALU.mult))
            own(dve.tensor_copy(sm[:, 22, :], bank[5][:, 0:16]))
            settled()
            own(dve.tensor_tensor(sm[:, 23, 0:8], sm[:, 11, 0:8], bank[5][:, 16:24], ALU.add))
            own(dve.tensor_tensor(sm[:, 21, :], sm[:, 19, :], sm[:, 22, :], ALU.add))
            settled()
            dve.tensor_copy(sm[:, 9, :], sm[:, 22, :]).then_inc(g1_dve, 4)
            dve.wait_ge(g1_pe, 3)
            dve.tensor_copy(rows2[0:8, :, :].rearrange("p a t -> p (a t)"), bank[4][0:8, :]).then_inc(g1_dve, 1)

            def conv(s):
                dst = (gq, gk, gv)[s // 2]
                dve.wait_ge(ev1, 2 * s + 2)
                if s == 0:
                    dve.wait_ge(pack_e, 1)
                for k in range(GD_K):
                    for a in range(4):
                        o = dst[:, 4 * (s % 2) + a, :]
                        i = graw[:, s % 2, a, k:k + S]
                        t = taps[:, k, 4 * s + a:4 * s + a + 1]
                        if k == 0:
                            ins = dve.tensor_scalar(o, i, t, None, ALU.mult)
                        else:
                            ins = dve.scalar_tensor_tensor(out=o, in0=i, scalar=t, in1=o, op0=ALU.mult, op1=ALU.add)
                        if k < GD_K - 1:
                            own(ins)
                    if k < GD_K - 1:
                        settled()
                ins.then_inc(conv_ok, 1)

            def squares(s):
                for a in range(2):
                    dve.wait_ge(ssq_pe, 2 * s + a + 1)
                    dve.tensor_scalar(rsq[:, 4 * s + 2 * a:4 * s + 2 * a + 2, :], b2([6, 0, 2, 4][s] + a), EPS, None,
                                      ALU.add).then_inc(ssq_ev, 1)

            for s in range(6):
                conv(s)
                if 2 <= s < 6:
                    squares(s - 2)
            for s in range(4):
                dst = (gq, gk)[s // 2][:, 4 * (s % 2):4 * (s % 2) + 4, :]
                dve.wait_ge(ln_ok, s + 1)
                dve.scalar_tensor_tensor(out=dst, in0=rsq[:, 4 * s:4 * s + 4, :],
                                         scalar=GD_DK ** -0.5 if s < 2 else 1.0, in1=dst,
                                         op0=ALU.mult, op1=ALU.mult).then_inc(qk_ok, 1)
            dve.wait_ge(g1_act, 4)
            for gi in range(8):
                hg = gi % 2
                hs = slice(4 * hg, 4 * hg + 4)
                dve.wait_ge(kv_t, 8 if gi >= 4 else gi + 1)
                if gi < 2:
                    dst, sc = kbg[:, hs, :], sm[:, 20, 4 * hg:4 * hg + 4]
                elif gi < 4:
                    dst, sc = kdec[:, hs, :], sm[:, 23, 8 + 4 * hg:12 + 4 * hg]
                else:
                    c = (gi - 4) // 2
                    dst, sc = vb[:, c, hs, :], sm[:, 18, 8 * c + 4 * hg:8 * c + 4 * hg + 4]
                dve.tensor_tensor(dst, b2([0, 1, 2, 3, 4, 5, 6, 7][gi], 4), sc.unsqueeze(2).to_broadcast([P, 4, P]),
                                  ALU.mult).then_inc(kv_ev, 1)
            for h in range(GD_H):
                dve.wait_ge(gam_ok, h + 1)
                dve.wait_ge(kq_ok, h + 1)
                kq = bank[h % 2][:, :].rearrange("p (a c t) -> p a c t", a=2, c=TC)
                own(dve.scalar_tensor_tensor(out=nAT[:, :, h, :], in0=kq[:, 0], scalar=-1.0, in1=gam[:, h % 2, 0],
                                             op0=ALU.mult, op1=ALU.mult))
                dve.tensor_tensor(attT[:, :, h, :], kq[:, 1], gam[:, h % 2, 1], ALU.mult).then_inc(att_ok, 1)
            settled()
            for gi in range(4):
                c, hs = gi // 2, slice(4 * (gi % 2), 4 * (gi % 2) + 4)
                eye = ident[:, :].unsqueeze(1).to_broadcast([P, 4, P])
                own(dve.tensor_copy(Tn[:, c, hs, :], eye))
                own(dve.tensor_copy(Tt[:, c, hs, :], eye))
            settled()
            for l in range(7):
                lo = low[:, l, :].unsqueeze(1).to_broadcast([P, 4, P])
                up = upp[:, l, :].unsqueeze(1).to_broadcast([P, 4, P])
                for gi in range(4):
                    c, hs = gi // 2, slice(4 * (gi % 2), 4 * (gi % 2) + 4)
                    if l == 0:
                        dve.wait_ge(inv_x, gi + 1)
                        own(dve.copy_predicated(Tn[:, c, hs, :], lo, b2(2 * gi, 4)))
                        dve.copy_predicated(Tt[:, c, hs, :], up, nAT[:, c, hs, :]).then_inc(inv_t, 1)
                        continue
                    dve.wait_ge(inv_d, 4 * (l - 1) + gi + 1)
                    if l < 6:
                        own(dve.copy_predicated(Tn[:, c, hs, :], lo, b2(2 * gi, 4)))
                    dve.copy_predicated(Tt[:, c, hs, :], up, b2(2 * gi + 1, 4)).then_inc(inv_t, 1)
            og = xn[:, :, :].rearrange("p c (h d) -> p c h d", h=GD_H)
            for gi in range(2):
                hs = slice(4 * gi, 4 * gi + 4)
                dve.wait_ge(s_pe, 4 + 3 * gi + 2)
                own(dve.tensor_copy(og[:, 0, hs, :], b2(5 + 2 * gi, 4)))
                dve.wait_ge(s_pe, 4 + 3 * gi + 3)
                dve.tensor_tensor(og[:, 1, hs, :], b2(1 + 2 * gi, 4),
                                  sm[:, 20, 8 + 4 * gi:12 + 4 * gi].unsqueeze(2).to_broadcast([P, 4, P]),
                                  ALU.mult).then_inc(s_dve, 1)
            for gi in range(2):
                hs = slice(4 * gi, 4 * gi + 4)
                dve.wait_ge(s_pe, 10 + 2 * gi + 2)
                dve.wait_ge(s_dve, gi + 1)
                own(dve.tensor_tensor(og[:, 1, hs, :], og[:, 1, hs, :], b2(4 + 2 * gi, 4), ALU.add))
            settled()
            xr = xn[:, :, :].rearrange("p c (h d) -> p (c h) d", h=GD_H)
            step(dve.tensor_tensor(osq, xr, xr, ALU.mult))
            step(dve.tensor_reduce(ss[:, 4, :], osq, AX.X, ALU.add))
            normed(4, TC * GD_H, 4, GD_DV)
            for c in range(TC):
                own(dve.tensor_tensor(og[:, c], og[:, c], rs[:, 4, 8 * c:8 * c + 8].unsqueeze(2)
                                      .to_broadcast([P, 8, P]), ALU.mult))
            settled()
            for c in range(TC):
                dve.tensor_tensor(xn[:, c, :], xn[:, c, :], gz[:, c, :], ALU.mult).then_inc(xn_ok[4], 1)
            turned(4, lambda k: gains[:, 5 * DC:5 * DC + 1].unsqueeze(2))
            residual(2, (GDN0 + 8, GDN0 + 9), proj_banks)

            dve.wait_ge(res[2], 4)
            norm(5, 5)
            turned(5, gcol(4))
            r16 = "p (c n) -> p c n"

            def t8(i):
                return rt[:, i, :].rearrange(r16, c=TC)

            ramp = iot[:, 0:NE].unsqueeze(1).to_broadcast([P, TC, NE])

            def col(i):
                return rt[:, i, 0:TC]

            def wide(i):
                return col(i).unsqueeze(2).to_broadcast([P, TC, NE])

            dve.wait_ge(r_pe, 1)
            step(dve.tensor_copy(t8(0), bank[4][:, 0:16].rearrange(r16, c=TC)))

            def top(src, m, hot):
                step(dve.tensor_reduce(col(m), t8(src), AX.X, ALU.max))
                step(dve.tensor_tensor(t8(8), t8(src), wide(m), ALU.is_equal))
                step(dve.scalar_tensor_tensor(out=t8(8), in0=t8(8), scalar=-100.0, in1=ramp, op0=ALU.mult,
                                              op1=ALU.add))
                step(dve.tensor_reduce(col(9), t8(8), AX.X, ALU.min))
                step(dve.tensor_tensor(t8(hot), t8(8), wide(9), ALU.is_equal))

            top(0, 3, 1)
            step(dve.scalar_tensor_tensor(out=t8(7), in0=t8(1), scalar=NEG, in1=t8(0), op0=ALU.mult, op1=ALU.add))
            top(7, 4, 2)
            dve.tensor_tensor(col(5), col(4), col(3), ALU.subtract).then_inc(r_dve, 1)
            dve.tensor_tensor(t8(10), t8(1), t8(2), ALU.add).then_inc(r_dve, 1)
            dve.wait_ge(r_act, 1)
            step(dve.tensor_scalar(col(11), col(6), 1.0, None, ALU.add))
            step(dve.reciprocal(col(12), col(11)))
            step(dve.tensor_tensor(col(13), col(6), col(12), ALU.mult))
            own(dve.tensor_tensor(t8(1), t8(1), wide(12), ALU.mult))
            step(dve.tensor_tensor(t8(2), t8(2), wide(13), ALU.mult))
            step(dve.tensor_tensor(gate9[:, :, 0:NE], t8(1), t8(2), ALU.add))
            own(dve.tensor_copy(gate9[:, :, NE:NE + 1], gate9[:, :, 0:1]))
            dve.wait_ge(r_pe, 2)
            rk = bank[5][:, 0:16].rearrange(r16, c=TC)
            step(dve.scalar_tensor_tensor(out=t8(14), in0=rk, scalar=1.0, in1=t8(10), op0=ALU.add, op1=ALU.mult))
            step(dve.tensor_scalar(posm[:, :, 0:NE], t8(14), -1.0, None, ALU.add))
            dve.tensor_scalar(posm[:, :, NE:NE + 1], posm[:, :, 0:1], -float(CAP), None, ALU.add).then_inc(e_x, 1)
            dve.wait_ge(e_x, 1)
            step(dve.tensor_reduce(rt[0:1, 15, 0:1], bank[5][0:1, 16:24], AX.X, ALU.max))
            step(dve.tensor_scalar(rt[0:1, 15, 1:2], rt[0:1, 15, 0:1], -0.5, None, ALU.is_gt))
            for b in range(1, ROUNDS):
                step(dve.scalar_tensor_tensor(out=rt[0:1, 15, b + 1:b + 2], in0=rt[0:1, 15, 0:1],
                                              scalar=float(b * CAP), in1=rt[0:1, 15, b:b + 1], op0=ALU.is_gt,
                                              op1=ALU.add))
            dve.tensor_copy(nrounds[0:1, 0:1], rt[0:1, 15, ROUNDS:ROUNDS + 1]).then_inc(routed, 1)
            settled()
            dve.wait_ge(routed, 1)

            def select(e):
                for c in range(TC):
                    dve.tensor_scalar(eP[:, c, :], iot[:, 0:CAP], posm[:, c, bass.ds(e, 1)], None, ALU.is_equal)
                for c in range(TC):
                    ins = dve.tensor_scalar(ePG[:, c, :], iot[:, 0:CAP], posm[:, c, bass.ds(e, 1)],
                                            gate9[:, c, bass.ds(e, 1)], ALU.is_equal, ALU.mult)
                ins.then_inc(e_sel, 1)

            select(0)
            nr = dve.value_load(nrounds[0:1, 0:1], min_val=1, max_val=ROUNDS)
            gm = gcol(4)
            with dve.Fori(0, nr) as b:
                with dve.Fori(0, NE) as e:
                    it = dve.snap(b * NE + e)
                    for a in range(2):
                        dve.wait_ge(e_gather, it * 3 + (a + 1))
                        gh = gains[:, 4 * DC + 4 * a:4 * DC + 4 * a + 4].unsqueeze(2).to_broadcast([P, 4, CAP])
                        dve.tensor_tensor(exg[:, 4 * a:4 * a + 4, :],
                                          bank[4 + a][:, 0:4 * CAP].rearrange("p (a n) -> p a n", a=4), gh,
                                          ALU.mult).then_inc(e_xg, 1)
                    for j in range(FJ):
                        products(dve, MOE0 + place[("up", j)], 1, it)
                        dve.wait_ge(e_silu, it * FJ + (j + 1))
                        dve.tensor_tensor(ehh[:, j % 2, :, :],
                                          bank[2 + j % 2][:, 0:FC * CAP].rearrange("p (a n) -> p a n", a=FC),
                                          esg[:, j % 2, :, :], ALU.mult).then_inc(e_hh, 1)
                        if j == 3:
                            select(e + 1)
                    products(dve, MOE0 + PER - 1, 1, it)
                    dve.tensor_copy(eyT[:, 4:8, :], bank[7][:, 0:4 * CAP].rearrange("p (a n) -> p a n", a=4)) \
                       .then_inc(e_yT, 1)
                    dve.wait_ge(e_tr, it * 2 + 2)
                    dve.tensor_copy(eyg[0:CAP, 512:1024], bank[5][0:CAP, :]).then_inc(e_yg, 1)
                    for m in range(4):
                        c, half = m // 2, m % 2
                        dve.wait_ge(e_sc, it * 4 + (m + 1))
                        v = x[:, c, 512 * half:512 * (half + 1)]
                        dve.tensor_tensor(v, v, bank[m][:, :], ALU.add).then_inc(e_x, 1)
                dve.wait_ge(e_sel, b * NE + (NE + 1))
                dve.tensor_scalar(posm[:, :, :], posm[:, :, :], -float(CAP), None, ALU.add).then_inc(e_own, 1)
                dve.wait_ge(e_own, b + 1)

            dve.wait_ge(sq_sum[6], TC)
            normed(6, TC, 6, D)
            dve.wait_ge(par_in, 16 * (N_PAR + 1))
            for c in range(TC):
                dve.scalar_tensor_tensor(out=fout[:, c, :], in0=x[:, c, :], scalar=rs[:, 6, c:c + 1],
                                         in1=fgain[:, :], op0=ALU.mult, op1=ALU.mult).then_inc(fin_ok, 1)

        @block.tensor
        def _(pe):
            mm = pe.matmul

            def arrived(k):
                pe.wait_ge(landed[k % SLOTS], 16 * (k // SLOTS + 1))

            def turn(i):
                pe.wait_ge(xn_ok[i], TC)
                for k in range(4):
                    for a in range(2):
                        for c in range(TC):
                            d = 2 * k + a
                            ins = pe.transpose(bank[k][:, a * S + c * P:a * S + (c + 1) * P],
                                               xn[:, c, d * P:(d + 1) * P], ident[:, :])
                    ins.then_inc(tr_ok[i], 1)
                pe.wait_ge(hT_ok[i], 4)

            def tall(k, at):
                arrived(k)
                wk = slab_at(k)[0]
                for a in range(4):
                    o = bank[at + a // 2][:, (a % 2) * S:(a % 2 + 1) * S]
                    for c in range(DC):
                        ins = mm(o, wk[:, c, a * P:(a + 1) * P], hT[:, c, :], start=(c == 0), stop=(c == DC - 1))
                    if a % 2 == 1:
                        ins.then_inc(slab_used if a == 3 else slab_half, 1)

            def flat(k, at):
                arrived(k)
                wk = slab_at(k)[0]
                for t in range(TC):
                    for c in range(DC):
                        ins = mm(bank[at + t][:, :], hT[:, c, t * P:(t + 1) * P], wk[:, c, :],
                                 start=(c == 0), stop=(c == DC - 1))
                    ins.then_inc(slab_used if t else slab_half, 1)

            pe.wait_ge(consts, 1)
            pe.wait_ge(par_in, 16 * N_PAR)
            pe.transpose(bank[4][:, 0:41], packG[0:41, :], ident[0:41, 0:41])
            pe.transpose(bank[4][:, 128:224], packT[0:96, :], ident[0:96, 0:96]).then_inc(pack_t, 1)

            turn(0)
            pe.wait_ge(pack_e, 1)
            for t in range(TC):
                for c in range(DC):
                    ins = mm(bank[4][:, 8 * t:8 * t + 8], hT[:, c, t * P:(t + 1) * P], w_if[:, c, :],
                             start=(c == 0), stop=(c == DC - 1))
            ins.then_inc(g0_pe, 1)
            tall(0, 6)
            pe.wait_ge(g0_dve, 3)
            lf = sm[:, 4, :]
            mm(bank[5][:, 0:4], incl[:, :], lf[:, 0:4], start=True, stop=True)
            mm(bank[5][:, 4:8], incl[:, :], lf[:, 4:8], start=True, stop=False)
            mm(bank[5][:, 4:8], ones[:, :], lf[:, 0:4], start=False, stop=True).then_inc(g0_pe, 1)
            tall(1, 0)
            pe.wait_ge(g0_dve, 4)
            for c in range(TC):
                ins = pe.transpose(bank[5][0:4, 256 + c * P:256 + (c + 1) * P], sm[:, 5, 4 * c:4 * c + 4], ident[:, :])
            ins.then_inc(g0_pe, 1)
            flat(2, 2)
            pe.wait_ge(g0_dve, 7)
            for c in range(TC):
                ins = pe.transpose(bank[5][:, 16 + 4 * c:20 + 4 * c], mrow[0:4, 1, c * P:(c + 1) * P], ident[0:4, 0:4])
            ins.then_inc(g0_pe, 1)
            pe.wait_ge(g0_dve, 8)
            flat(3, 4)
            pe.wait_ge(ev0, 2)
            flat(4, 6)
            pe.wait_ge(ev0, 4)
            flat(5, 0)

            def weigh(h):
                o = bank[2 + 4 * (h % 2)]
                pick = ident[0:4, h:h + 1].to_broadcast([4, P])
                nmu = mrow[0:4, 2, :]
                if h >= 2:
                    pe.wait_ge(h_w, h - 1)
                mm(o[:, 0:256], pick, nmu, start=True, stop=False)
                mm(o[:, 0:128], ident[:, :], neg[:, 1, 0, :], start=False, stop=True)
                mm(o[:, 256:384], pick, nmu[:, 128:256], start=True, stop=False)
                mm(o[:, 256:384], ident[:, :], neg[:, 1, 0, :], start=False, stop=True).then_inc(h_bc, 1)
                if h >= 2:
                    pe.wait_ge(h_sc, h - 1)
                o = bank[3 + 4 * (h % 2)]
                mm(o[:, 0:256], mk[:, h, 0:128], mq[:, h, :], start=True, stop=True)
                mm(o[:, 256:384], mk[:, h, 128:256], mq[:, h, 128:256], start=True, stop=True).then_inc(h_qk, 1)

            def gather_values(h):
                pe.wait_ge(h_sc, h + 1)
                if h >= 2:
                    pe.wait_ge(h_hs, TC * (h - 1))
                sc = msc[:, h % 2, :]
                at = (0, 4)[h % 2]
                mm(bank[at][:, 0:257], sc[:, 0:128], mv[:, 0, h, :], start=True, stop=True)
                mm(bank[at + 1][:, 0:257], sc[:, 128:256], mv[:, 0, h, :], start=True, stop=False)
                mm(bank[at + 1][:, 0:257], sc[:, 256:384], mv[:, 1, h, :], start=False, stop=True).then_inc(h_num, 1)

            pe.wait_ge(ev0v, 4)
            weigh(0)
            pe.wait_ge(ev0, 8)
            for h in range(ML_H):
                if h + 1 < ML_H:
                    weigh(h + 1)
                gather_values(h)
            turn(1)
            pe.wait_ge(h_hs, TC * ML_H)
            flat(6, 4)
            flat(7, 6)

            turn(2)
            pe.wait_ge(res[0], 4)

            def ffn_in(kind, j, at):
                k = ffn_slab[(kind, j)]
                arrived(k)
                wk = slab_at(k)[0]
                for a in range(4):
                    o = bank[at + a // 2][:, (a % 2) * S:(a % 2 + 1) * S]
                    if j >= 1 and a % 2 == 0:
                        pe.wait_ge(f_hh, 2 * (j - 1) + a // 2 + 1)
                    for c in range(DC):
                        ins = mm(o, wk[:, c, a * P:(a + 1) * P], hT[:, c, :], start=(c == 0), stop=(c == DC - 1))
                    if a % 2 == 1:
                        ins.then_inc(slab_used if a == 3 else slab_half, 1)

            def ffn_out(j):
                k = ffn_slab[("down", j)]
                arrived(k)
                wk = slab_at(k)[1]
                for a in range(FC):
                    if a % 2 == 0:
                        pe.wait_ge(f_hh, 2 * j + a // 2 + 1)
                    for t in range(TC):
                        for half in range(2):
                            ins = mm(bank[4 + 2 * t + half][:, :], fhh[:, j % 2, a, t * P:(t + 1) * P],
                                     wk[:, a, 512 * half:512 * (half + 1)],
                                     start=(j == 0 and a == 0), stop=(j == FJ - 1 and a == FC - 1))
                    if a == FC // 2 - 1:
                        ins.then_inc(slab_half, 1)
                ins.then_inc(slab_used, 1)

            for j in range(FJ + 1):
                if j < FJ:
                    ffn_in("gate", j, 0)
                    ffn_in("up", j, 2)
                if j > 0:
                    ffn_out(j - 1)

            turn(3)
            pe.wait_ge(res[1], 4)
            for t in range(TC):
                for c in range(DC):
                    ins = mm(bank[4][:, 16 * t:16 * t + 16], hT[:, c, t * P:(t + 1) * P], w_ba[:, c, :],
                             start=(c == 0), stop=(c == DC - 1))
            ins.then_inc(g1_pe, 1)

            def gdn_in(s):
                at = 2 * ((s + 3) % 4)
                if s >= 4:
                    pe.wait_ge(ev1, 2 * (s - 3))
                if s >= 6:
                    pe.wait_ge(ssq_ev, 8)
                (tall if s < 6 else flat)(GDN0 + s, at)

            def lengths(s):
                at = [6, 0, 2, 4][s]
                pe.wait_ge(sqr_ok, s + 1)
                pe.wait_ge(ev1, 2 * ([0, 1, 2, 3][s] + 1))
                for a in range(2):
                    mm(bank[at + a][:, :], ones[:, :],
                       sqb[:, s % 2, 2 * a:2 * a + 2, :].rearrange("p a t -> p (a t)"),
                       start=True, stop=True).then_inc(ssq_pe, 1)

            gdn_in(0)
            pe.wait_ge(g1_dve, 4)
            g = sm[:, 4, :]
            mm(bank[5][:, 0:16], incl[:, :], g, start=True, stop=True)
            mm(bank[5][:, 16:24], ones[:, :], g[:, 0:8], start=True, stop=True).then_inc(g1_pe, 1)
            gdn_in(1)
            pe.wait_ge(g1_dve, 8)
            for a, r in ((0, 21), (1, 22)):
                for c in range(TC):
                    ins = pe.transpose(bank[4][0:8, a * S + c * P:a * S + (c + 1) * P], sm[:, r, 8 * c:8 * c + 8],
                                       ident[:, :])
            ins.then_inc(g1_pe, 1)
            gdn_in(2)
            pe.wait_ge(g1_dve, 9)
            lengths(0)
            gdn_in(3)
            pe.wait_ge(ssq_ev, 2)
            gdn_in(4)
            lengths(1)
            pe.wait_ge(ssq_ev, 4)
            gdn_in(5)
            lengths(2)
            lengths(3)
            gdn_in(6)
            gdn_in(7)
            pe.wait_ge(ev1, 16)
            pe.wait_ge(qk_ok, 4)
            pe.wait_ge(silu_ok, 2)
            for gi in range(8):
                hg = gi % 2
                src, c = ((gk, 1), (gk, 0), (gv, 0), (gv, 1))[gi // 2]
                for a in range(4):
                    ins = pe.transpose(bank[gi][:, a * P:(a + 1) * P], src[:, 4 * hg + a, c * P:(c + 1) * P],
                                       ident[:, :])
                ins.then_inc(kv_t, 1)

            def decay(h):
                pe.wait_ge(kv_ev, 5 + h % 2 + 1) if h < 2 else pe.wait_ge(gam_ok, h - 1)
                o = bank[4 + h % 2][:, :]
                mm(o, ident[0:8, h:h + 1].to_broadcast([8, P]), rows2[0:8, :, :].rearrange("p a t -> p (a t)"),
                   start=True, stop=False)
                mm(o, ident[:, :], neg[:, :, :, :].rearrange("p a c t -> p (a c t)"), start=False,
                   stop=True).then_inc(bc_ok, 1)

            def scores(h):
                if h >= 2:
                    pe.wait_ge(att_ok, h - 1)
                for a, q in ((0, gk), (1, gq)):
                    for c in range(TC):
                        ins = mm(bank[h % 2][:, (2 * a + c) * P:(2 * a + c + 1) * P], gk[:, h, c * P:(c + 1) * P],
                                 q[:, h, c * P:(c + 1) * P], start=True, stop=True)
                ins.then_inc(kq_ok, 1)

            pe.wait_ge(kv_ev, 2)
            for h in range(GD_H):
                decay(h)
                scores(h)
            pe.wait_ge(att_ok, 8)
            pe.wait_ge(kv_ev, 8)
            for gi in range(4):
                c = gi // 2
                for a in range(4):
                    h = 4 * (gi % 2) + a
                    ins = mm(bank[2 * gi][:, a * P:(a + 1) * P], nAT[:, c, h, :], ident[:, :], start=True, stop=True)
                ins.then_inc(inv_x, 1)
            for l in range(1, 7):
                for gi in range(4):
                    c = gi // 2
                    pe.wait_ge(inv_t, 4 * (l - 1) + gi + 1)
                    for a in range(4):
                        h = 4 * (gi % 2) + a
                        ins = mm(bank[2 * gi][:, a * P:(a + 1) * P], nAT[:, c, h, :], Tn[:, c, h, :],
                                 start=True, stop=True)
                    ins.then_inc(inv_x, 1)
                for gi in range(4):
                    c = gi // 2
                    pe.wait_ge(inv_xs, 4 * (l - 1) + gi + 1)
                    for a in range(4):
                        h = 4 * (gi % 2) + a
                        o = slice(a * P, (a + 1) * P)
                        if l < 6:
                            mm(bank[2 * gi][:, o], Tt[:, c, h, :], xs[:, gi, a, :], start=True, stop=True)
                        ins = mm(bank[2 * gi + 1][:, o], xs[:, gi, a, :], Tt[:, c, h, :], start=True, stop=True)
                    ins.then_inc(inv_d, 1)
            def heads4(gi, at, signal, *products):
                for a in range(4):
                    h = 4 * gi + a
                    for m, (l, r) in enumerate(products):
                        ins = mm(bank[at][:, a * P:(a + 1) * P], l(h), r(h), start=(m == 0),
                                 stop=(m == len(products) - 1))
                ins.then_inc(signal, 1)

            pe.wait_ge(inv_t, 28)
            for gi in range(2):
                heads4(gi, 2 * gi, s_pe, (lambda h: Tt[:, 0, h, :], lambda h: vb[:, 0, h, :]))
                heads4(gi, 2 * gi + 1, s_pe, (lambda h: kbg[:, h, :], lambda h: Tt[:, 1, h, :]))
            for gi in range(2):
                pe.wait_ge(s_act, 2 * gi + 2)
                heads4(gi, 4 + 2 * gi, s_pe, (lambda h: kdec[:, h, :], lambda h: vn[:, 0, h, :]))
                heads4(gi, 5 + 2 * gi, s_pe, (lambda h: attT[:, 0, h, :], lambda h: vn[:, 0, h, :]))
                pe.wait_ge(s_act, 4 + gi + 1)
                heads4(gi, 1 + 2 * gi, s_pe, (lambda h: gq[:, h, P:S], lambda h: st1[:, h, :]))
            for gi in range(2):
                heads4(gi, 2 * gi, s_pe, (lambda h: Tt[:, 1, h, :], lambda h: vb[:, 1, h, :]),
                       (lambda h: nwT[:, h, :], lambda h: st1[:, h, :]))
                pe.wait_ge(s_act, 6 + gi + 1)
                heads4(gi, 4 + 2 * gi, s_pe, (lambda h: attT[:, 1, h, :], lambda h: vn[:, 1, h, :]))
            turn(4)
            flat(GDN0 + 8, 4)
            flat(GDN0 + 9, 6)

            turn(5)
            pe.wait_ge(res[2], 4)
            for t in range(TC):
                for c in range(DC):
                    ins = mm(bank[4][:, 8 * t:8 * t + 8], hT[:, c, t * P:(t + 1) * P], w_rt[:, c, :],
                             start=(c == 0), stop=(c == DC - 1))
            ins.then_inc(r_pe, 1)
            pe.wait_ge(r_dve, 2)
            sel = rt[:, 10, :]
            mm(bank[5][:, 0:8], strict[:, :], sel[:, 0:8], start=True, stop=True)
            mm(bank[5][:, 8:16], strict[:, :], sel[:, 8:16], start=True, stop=False)
            mm(bank[5][:, 8:16], ones[:, :], sel[:, 0:8], start=False, stop=True)
            mm(bank[5][:, 16:24], ones[:, :], sel[:, 0:8], start=True, stop=False)
            mm(bank[5][:, 16:24], ones[:, :], sel[:, 8:16], start=False, stop=True).then_inc(r_pe, 1)
            pe.wait_ge(routed, 1)
            nr = pe.value_load(nrounds[0:1, 0:1], min_val=1, max_val=ROUNDS)

            with pe.Fori(0, nr) as b:
                with pe.Fori(0, NE) as e:
                    it = pe.snap(b * NE + e)
                    pe.wait_ge(e_sel, it + 1)
                    for a in range(2):
                        for q in range(4):
                            d = 4 * a + q
                            for c in range(TC):
                                ins = mm(bank[4 + a][:, q * CAP:(q + 1) * CAP], xn[:, c, d * P:(d + 1) * P],
                                         eP[:, c, :], start=(c == 0), stop=(c == TC - 1))
                        ins.then_inc(e_gather, 1)
                    for c in range(TC):
                        ins = pe.transpose(bank[6][0:CAP, c * P:(c + 1) * P], ePG[:, c, :], ident[:, :])
                    ins.then_inc(e_gather, 1)
                    pe.wait_ge(e_x, it * 4 + 1)
                    for m, (kind, j) in enumerate(order):
                        k = MOE0 + m
                        pe.wait_ge(landed[k % SLOTS], it * (16 * PER // SLOTS) + 16 * (k // SLOTS + 1))
                        if kind == "down":
                            pe.wait_ge(e_hh, it * FJ + (j + 1))
                            if j == 0:
                                pe.wait_ge(e_gt, it + 1)
                            wk = slab_at(k)[1]
                            for d in range(DC):
                                for a in range(FC):
                                    o = bank[6 + d // 4][:, (d % 4) * CAP:(d % 4 + 1) * CAP]
                                    ins = mm(o, wk[:, a, d * P:(d + 1) * P], ehh[:, j % 2, a, :],
                                             start=(j == 0 and a == 0 and d % 4 == 0),
                                             stop=(j == FJ - 1 and a == FC - 1), skip_group_check=True)
                            ins.then_inc(slab_used, 1)
                            continue
                        if m == 0:
                            pe.wait_ge(e_xg, it * 2 + 2)
                        if j >= 2:
                            pe.wait_ge(e_hh, it * FJ + (j - 1))
                        wk = slab_at(k)[0]
                        at = (0 if kind == "gate" else 2) + j % 2
                        for a in range(FC):
                            for c in range(DC):
                                ins = mm(bank[at][:, a * CAP:(a + 1) * CAP], wk[:, c, a * P:(a + 1) * P],
                                         exg[:, c, :], start=(c == 0), stop=(c == DC - 1))
                        ins.then_inc(slab_used, 1)
                    pe.wait_ge(e_yT, it * 2 + 2)
                    for d in range(DC):
                        ins = pe.transpose(bank[4 + d // 4][0:CAP, (d % 4) * P:(d % 4 + 1) * P], eyT[:, d, :],
                                           ident[:, :])
                        if d % 4 == 3:
                            ins.then_inc(e_tr, 1)
                    pe.wait_ge(e_yg, it * 2 + 2)
                    for m in range(4):
                        c, half = m // 2, m % 2
                        mm(bank[m][:, :], eGT[0:CAP, c * P:(c + 1) * P], eyg[0:CAP, 512 * half:512 * (half + 1)],
                           start=True, stop=True).then_inc(e_sc, 1)


_INS = ['x', 'l0_norm_mix', 'l0_ml_w_in', 'l0_ml_b_if', 'l0_ml_head_gain', 'l0_ml_w_out', 'l0_norm_ffn',
        'l0_ffn_w_gate', 'l0_ffn_w_up', 'l0_ffn_w_down', 'l1_norm_mix', 'l1_gdn_w_in', 'l1_gdn_conv',
        'l1_gdn_a_log', 'l1_gdn_dt_bias', 'l1_gdn_out_gain', 'l1_gdn_w_out', 'l1_norm_ffn', 'l1_moe_router',
        'l1_moe_w_gate', 'l1_moe_w_up', 'l1_moe_w_down', 'final_norm']


def kernel(**inputs):
    import numpy as _np
    import concourse.bacc as _bacc
    from concourse import mybir as _mybir
    from concourse.bass_utils import run_bass_kernel_spmd as _run

    nc = _bacc.Bacc("TRN2", target_bir_lowering=False, num_devices=1,
                     dynamic_dma_scratch_size=1024)
    arrays, args = {}, {}
    for name in _INS:
        a = _np.ascontiguousarray(inputs[name])
        arrays[f"in_{name}"] = a
        args[name] = nc.dram_tensor(f"in_{name}", a.shape, _mybir.dt.from_np(a.dtype), kind="ExternalInput").ap()
    out = nc.dram_tensor("out_dram", (1, S, D), _mybir.dt.float32, kind="ExternalOutput").ap()
    bass_hybrid_trunk(nc, out, args)
    r = _run(nc, [arrays], core_ids=[0])
    return r.results[0]["out_dram"]
```

```python
from contextlib import ExitStack

import concourse.bass as bass
from concourse import mybir

P = 128
S = 256
TC = S // P
D = 1024
DC = D // P
EPS = 1e-6

ML_H, ML_DQK, ML_DV = 4, 128, 256
GD_H, GD_DK, GD_DV, GD_K = 8, 128, 128, 4
FF = 3584
NE = 8
CAP = 96
ROUNDS = -(-S // CAP)

SLAB = 512
UNIT = DC * SLAB // 2
RAW = 7
CUT = 3
FJ = FF // SLAB
FC = SLAB // P
NEG = -1e30

F32 = mybir.dt.float32
F32R = mybir.dt.float32r
I32 = mybir.dt.int32
U8 = mybir.dt.uint8
ALU = mybir.AluOpType
ACT = mybir.ActivationFunctionType
AX = mybir.AxisListType


def bass_hybrid_trunk(nc, out, w):
    ctx = ExitStack()
    with ctx:
        def sb(name, shape, dt=F32):
            return ctx.enter_context(nc.sbuf_tensor(name, shape, dt))

        def sem(name):
            return ctx.enter_context(nc.semaphore(name))

        raw = sb("raw", [P, RAW, UNIT])
        whi = sb("whi", [P, CUT, UNIT], F32R)
        wlo = sb("wlo", [P, CUT, UNIT], F32R)
        hTr = sb("hTr", [P, 2, DC * S], F32R)
        hr = sb("hr", [P, 2, FC * S], F32R)
        x = sb("x", [P, TC, D])
        xn = sb("xn", [P, TC, D])
        hT = sb("hT", [P, DC, S])
        area = sb("area", [P, 15424])

        ident = sb("ident", [P, P])
        one = sb("one", [P, 1])
        ones = one[:, :].to_broadcast([P, P])
        incl = sb("incl", [P, P])
        neg = sb("neg", [P, 2, P])
        low = sb("low", [P, 7, P], U8)
        upp = sb("upp", [P, 7, P], U8)
        iot = sb("iot", [P, CAP])
        mhalf = sb("mhalf", [P, 16])
        gains = sb("gains", [P, 5 * DC + 1])
        taps = sb("taps", [P, GD_K, 24])
        w_if = sb("w_if", [P, DC, 2 * ML_H])
        w_ba = sb("w_ba", [P, DC, 2 * GD_H])
        w_rt = sb("w_rt", [P, DC, NE])
        bif = sb("bif", [P, 2 * ML_H])
        dtb = sb("dtb", [P, GD_H])
        alog = sb("alog", [P, GD_H])
        ss = sb("ss", [P, 7, 16])
        va = sb("va", [P, 7, 16])
        rs = sb("rs", [P, 7, 16])
        sm = sb("sm", [P, 24, 16])
        den = sb("den", [P, 2, 8])
        nrounds = sb("nrounds", [1, 1], I32)

        def view(at, n, pat=None, **kw):
            v = area[:, at:at + n]
            return v.rearrange(pat, **kw) if pat else v

        packG = view(8872, 128)
        packT = view(9000, 128)
        xorI = view(9200, 3 * 128).bitcast(I32).rearrange("p (a n) -> p a n", a=3)
        xorF = view(9584, 4 * 128, "p (a n) -> p a n", a=4)
        mq = view(0, 1024, "p (h t) -> p h t", h=ML_H)
        mk = view(1024, 1024, "p (h t) -> p h t", h=ML_H)
        mv = view(2048, TC * ML_H * 257, "p (c h n) -> p c h n", c=TC, h=ML_H)
        mog = view(4104, 2048, "p (c n) -> p c n", c=TC)
        mw = view(6152, 2 * 384, "p (b n) -> p b n", b=2)
        msc = view(6920, 2 * 384, "p (b n) -> p b n", b=2)
        mrow = view(7688, 3 * S, "p (a n) -> p a n", a=3)
        msq = view(8456, 256)
        fsg = view(0, 1024, "p (a t) -> p a t", a=FC)
        fhh = view(1024, 1024, "p (a t) -> p a t", a=FC)
        gq = view(0, 2048, "p (h t) -> p h t", h=GD_H)
        gk = view(2048, 2048, "p (h t) -> p h t", h=GD_H)
        gv = view(4096, 2048, "p (h t) -> p h t", h=GD_H)
        gz = view(6144, 2048, "p (c n) -> p c n", c=TC)
        RW = S + GD_K - 1
        graw = view(8192, 8 * RW, "p (b a n) -> p b a n", b=2, a=4)
        kbg = view(8192, 1024, "p (h d) -> p h d", h=GD_H)
        kdec = view(9216, 1024, "p (h d) -> p h d", h=GD_H)
        nAT = view(10304, 2048, "p (c h t) -> p c h t", c=TC, h=GD_H)
        attT = view(12352, 2048, "p (c h t) -> p c h t", c=TC, h=GD_H)
        rsq = view(10304, 4096, "p (h t) -> p h t", h=2 * GD_H)
        gam = view(14400, 1024, "p (b a c t) -> p b a c t", b=2, a=2, c=TC)
        vb = view(4096, 2048, "p (c h d) -> p c h d", c=TC, h=GD_H)
        xs = view(2048, 2048, "p (g h t) -> p g h t", g=4, h=4)
        nwT = view(2048, 1024, "p (h t) -> p h t", h=GD_H)
        st1 = view(3072, 1024, "p (h t) -> p h t", h=GD_H)
        vn = view(10304, 2048, "p (c h d) -> p c h d", c=TC, h=GD_H)
        osq = view(12352, 2048, "p (g d) -> p g d", g=16)
        rows2 = sb("rows2", [GD_H, 2, S])
        sqb = xn[:, :, :].rearrange("p b (h t) -> p b h t", h=4)
        Tn = xn[:, :, :].rearrange("p c (h t) -> p c h t", h=GD_H)
        Tt = hT[:, :, :].rearrange("p a b -> p (a b)").rearrange("p (c h t) -> p c h t", c=TC, h=GD_H)
        eP = view(0, TC * CAP, "p (c n) -> p c n", c=TC)
        ePG = view(256, TC * CAP, "p (c n) -> p c n", c=TC)
        eGT = view(512, S)
        exg = view(768, DC * CAP, "p (c n) -> p c n", c=DC)
        esg = view(1792, 512)
        ehh = view(2816, 512)
        eyg = view(4864, D)
        fgain = view(6144, D)
        fout = view(7168, 2 * D, "p (c n) -> p c n", c=TC)
        tok9 = view(9216, 2 * TC * 9, "p (a c n) -> p a c n", a=2, c=TC)
        posm, gate9 = tok9[:, 0], tok9[:, 1]
        rt = view(9280, 16 * 16, "p (a n) -> p a n", a=16)

        bank = [ctx.enter_context(nc.psum_tensor(f"bank{i}", [P, 512], F32)) for i in range(8)]

        def b2(i, n=2):
            return bank[i][:, :].rearrange("p (a t) -> p a t", a=n)

        x_in = sem("x_in")
        par_in, par2_in, par3_in = sem("par_in"), sem("par2_in"), sem("par3_in")
        landed = [sem(f"landed{i}") for i in range(RAW)]
        hi_ok = sem("hi_ok")
        lo_ok = sem("lo_ok")
        unit_used = sem("unit_used")
        pool_step = sem("pool_step")
        consts = sem("consts")
        dve_step = sem("dve_step")
        act_step = sem("act_step")
        masks = sem("masks")
        pack_t = sem("pack_t")
        pack_e = sem("pack_e")
        tap_t, tap_e = sem("tap_t"), sem("tap_e")
        sq_sum = [sem(f"sq_sum{i}") for i in range(7)]
        var_ok = [sem(f"var_ok{i}") for i in range(7)]
        rs_ok = [sem(f"rs_ok{i}") for i in range(7)]
        xn_ok = [sem(f"xn_ok{i}") for i in range(6)]
        tr_ok = [sem(f"tr_ok{i}") for i in range(6)]
        hT_d = [sem(f"hT_d{i}") for i in range(6)]
        hT_a = [sem(f"hT_a{i}") for i in range(6)]
        hT_hi = [sem(f"hT_hi{i}") for i in range(6)]
        hT_lo = [sem(f"hT_lo{i}") for i in range(6)]
        ev0, ev0v = sem("ev0"), sem("ev0v")
        g0_pe, g0_dve, g0_act = sem("g0_pe"), sem("g0_dve"), sem("g0_act")
        h_bc, h_w, h_qk, h_sc, h_num, h_hs = [sem(n) for n in ("h_bc", "h_w", "h_qk", "h_sc", "h_num", "h_hs")]
        res = [sem(f"res{i}") for i in range(3)]
        f_silu, f_hh, f_hi, f_lo = sem("f_silu"), sem("f_hh"), sem("f_hi"), sem("f_lo")
        ev1 = sem("ev1")
        conv_ok, silu_ok, sqr_ok, ssq_pe, ssq_ev, ln_ok, qk_ok = [sem(n) for n in (
            "conv_ok", "silu_ok", "sqr_ok", "ssq_pe", "ssq_ev", "ln_ok", "qk_ok")]
        g1_pe, g1_dve, g1_act = sem("g1_pe"), sem("g1_dve"), sem("g1_act")
        kv_t, kv_ev = sem("kv_t"), sem("kv_ev")
        bc_ok, gam_ok, kq_ok, att_ok = sem("bc_ok"), sem("gam_ok"), sem("kq_ok"), sem("att_ok")
        inv_x, inv_xs, inv_d, inv_t = sem("inv_x"), sem("inv_xs"), sem("inv_d"), sem("inv_t")
        s_pe, s_act, s_dve = sem("s_pe"), sem("s_act"), sem("s_dve")
        r_pe, r_dve, r_act, routed = sem("r_pe"), sem("r_dve"), sem("r_act"), sem("routed")
        e_sel, e_gather, e_xg, e_xhi, e_xlo, e_gt, e_silu, e_hh, e_t, e_thi, e_tlo, e_yg, e_yg2, e_sc, e_x = [
            sem(n) for n in ("e_sel", "e_gather", "e_xg", "e_xhi", "e_xlo", "e_gt", "e_silu", "e_hh", "e_t",
                             "e_thi", "e_tlo", "e_yg", "e_yg2", "e_sc", "e_x")]
        e_own = sem("e_own")
        fin_ok = sem("fin_ok")
        stored = sem("stored")

        def cols(m, a):
            return m[:, a:a + SLAB].rearrange("(c p) n -> p c n", p=P)

        def rows(m, a):
            return m[a:a + SLAB, :].rearrange("(c p) n -> p c n", p=P)

        slabs = [cols(w["l0_ml_w_in"], SLAB * i) for i in range(6)]
        slabs += [cols(w["l0_ml_w_out"], SLAB * i) for i in range(2)]
        FFN0 = len(slabs)
        for j in range(FJ):
            slabs += [cols(w["l0_ffn_w_gate"], SLAB * j), cols(w["l0_ffn_w_up"], SLAB * j),
                      rows(w["l0_ffn_w_down"], SLAB * j)]
        GDN0 = len(slabs)
        slabs += [cols(w["l1_gdn_w_in"], SLAB * i) for i in range(8)]
        slabs += [cols(w["l1_gdn_w_out"], SLAB * i) for i in range(2)]
        MOE0 = len(slabs)
        PER = 3 * FJ
        order = []
        for j in range(FJ + 1):
            if j < FJ:
                order += [("gate", j), ("up", j)]
            if j > 0:
                order += [("down", j - 1)]
        place = {key: m for m, key in enumerate(order)}

        ffn_slab = {key: FFN0 + m for key, m in place.items()}
        by_kind = {"gate": "l0_ffn_w_gate", "up": "l0_ffn_w_up", "down": "l0_ffn_w_down"}
        for (kind, j), k in ffn_slab.items():
            slabs[k] = (rows if kind == "down" else cols)(w[by_kind[kind]], SLAB * j)

        def unit_view(buf, slot, down):
            return buf[:, slot, :].rearrange("p (c n) -> p c n", c=2 if down else 4)

        MU0 = 2 * MOE0
        UPER = 2 * PER
        AHEAD = CUT

        def products(eng, k, item=0):
            eng.wait_ge(unit_used, item * UPER + (2 * k + 2))

        def cut_hi(act, u, item=0):
            act.wait_ge(landed[u % RAW], item * (16 * UPER // RAW) + 16 * (u // RAW + 1))
            if u >= CUT:
                act.wait_ge(unit_used, item * UPER + (u - CUT + 1))
            act.activation(whi[:, u % CUT, :], raw[:, u % RAW, :], ACT.Copy).then_inc(hi_ok, 1)

        def cut_lo(dve, u, item=0):
            dve.wait_ge(hi_ok, item * UPER + (u + 1))
            dve.tensor_tensor(wlo[:, u % CUT, :], raw[:, u % RAW, :], whi[:, u % CUT, :].bitcast(F32), ALU.subtract) \
               .then_inc(lo_ok, 1)

        class Cuts:

            def __init__(self, eng, cut):
                self.eng, self.cut, self.done = eng, cut, 0

            def to(self, n, item=0):
                while self.done <= n:
                    self.cut(self.eng, self.done, item)
                    self.done += 1

            def through(self, k, item=0):
                self.to(2 * k + CUT, item)

        N_PAR, N_PAR2 = 8, 8

        block = ctx.enter_context(nc.Block())

        @block.sync
        def _(sp):
            xv = w["x"].rearrange("b (c p) d -> p (b c) d", p=P)
            sp.dma_start(x[:, :, :], xv).then_inc(x_in, 16)
            g = [w["l0_norm_mix"], w["l0_ml_head_gain"], w["l0_norm_ffn"], w["l1_norm_mix"], w["l1_norm_ffn"]]
            for i, a in enumerate(g):
                sp.dma_start(packG[DC * i:DC * (i + 1), :], a.rearrange("(c p) -> c p", p=P)).then_inc(par_in, 16)
            sp.dma_start(packG[5 * DC:5 * DC + 1, :], w["l1_gdn_out_gain"].rearrange("(c p) -> c p", p=P)) \
              .then_inc(par_in, 16)

            def small(dst, name, at, m, s):
                sp.dma_start(dst[:, :, :], w[name][:, at:at + m].rearrange("(c p) n -> p c n", p=P)).then_inc(s, 16)

            small(w_if, "l0_ml_w_in", 3072, 2 * ML_H, par_in)
            sp.dma_start(bif[:, :], w["l0_ml_b_if"].partition_broadcast(P)).then_inc(par_in, 16)
            for k, src in enumerate(slabs):
                down = src.shape[1] == FC
                for half in range(2):
                    u, c = 2 * k + half, src.shape[1] // 2
                    if u >= RAW:
                        sp.wait_ge(lo_ok, u - RAW + 1)
                    sp.dma_start(unit_view(raw, u % RAW, down), src[:, c * half:c * (half + 1), :]) \
                      .then_inc(landed[u % RAW], 16)
                if k == 3:
                    for q in range(GD_K):
                        sp.dma_start(packT[24 * q:24 * (q + 1), :],
                                     w["l1_gdn_conv"][q, :].rearrange("(c p) -> c p", p=P)).then_inc(par2_in, 16)
                    small(w_ba, "l1_gdn_w_in", 4096, 2 * GD_H, par2_in)
                    small(w_rt, "l1_moe_router", 0, NE, par2_in)
                    for dst, name in ((dtb, "l1_gdn_dt_bias"), (alog, "l1_gdn_a_log")):
                        sp.dma_start(dst[:, :], w[name].partition_broadcast(P)).then_inc(par2_in, 16)
            moe = {"gate": "l1_moe_w_gate", "up": "l1_moe_w_up", "down": "l1_moe_w_down"}

            def load(it, e, r):
                kind, j = order[r // 2 % PER]
                u, half, wm = MU0 + r, r % 2, w[moe[kind]]
                sp.wait_ge(lo_ok, it * UPER + (u - RAW + 1))
                if kind == "down":
                    part = slice(SLAB * j + 256 * half, SLAB * j + 256 * (half + 1))
                    src = wm[bass.ds(e, 1), part, :]
                else:
                    src = wm[bass.ds(e, 1), 512 * half:512 * (half + 1), SLAB * j:SLAB * (j + 1)]
                sp.dma_start(unit_view(raw, u % RAW, kind == "down"),
                             src.rearrange("a (c p) n -> p (a c) n", p=P)).then_inc(landed[u % RAW], 16)

            def load_round(b):
                with sp.Fori(0, NE) as e:
                    it = sp.snap(b * NE + e)
                    for r in range(UPER):
                        load(it, e, r)

            load_round(0)
            sp.wait_ge(routed, 1)
            nr = sp.value_load(nrounds[0:1, 0:1], min_val=1, max_val=ROUNDS)
            with sp.If(nr > 1):
                with sp.Fori(1, nr) as b:
                    load_round(b)
            for r in range(AHEAD):
                load(nr * NE, 0, r)
            ov = out.rearrange("b (c p) d -> p (b c) d", p=P)
            for c in range(TC):
                sp.wait_ge(fin_ok, c + 1)
                sp.dma_start(ov[:, c, :], fout[:, c, :]).then_inc(stored, 16)
            sp.wait_ge(stored, 16 * TC)

        @block.gpsimd
        def _(pool):
            n = [0]

            def own(ins):
                n[0] += 1
                ins.then_inc(pool_step, 1)

            def settled():
                pool.wait_ge(pool_step, n[0])

            own(pool.memset(ident[:, :], 0.0))
            own(pool.memset(one[:, :], 1.0))
            own(pool.memset(incl[:, :], 1.0))
            own(pool.memset(neg[:, :, :], 0.0))
            own(pool.memset(mhalf[:, :], -0.5))
            own(pool.iota(xorI[:, 0, :], pattern=[[1, P]], base=0, channel_multiplier=0))
            own(pool.iota(xorI[:, 1, :], pattern=[[0, P]], base=0, channel_multiplier=1))
            own(pool.iota(iot[:, :], pattern=[[1, CAP]], base=0, channel_multiplier=0,
                          allow_small_or_imprecise_dtypes=True))
            settled()
            own(pool.affine_select(out=ident[:, :], in_=ident[:, :], compare_op=ALU.not_equal, fill=1.0, base=0,
                                   pattern=[[-1, P]], channel_multiplier=1))
            own(pool.affine_select(out=incl[:, :], in_=incl[:, :], compare_op=ALU.is_ge, fill=0.0, base=0,
                                   pattern=[[1, P]], channel_multiplier=-1))
            for a, op in ((0, ALU.is_gt), (1, ALU.is_ge)):
                own(pool.affine_select(out=neg[:, a, :], in_=neg[:, a, :], compare_op=op, fill=NEG, base=0,
                                       pattern=[[1, P]], channel_multiplier=-1))
            settled()
            pool.memset(mv[:, :, :, 256:257], 1.0).then_inc(consts, 1)

            def root(i, m):
                pool.wait_ge(var_ok[i], 1)
                pool.tensor_tensor(rs[:, i, 0:m], va[:, i, 0:m], mhalf[:, 0:m], ALU.pow).then_inc(rs_ok[i], 1)

            root(0, TC)
            root(1, TC * ML_H)
            root(2, TC)
            pool.wait_ge(res[1], 4)
            pool.memset(graw[:, :, :, 0:GD_K - 1], 0.0).then_inc(consts, 1)
            root(3, TC)
            root(4, TC * GD_H)
            root(5, TC)
            root(6, TC)

        @block.scalar
        def _(act):
            n = [0]

            def own(ins):
                n[0] += 1
                ins.then_inc(act_step, 1)
                act.wait_ge(act_step, n[0])

            def sum_squares(i):
                for c in range(TC):
                    act.activation(xn[:, c, :], x[:, c, :], ACT.Square,
                                   accum_out=ss[:, i, c:c + 1]).then_inc(sq_sum[i], 1)

            def turned(i, gcol):
                def high(k):
                    act.activation(hTr[:, 0, 512 * k:512 * (k + 1)],
                                   hT[:, 2 * k:2 * k + 2, :].rearrange("p a t -> p (a t)"), ACT.Copy) \
                       .then_inc(hT_hi[i], 1)

                for k in (2, 3):
                    act.wait_ge(tr_ok[i], k + 1)
                    for a in range(2):
                        c = 2 * k + a
                        act.activation(hT[:, c, :], b2(k)[:, a, :], ACT.Copy, scale=gcol(c)).then_inc(hT_a[i], 1)
                    if k == 2:
                        for m in range(2):
                            act.wait_ge(hT_d[i], m + 1)
                            high(m)
                for k in (2, 3):
                    act.wait_ge(hT_a[i], 2 * (k - 1))
                    high(k)

            cuts = Cuts(act, cut_hi)

            act.wait_ge(x_in, 16)
            sum_squares(0)
            act.wait_ge(pack_e, 1)
            turned(0, lambda c: gains[:, c:c + 1])
            cuts.to(CUT - 1)

            act.wait_ge(g0_dve, 2)
            act.activation(sm[:, 2, 0:8], sm[:, 1, 0:8], ACT.Exp, scale=-1.0).then_inc(g0_act, 1)
            act.wait_ge(g0_act, 1)
            act.activation(sm[:, 3, 0:8], sm[:, 2, 0:8], ACT.Ln, bias=1.0).then_inc(g0_act, 1)

            for s, dst, scale in ((0, mq, 1.0), (1, mk, ML_DQK ** -0.5)):
                cuts.through(s)
                products(act, s)
                for a in range(2):
                    act.activation(dst[:, 2 * a:2 * a + 2, :], b2([6, 0][s] + a), ACT.Copy, scale=scale) \
                       .then_inc(ev0, 1)
            cuts.through(2)
            act.wait_ge(g0_dve, 8)
            act.activation(sm[:, 8, 0:8], sm[:, 7, 0:8], ACT.Exp, scale=-1.0).then_inc(g0_act, 1)
            for s, at in ((4, 6), (5, 0)):
                cuts.through(s)
                products(act, s)
                for c in range(TC):
                    act.activation(mog[:, c, SLAB * (s - 4):SLAB * (s - 3)], bank[at + c][:, :], ACT.Sigmoid) \
                       .then_inc(ev0, 1)
            cuts.to(2 * 5 + 1 + CUT)
            for h in range(ML_H):
                act.wait_ge(h_bc, h + 1)
                if h >= 2:
                    act.wait_ge(h_sc, h - 1)
                D0 = bank[2 + 4 * (h % 2)]
                act.activation(mw[:, h % 2, 0:256], D0[:, 0:256], ACT.Exp, bias=sm[:, 5, h:h + 1])
                act.activation(mw[:, h % 2, 256:384], D0[:, 256:384], ACT.Exp,
                               bias=sm[:, 5, 4 + h:5 + h]).then_inc(h_w, 1)
            for h in range(ML_H):
                for c in range(TC):
                    act.wait_ge(h_hs, TC * h + c + 1)
                    if h or c:
                        act.wait_ge(sq_sum[1], TC * h + c)
                    act.activation(msq[:, :], xn[:, c, ML_DV * h:ML_DV * (h + 1)], ACT.Square,
                                   accum_out=ss[:, 1, 4 * c + h:4 * c + h + 1]).then_inc(sq_sum[1], 1)
            turned(1, lambda c: gains[:, DC + c:DC + c + 1])

            cuts.to(2 * FFN0 - 1 + CUT)
            act.wait_ge(res[0], 4)
            sum_squares(2)
            turned(2, lambda c: gains[:, 2 * DC + c:2 * DC + c + 1])
            for j in range(FJ):
                cuts.through(ffn_slab[("gate", j)])
                products(act, ffn_slab[("gate", j)])
                if j >= 1:
                    act.wait_ge(f_hh, 2 * j)
                for a in range(2):
                    act.activation(fsg[:, 2 * a:2 * a + 2, :], b2(a), ACT.Silu).then_inc(f_silu, 1)
                if j >= 1:
                    cuts.through(ffn_slab[("up", j)])
                    cuts.through(ffn_slab[("down", j - 1)])
                    products(act, ffn_slab[("down", j - 1)])
                else:
                    cuts.through(ffn_slab[("up", j)])
                for a in range(2):
                    act.wait_ge(f_hh, 2 * j + a + 1)
                    act.activation(hr[:, 0, 512 * a:512 * (a + 1)],
                                   fhh[:, 2 * a:2 * a + 2, :].rearrange("p a t -> p (a t)"), ACT.Copy) \
                       .then_inc(f_hi, 1)
            cuts.to(2 * GDN0 - 1 + CUT)

            act.wait_ge(res[1], 4)
            sum_squares(3)
            turned(3, lambda c: gains[:, 3 * DC + c:3 * DC + c + 1])
            act.wait_ge(par2_in, 16 * N_PAR2)
            act.activation(sm[:, 10, 0:8], alog[:, :], ACT.Exp).then_inc(g1_act, 1)
            act.wait_ge(g1_dve, 3)
            act.activation(sm[:, 14:16, :], sm[:, 12:14, :], ACT.Exp, scale=-1.0).then_inc(g1_act, 1)
            act.wait_ge(g1_act, 2)
            act.activation(sm[:, 16:18, :], sm[:, 14:16, :], ACT.Ln, bias=1.0).then_inc(g1_act, 1)
            cuts.through(GDN0)
            act.wait_ge(g1_dve, 8)
            act.activation(sm[:, 18, :], sm[:, 19, :], ACT.Exp)
            act.activation(sm[:, 20, 0:8], sm[:, 21, 8:16], ACT.Exp)
            act.activation(sm[:, 20, 8:16], sm[:, 22, 8:16], ACT.Exp)
            act.activation(sm[:, 23, 8:16], sm[:, 23, 0:8], ACT.Exp).then_inc(g1_act, 1)
            act.wait_ge(consts, 2)

            def conv_in(s):
                if s >= 2:
                    act.wait_ge(conv_ok, s - 1)
                cuts.through(GDN0 + s)
                products(act, GDN0 + s)
                for a in range(2):
                    act.activation(graw[:, s % 2, 2 * a:2 * a + 2, GD_K - 1:RW], b2(2 * ((s + 3) % 4) + a),
                                   ACT.Copy).then_inc(ev1, 1)

            def conv_act(s):
                dst = (gq, gk, gv)[s // 2][:, 4 * (s % 2):4 * (s % 2) + 4, :]
                act.wait_ge(conv_ok, s + 1)
                ins = act.activation(dst, dst, ACT.Silu)
                if s < 4:
                    own(ins)
                    if s >= 2:
                        act.wait_ge(ssq_pe, 2 * (s - 1))
                    act.activation(sqb[:, s % 2, :, :], dst, ACT.Square).then_inc(sqr_ok, 1)
                else:
                    ins.then_inc(silu_ok, 1)

            conv_in(0)
            for s in range(1, 6):
                conv_in(s)
                conv_act(s - 1)
            conv_act(5)
            for s in range(4):
                act.wait_ge(ssq_ev, 2 * s + 2)
                r = rsq[:, 4 * s:4 * s + 4, :]
                own(act.activation(r, r, ACT.Ln))
                act.activation(r, r, ACT.Exp, scale=-0.5).then_inc(ln_ok, 1)
            for s in (6, 7):
                cuts.through(GDN0 + s)
                products(act, GDN0 + s)
                for c in range(TC):
                    act.activation(gz[:, c, SLAB * (s - 6):SLAB * (s - 5)], bank[2 * ((s + 3) % 4) + c][:, :],
                                   ACT.Silu).then_inc(ev1, 1)
            cuts.to(2 * (GDN0 + 8) - 1 + CUT)
            for h in range(GD_H):
                act.wait_ge(bc_ok, h + 1)
                if h >= 2:
                    act.wait_ge(att_ok, h - 1)
                Db = bank[4 + h % 2][:, :].rearrange("p (a c t) -> p a c t", a=2, c=TC)
                for c in range(TC):
                    ins = act.activation(gam[:, h % 2, :, c, :], Db[:, :, c, :], ACT.Exp,
                                         bias=sm[:, 11, 8 * c + h:8 * c + h + 1])
                ins.then_inc(gam_ok, 1)
            for l in range(1, 7):
                for gi in range(4):
                    act.wait_ge(inv_x, 4 * l + gi + 1)
                    act.activation(xs[:, gi, :, :], b2(2 * gi, 4), ACT.Copy).then_inc(inv_xs, 1)
            for gi in range(2):
                hs = slice(4 * gi, 4 * gi + 4)
                act.wait_ge(s_pe, 2 * gi + 1)
                act.activation(vn[:, 0, hs, :], b2(2 * gi, 4), ACT.Copy).then_inc(s_act, 1)
                act.wait_ge(s_pe, 2 * gi + 2)
                act.activation(nwT[:, hs, :], b2(2 * gi + 1, 4), ACT.Copy, scale=-1.0).then_inc(s_act, 1)
            for gi in range(2):
                hs = slice(4 * gi, 4 * gi + 4)
                act.wait_ge(s_pe, 4 + 3 * gi + 1)
                act.activation(st1[:, hs, :], b2(4 + 2 * gi, 4), ACT.Copy).then_inc(s_act, 1)
            for gi in range(2):
                hs = slice(4 * gi, 4 * gi + 4)
                act.wait_ge(s_pe, 10 + 2 * gi + 1)
                act.activation(vn[:, 1, hs, :], b2(2 * gi, 4), ACT.Copy).then_inc(s_act, 1)
            turned(4, lambda c: gains[:, 5 * DC:5 * DC + 1])
            cuts.to(MU0 - 1 + CUT)

            act.wait_ge(res[2], 4)
            sum_squares(5)
            turned(5, lambda c: gains[:, 4 * DC + c:4 * DC + c + 1])
            act.dma_start(fgain[:, :], w["final_norm"].partition_broadcast(P)).then_inc(par3_in, 16)
            act.wait_ge(r_dve, 1)
            act.activation(rt[:, 6, 0:TC], rt[:, 5, 0:TC], ACT.Exp).then_inc(r_act, 1)
            cuts.to(MU0 + AHEAD - 1)
            act.wait_ge(routed, 1)
            nr = act.value_load(nrounds[0:1, 0:1], min_val=1, max_val=ROUNDS)
            with act.Fori(0, nr) as b:
                with act.Fori(0, NE) as e:
                    it = act.snap(b * NE + e)
                    cuts.done = MU0 + AHEAD
                    act.wait_ge(e_gather, it * 3 + 3)
                    act.activation(eGT[0:CAP, :], bank[0][0:CAP, 0:S], ACT.Copy).then_inc(e_gt, 1)
                    for a in range(2):
                        act.wait_ge(e_xg, it * 2 + (a + 1))
                        act.activation(hTr[:, 0, 4 * CAP * a:4 * CAP * (a + 1)],
                                       exg[:, 4 * a:4 * a + 4, :].rearrange("p a n -> p (a n)"), ACT.Copy) \
                           .then_inc(e_xhi, 1)

                    def high(j):
                        act.wait_ge(e_t, it * FJ + (j + 1))
                        act.activation(hr[:, 0, 0:FC * CAP], bank[2][:, 0:FC * CAP], ACT.Copy).then_inc(e_thi, 1)

                    for j in range(FJ):
                        k = MOE0 + place[("gate", j)]
                        cuts.through(k, it)
                        products(act, k, it)
                        if j >= 1:
                            act.wait_ge(e_hh, it * FJ + j)
                        act.activation(esg[0:CAP, :], bank[0][0:CAP, :], ACT.Silu).then_inc(e_silu, 1)
                        if j >= 1:
                            high(j - 1)
                    cuts.through(MOE0 + place[("up", FJ - 1)], it)
                    high(FJ - 1)
                    cuts.through(MOE0 + PER - 1, it)
                    products(act, MOE0 + PER - 1, it)
                    act.activation(eyg[0:CAP, 0:512], bank[6][0:CAP, :], ACT.Copy).then_inc(e_yg, 1)
                    cuts.to(MU0 + UPER + AHEAD - 1, it)
            act.wait_ge(e_x, nr * (4 * NE) + 1)
            sum_squares(6)

        @block.vector
        def _(dve):
            n = [0]

            def own(ins):
                n[0] += 1
                ins.then_inc(dve_step, 1)

            def settled():
                dve.wait_ge(dve_step, n[0])

            def step(ins):
                own(ins)
                settled()

            cuts = Cuts(dve, cut_lo)

            def level_masks(l):
                if l == 0:
                    step(dve.tensor_tensor(xorI[:, 2, :], xorI[:, 0, :], xorI[:, 1, :], ALU.bitwise_xor))
                    step(dve.tensor_copy(xorF[:, 0, :], xorI[:, 2, :]))
                    step(dve.tensor_tensor(xorF[:, 2, :], xorF[:, 0, :], incl[:, :], ALU.mult))
                    step(dve.tensor_tensor(xorF[:, 1, :], xorF[:, 0, :], xorF[:, 2, :], ALU.subtract))
                for dst, src in ((low, xorF[:, 1, :]), (upp, xorF[:, 2, :])):
                    step(dve.tensor_scalar(xorF[:, 0, :], src, float(2 ** l), None, ALU.is_ge))
                    step(dve.scalar_tensor_tensor(out=dst[:, l, :], in0=src, scalar=float(2 ** (l + 1)),
                                                  in1=xorF[:, 0, :], op0=ALU.is_lt, op1=ALU.mult))

            dve.wait_ge(consts, 1)
            dve.wait_ge(pack_t, 1)
            dve.tensor_copy(gains[:, :], bank[4][:, 0:5 * DC + 1]).then_inc(pack_e, 1)

            def normed(i, m, slot, width, last=False):
                dve.tensor_scalar(va[:, i, 0:m], ss[:, i, 0:m], 1.0 / width, EPS, ALU.mult, ALU.add) \
                   .then_inc(var_ok[i], 1)
                dve.wait_ge(rs_ok[i], 1)

            def norm(i, k):
                dve.wait_ge(sq_sum[i], TC)
                normed(i, TC, i, D)
                for c in range(TC):
                    dve.tensor_scalar(xn[:, c, :], x[:, c, :], rs[:, i, c:c + 1], None, ALU.mult) \
                       .then_inc(xn_ok[k], 1)

            def turned(i, g):
                for k in (0, 1):
                    dve.wait_ge(tr_ok[i], k + 1)
                    dve.tensor_tensor(hT[:, 2 * k:2 * k + 2, :], b2(k), g(k).to_broadcast([P, 2, S]), ALU.mult) \
                       .then_inc(hT_d[i], 1)
                for k in range(4):
                    part = slice(512 * k, 512 * (k + 1))
                    dve.wait_ge(hT_hi[i], k + 1)
                    dve.tensor_tensor(hTr[:, 1, part], hT[:, 2 * k:2 * k + 2, :].rearrange("p a t -> p (a t)"),
                                      hTr[:, 0, part].bitcast(F32), ALU.subtract).then_inc(hT_lo[i], 1)

            def gcol(i):
                return lambda k: gains[:, DC * i + 2 * k:DC * i + 2 * k + 2].unsqueeze(2)

            dve.wait_ge(pack_e, 1)
            norm(0, 0)
            turned(0, gcol(0))
            cuts.to(CUT - 1)
            G = sm[:, 0, :].rearrange("p (c n) -> p c n", c=TC)
            dve.wait_ge(g0_pe, 1)
            dve.wait_ge(par_in, 16 * N_PAR)
            dve.tensor_tensor(G, bank[4][:, 0:16].rearrange("p (c n) -> p c n", c=TC),
                              bif[:, :].unsqueeze(1).to_broadcast([P, TC, 8]), ALU.add).then_inc(g0_dve, 1)
            dve.wait_ge(g0_dve, 1)
            four = "p (c n) -> p c n"
            dve.scalar_tensor_tensor(out=sm[:, 1, 0:8].rearrange(four, c=TC), in0=G[:, :, 4:8], scalar=-1.0,
                                     in1=G[:, :, 4:8], op0=ALU.mult, op1=ALU.max).then_inc(g0_dve, 1)
            dve.wait_ge(g0_act, 2)
            dve.scalar_tensor_tensor(out=sm[:, 4, 0:8].rearrange(four, c=TC), in0=G[:, :, 4:8], scalar=0.0,
                                     in1=sm[:, 3, 0:8].rearrange(four, c=TC), op0=ALU.min,
                                     op1=ALU.subtract).then_inc(g0_dve, 1)
            cuts.through(0)
            dve.wait_ge(g0_pe, 2)
            own(dve.tensor_copy(sm[:, 6, 0:8], bank[5][:, 0:8]))
            dve.tensor_tensor(sm[:, 5, 0:8].rearrange(four, c=TC), G[:, :, 0:4],
                              bank[5][:, 0:8].rearrange(four, c=TC), ALU.subtract).then_inc(g0_dve, 1)
            cuts.through(1)
            dve.wait_ge(g0_pe, 3)
            dve.tensor_copy(mrow[0:4, 0, :], bank[5][0:4, 256:512]).then_inc(g0_dve, 1)
            dve.wait_ge(g0_dve, 5)
            dve.tensor_tensor_scan(mrow[0:4, 1, :], mrow[0:4, 0, :], mrow[0:4, 0, :], 0.0, ALU.max, ALU.max) \
               .then_inc(g0_dve, 1)
            dve.wait_ge(g0_dve, 6)
            dve.tensor_scalar(mrow[0:4, 2, :], mrow[0:4, 1, :], -1.0, None, ALU.mult).then_inc(g0_dve, 1)
            cuts.through(2)
            dve.wait_ge(g0_pe, 4)
            dve.tensor_tensor(sm[:, 7, 0:8], sm[:, 6, 0:8], bank[5][:, 16:24], ALU.add).then_inc(g0_dve, 1)
            for s, at in ((2, 2), (3, 4)):
                cuts.through(s)
                products(dve, s)
                for c in range(TC):
                    dve.tensor_copy(mv[:, c, 2 * (s - 2):2 * (s - 2) + 2, 0:256], b2(at + c)).then_inc(ev0v, 1)

            def head_scores(h):
                dve.wait_ge(h_w, h + 1)
                dve.wait_ge(h_qk, h + 1)
                dve.tensor_tensor(msc[:, h % 2, :], bank[3 + 4 * (h % 2)][:, 0:384], mw[:, h % 2, :], ALU.mult) \
                   .then_inc(h_sc, 1)

            def head_out(h):
                dve.wait_ge(h_num, h + 1)
                for c in range(TC):
                    nb = bank[(0, 4)[h % 2] + c]
                    e_m = sm[:, 8, 4 * c + h:4 * c + h + 1]
                    step(dve.tensor_tensor(den[:, 0, c:c + 1], nb[:, 256:257], e_m, ALU.max))
                    step(dve.scalar_tensor_tensor(out=den[:, 0, c:c + 1], in0=nb[:, 256:257], scalar=-1.0,
                                                  in1=den[:, 0, c:c + 1], op0=ALU.mult, op1=ALU.max))
                    step(dve.reciprocal(den[:, 1, c:c + 1], den[:, 0, c:c + 1]))
                    dve.tensor_scalar(xn[:, c, ML_DV * h:ML_DV * (h + 1)], nb[:, 0:256], den[:, 1, c:c + 1], None,
                                      ALU.mult).then_inc(h_hs, 1)

            cuts.to(2 * 5 + 1 + CUT)
            dve.wait_ge(g0_act, 3)
            for h in range(ML_H):
                head_scores(h)
                if h >= 1:
                    head_out(h - 1)
            head_out(ML_H - 1)
            dve.wait_ge(sq_sum[1], TC * ML_H)
            normed(1, TC * ML_H, 1, ML_DV)
            for c in range(TC):
                for h in range(ML_H):
                    v = xn[:, c, ML_DV * h:ML_DV * (h + 1)]
                    ins = dve.scalar_tensor_tensor(out=v, in0=v, scalar=rs[:, 1, 4 * c + h:4 * c + h + 1],
                                                   in1=mog[:, c, ML_DV * h:ML_DV * (h + 1)],
                                                   op0=ALU.mult, op1=ALU.mult)
                ins.then_inc(xn_ok[1], 1)
            turned(1, gcol(1))

            def residual(i, ready, banks):
                for m, (c, half, at) in enumerate(banks):
                    if len(ready) == 2 and m % 2 == 0:
                        cuts.through(ready[m // 2])
                        products(dve, ready[m // 2])
                    v = x[:, c, 512 * half:512 * (half + 1)]
                    dve.tensor_tensor(v, v, bank[at][:, :], ALU.add).then_inc(res[i], 1)

            proj_banks = [(c, half, 4 + 2 * half + c) for half in range(2) for c in range(TC)]
            residual(0, (6, 7), proj_banks)
            cuts.to(2 * FFN0 - 1 + CUT)

            dve.wait_ge(res[0], 4)
            norm(2, 2)
            turned(2, gcol(2))
            for j in range(FJ):
                cuts.through(ffn_slab[("gate", j)])
                cuts.through(ffn_slab[("up", j)])
                products(dve, ffn_slab[("up", j)])
                for a in range(2):
                    dve.wait_ge(f_silu, 2 * j + a + 1)
                    dve.tensor_tensor(fhh[:, 2 * a:2 * a + 2, :], b2(2 + a), fsg[:, 2 * a:2 * a + 2, :],
                                      ALU.mult).then_inc(f_hh, 1)
                if j >= 1:
                    cuts.through(ffn_slab[("down", j - 1)])
                for a in range(2):
                    part = slice(512 * a, 512 * (a + 1))
                    dve.wait_ge(f_hi, 2 * j + a + 1)
                    dve.tensor_tensor(hr[:, 1, part], fhh[:, 2 * a:2 * a + 2, :].rearrange("p a t -> p (a t)"),
                                      hr[:, 0, part].bitcast(F32), ALU.subtract).then_inc(f_lo, 1)
                level_masks(j)
            cuts.through(ffn_slab[("down", FJ - 1)])
            products(dve, ffn_slab[("down", FJ - 1)])
            residual(1, (), [(c, half, 4 + 2 * c + half) for c in range(TC) for half in range(2)])

            cuts.to(2 * GDN0 - 1 + CUT)

            dve.wait_ge(tap_t, 1)
            dve.tensor_copy(taps[:, :, :].rearrange("p a b -> p (a b)"), bank[0][:, 0:96]).then_inc(tap_e, 1)
            dve.wait_ge(res[1], 4)
            norm(3, 3)
            turned(3, gcol(3))
            SB = sm[:, 0:2, :]
            dve.wait_ge(g1_pe, 1)
            bk = bank[4][:, 0:32].rearrange("p (c n) -> p c n", c=TC)
            own(dve.tensor_copy(SB[:, :, 0:8], bk[:, :, 0:8]))
            own(dve.tensor_tensor(SB[:, :, 8:16], bk[:, :, 8:16], dtb[:, :].unsqueeze(1).to_broadcast([P, TC, 8]),
                                  ALU.add))
            settled()
            dve.scalar_tensor_tensor(out=sm[:, 12:14, :], in0=SB, scalar=-1.0, in1=SB, op0=ALU.mult,
                                     op1=ALU.max).then_inc(g1_dve, 3)
            dve.wait_ge(g1_act, 3)
            lnb = sm[:, 19, :].rearrange("p (c n) -> p c n", c=TC)
            gg = sm[:, 4, :].rearrange("p (c n) -> p c n", c=TC)
            own(dve.scalar_tensor_tensor(out=lnb, in0=SB[:, :, 0:8], scalar=0.0, in1=sm[:, 16:18, 0:8], op0=ALU.min,
                                         op1=ALU.subtract))
            step(dve.scalar_tensor_tensor(out=sm[:, 2:4, 0:8], in0=SB[:, :, 8:16], scalar=0.0,
                                          in1=sm[:, 16:18, 8:16], op0=ALU.max, op1=ALU.add))
            dve.scalar_tensor_tensor(out=gg, in0=sm[:, 2:4, 0:8], scalar=-1.0,
                                     in1=sm[:, 10, 0:8].unsqueeze(1).to_broadcast([P, TC, 8]),
                                     op0=ALU.mult, op1=ALU.mult).then_inc(g1_dve, 1)
            cuts.through(GDN0)
            dve.wait_ge(g1_pe, 2)
            own(dve.tensor_scalar(sm[:, 11, :], bank[5][:, 0:16], -1.0, None, ALU.mult))
            own(dve.tensor_copy(sm[:, 22, :], bank[5][:, 0:16]))
            settled()
            own(dve.tensor_tensor(sm[:, 23, 0:8], sm[:, 11, 0:8], bank[5][:, 16:24], ALU.add))
            own(dve.tensor_tensor(sm[:, 21, :], sm[:, 19, :], sm[:, 22, :], ALU.add))
            settled()
            dve.tensor_copy(sm[:, 9, :], sm[:, 22, :]).then_inc(g1_dve, 4)
            cuts.through(GDN0 + 1)
            dve.wait_ge(g1_pe, 3)
            dve.tensor_copy(rows2[0:8, :, :].rearrange("p a t -> p (a t)"), bank[4][0:8, :]).then_inc(g1_dve, 1)

            def conv(s):
                dst = (gq, gk, gv)[s // 2]
                cuts.through(GDN0 + s)
                dve.wait_ge(ev1, 2 * s + 2)
                if s == 0:
                    dve.wait_ge(tap_e, 1)
                for k in range(GD_K):
                    for a in range(4):
                        o = dst[:, 4 * (s % 2) + a, :]
                        i = graw[:, s % 2, a, k:k + S]
                        t = taps[:, k, 4 * s + a:4 * s + a + 1]
                        if k == 0:
                            ins = dve.tensor_scalar(o, i, t, None, ALU.mult)
                        else:
                            ins = dve.scalar_tensor_tensor(out=o, in0=i, scalar=t, in1=o, op0=ALU.mult, op1=ALU.add)
                        if k < GD_K - 1:
                            own(ins)
                    if k < GD_K - 1:
                        settled()
                ins.then_inc(conv_ok, 1)

            def squares(s):
                for a in range(2):
                    dve.wait_ge(ssq_pe, 2 * s + a + 1)
                    dve.tensor_scalar(rsq[:, 4 * s + 2 * a:4 * s + 2 * a + 2, :], b2([6, 0, 2, 4][s] + a), EPS, None,
                                      ALU.add).then_inc(ssq_ev, 1)

            for s in range(6):
                conv(s)
                if 2 <= s < 6:
                    squares(s - 2)
            for s in range(4):
                dst = (gq, gk)[s // 2][:, 4 * (s % 2):4 * (s % 2) + 4, :]
                if s % 2 == 0:
                    cuts.through(GDN0 + 6 + s // 2)
                dve.wait_ge(ln_ok, s + 1)
                dve.scalar_tensor_tensor(out=dst, in0=rsq[:, 4 * s:4 * s + 4, :],
                                         scalar=GD_DK ** -0.5 if s < 2 else 1.0, in1=dst,
                                         op0=ALU.mult, op1=ALU.mult).then_inc(qk_ok, 1)
            cuts.to(2 * (GDN0 + 8) - 1 + CUT)
            dve.wait_ge(g1_act, 4)
            for gi in range(8):
                hg = gi % 2
                hs = slice(4 * hg, 4 * hg + 4)
                dve.wait_ge(kv_t, 8 if gi >= 4 else gi + 1)
                if gi < 2:
                    dst, sc = kbg[:, hs, :], sm[:, 20, 4 * hg:4 * hg + 4]
                elif gi < 4:
                    dst, sc = kdec[:, hs, :], sm[:, 23, 8 + 4 * hg:12 + 4 * hg]
                else:
                    c = (gi - 4) // 2
                    dst, sc = vb[:, c, hs, :], sm[:, 18, 8 * c + 4 * hg:8 * c + 4 * hg + 4]
                dve.tensor_tensor(dst, b2([0, 1, 2, 3, 4, 5, 6, 7][gi], 4), sc.unsqueeze(2).to_broadcast([P, 4, P]),
                                  ALU.mult).then_inc(kv_ev, 1)
            for h in range(GD_H):
                dve.wait_ge(gam_ok, h + 1)
                dve.wait_ge(kq_ok, h + 1)
                kq = bank[h % 2][:, :].rearrange("p (a c t) -> p a c t", a=2, c=TC)
                own(dve.scalar_tensor_tensor(out=nAT[:, :, h, :], in0=kq[:, 0], scalar=-1.0, in1=gam[:, h % 2, 0],
                                             op0=ALU.mult, op1=ALU.mult))
                dve.tensor_tensor(attT[:, :, h, :], kq[:, 1], gam[:, h % 2, 1], ALU.mult).then_inc(att_ok, 1)
            settled()
            for gi in range(4):
                c, hs = gi // 2, slice(4 * (gi % 2), 4 * (gi % 2) + 4)
                eye = ident[:, :].unsqueeze(1).to_broadcast([P, 4, P])
                own(dve.tensor_copy(Tn[:, c, hs, :], eye))
                own(dve.tensor_copy(Tt[:, c, hs, :], eye))
            settled()
            for l in range(7):
                lo = low[:, l, :].unsqueeze(1).to_broadcast([P, 4, P])
                up = upp[:, l, :].unsqueeze(1).to_broadcast([P, 4, P])
                for gi in range(4):
                    c, hs = gi // 2, slice(4 * (gi % 2), 4 * (gi % 2) + 4)
                    if l == 0:
                        dve.wait_ge(inv_x, gi + 1)
                        own(dve.copy_predicated(Tn[:, c, hs, :], lo, b2(2 * gi, 4)))
                        dve.copy_predicated(Tt[:, c, hs, :], up, nAT[:, c, hs, :]).then_inc(inv_t, 1)
                        continue
                    dve.wait_ge(inv_d, 4 * (l - 1) + gi + 1)
                    if l < 6:
                        own(dve.copy_predicated(Tn[:, c, hs, :], lo, b2(2 * gi, 4)))
                    dve.copy_predicated(Tt[:, c, hs, :], up, b2(2 * gi + 1, 4)).then_inc(inv_t, 1)
            og = xn[:, :, :].rearrange("p c (h d) -> p c h d", h=GD_H)
            for gi in range(2):
                hs = slice(4 * gi, 4 * gi + 4)
                dve.wait_ge(s_pe, 4 + 3 * gi + 2)
                own(dve.tensor_copy(og[:, 0, hs, :], b2(5 + 2 * gi, 4)))
                dve.wait_ge(s_pe, 4 + 3 * gi + 3)
                dve.tensor_tensor(og[:, 1, hs, :], b2(1 + 2 * gi, 4),
                                  sm[:, 20, 8 + 4 * gi:12 + 4 * gi].unsqueeze(2).to_broadcast([P, 4, P]),
                                  ALU.mult).then_inc(s_dve, 1)
            for gi in range(2):
                hs = slice(4 * gi, 4 * gi + 4)
                dve.wait_ge(s_pe, 10 + 2 * gi + 2)
                dve.wait_ge(s_dve, gi + 1)
                own(dve.tensor_tensor(og[:, 1, hs, :], og[:, 1, hs, :], b2(4 + 2 * gi, 4), ALU.add))
            settled()
            xr = xn[:, :, :].rearrange("p c (h d) -> p (c h) d", h=GD_H)
            step(dve.tensor_tensor(osq, xr, xr, ALU.mult))
            step(dve.tensor_reduce(ss[:, 4, :], osq, AX.X, ALU.add))
            normed(4, TC * GD_H, 4, GD_DV)
            for c in range(TC):
                own(dve.tensor_tensor(og[:, c], og[:, c], rs[:, 4, 8 * c:8 * c + 8].unsqueeze(2)
                                      .to_broadcast([P, 8, P]), ALU.mult))
            settled()
            for c in range(TC):
                dve.tensor_tensor(xn[:, c, :], xn[:, c, :], gz[:, c, :], ALU.mult).then_inc(xn_ok[4], 1)
            turned(4, lambda k: gains[:, 5 * DC:5 * DC + 1].unsqueeze(2))
            residual(2, (GDN0 + 8, GDN0 + 9), proj_banks)
            cuts.to(MU0 - 1 + CUT)

            dve.wait_ge(res[2], 4)
            norm(5, 5)
            turned(5, gcol(4))
            r16 = "p (c n) -> p c n"

            def t8(i):
                return rt[:, i, :].rearrange(r16, c=TC)

            ramp = iot[:, 0:NE].unsqueeze(1).to_broadcast([P, TC, NE])

            def col(i):
                return rt[:, i, 0:TC]

            def wide(i):
                return col(i).unsqueeze(2).to_broadcast([P, TC, NE])

            dve.wait_ge(r_pe, 1)
            step(dve.tensor_copy(t8(0), bank[4][:, 0:16].rearrange(r16, c=TC)))

            def top(src, m, hot):
                step(dve.tensor_reduce(col(m), t8(src), AX.X, ALU.max))
                step(dve.tensor_tensor(t8(8), t8(src), wide(m), ALU.is_equal))
                step(dve.scalar_tensor_tensor(out=t8(8), in0=t8(8), scalar=-100.0, in1=ramp, op0=ALU.mult,
                                              op1=ALU.add))
                step(dve.tensor_reduce(col(9), t8(8), AX.X, ALU.min))
                step(dve.tensor_tensor(t8(hot), t8(8), wide(9), ALU.is_equal))

            top(0, 3, 1)
            step(dve.scalar_tensor_tensor(out=t8(7), in0=t8(1), scalar=NEG, in1=t8(0), op0=ALU.mult, op1=ALU.add))
            top(7, 4, 2)
            dve.tensor_tensor(col(5), col(4), col(3), ALU.subtract).then_inc(r_dve, 1)
            dve.tensor_tensor(t8(10), t8(1), t8(2), ALU.add).then_inc(r_dve, 1)
            dve.wait_ge(r_act, 1)
            step(dve.tensor_scalar(col(11), col(6), 1.0, None, ALU.add))
            step(dve.reciprocal(col(12), col(11)))
            step(dve.tensor_tensor(col(13), col(6), col(12), ALU.mult))
            own(dve.tensor_tensor(t8(1), t8(1), wide(12), ALU.mult))
            step(dve.tensor_tensor(t8(2), t8(2), wide(13), ALU.mult))
            step(dve.tensor_tensor(gate9[:, :, 0:NE], t8(1), t8(2), ALU.add))
            own(dve.tensor_copy(gate9[:, :, NE:NE + 1], gate9[:, :, 0:1]))
            dve.wait_ge(r_pe, 2)
            rk = bank[5][:, 0:16].rearrange(r16, c=TC)
            step(dve.tensor_tensor(t8(14), rk, t8(10), ALU.mult))
            step(dve.tensor_scalar(posm[:, :, 0:NE], t8(14), -1.0, None, ALU.add))
            dve.tensor_scalar(posm[:, :, NE:NE + 1], posm[:, :, 0:1], -float(CAP), None, ALU.add).then_inc(e_x, 1)
            dve.wait_ge(e_x, 1)
            step(dve.tensor_reduce(rt[0:1, 15, 0:1], bank[5][0:1, 16:24], AX.X, ALU.max))
            step(dve.tensor_scalar(rt[0:1, 15, 1:2], rt[0:1, 15, 0:1], -0.5, None, ALU.is_gt))
            for b in range(1, ROUNDS):
                step(dve.scalar_tensor_tensor(out=rt[0:1, 15, b + 1:b + 2], in0=rt[0:1, 15, 0:1],
                                              scalar=float(b * CAP), in1=rt[0:1, 15, b:b + 1], op0=ALU.is_gt,
                                              op1=ALU.add))
            dve.tensor_copy(nrounds[0:1, 0:1], rt[0:1, 15, ROUNDS:ROUNDS + 1]).then_inc(routed, 1)
            settled()
            dve.wait_ge(routed, 1)

            def select(e):
                for c in range(TC):
                    dve.tensor_scalar(eP[:, c, :], iot[:, 0:CAP], posm[:, c, bass.ds(e, 1)], None, ALU.is_equal)
                for c in range(TC):
                    ins = dve.tensor_scalar(ePG[:, c, :], iot[:, 0:CAP], posm[:, c, bass.ds(e, 1)],
                                            gate9[:, c, bass.ds(e, 1)], ALU.is_equal, ALU.mult)
                ins.then_inc(e_sel, 1)

            select(0)
            nr = dve.value_load(nrounds[0:1, 0:1], min_val=1, max_val=ROUNDS)
            gm = gcol(4)
            with dve.Fori(0, nr) as b:
                with dve.Fori(0, NE) as e:
                    it = dve.snap(b * NE + e)
                    cuts.done = MU0 + AHEAD
                    for a in range(2):
                        dve.wait_ge(e_gather, it * 3 + (a + 1))
                        gh = gains[:, 4 * DC + 4 * a:4 * DC + 4 * a + 4].unsqueeze(2).to_broadcast([P, 4, CAP])
                        dve.tensor_tensor(exg[:, 4 * a:4 * a + 4, :],
                                          bank[4 + a][:, 0:4 * CAP].rearrange("p (a n) -> p a n", a=4), gh,
                                          ALU.mult).then_inc(e_xg, 1)
                    for a in range(2):
                        part = slice(4 * CAP * a, 4 * CAP * (a + 1))
                        dve.wait_ge(e_xhi, it * 2 + (a + 1))
                        dve.tensor_tensor(hTr[:, 1, part], exg[:, 4 * a:4 * a + 4, :].rearrange("p a n -> p (a n)"),
                                          hTr[:, 0, part].bitcast(F32), ALU.subtract).then_inc(e_xlo, 1)

                    def low_part(j):
                        dve.wait_ge(e_thi, it * FJ + (j + 1))
                        dve.tensor_tensor(hr[:, 1, 0:FC * CAP], bank[2][:, 0:FC * CAP],
                                          hr[:, 0, 0:FC * CAP].bitcast(F32), ALU.subtract).then_inc(e_tlo, 1)

                    for j in range(FJ):
                        k = MOE0 + place[("gate", j)]
                        cuts.through(k, it)
                        if j >= 1:
                            low_part(j - 1)
                        k = MOE0 + place[("up", j)]
                        cuts.through(k, it)
                        products(dve, k, it)
                        dve.wait_ge(e_silu, it * FJ + (j + 1))
                        if j >= 1:
                            dve.wait_ge(e_t, it * FJ + j)
                        dve.tensor_tensor(ehh[0:CAP, :], bank[1][0:CAP, :], esg[0:CAP, :], ALU.mult) \
                           .then_inc(e_hh, 1)
                        if j == 3:
                            select(e + 1)
                    low_part(FJ - 1)
                    cuts.through(MOE0 + PER - 1, it)
                    products(dve, MOE0 + PER - 1, it)
                    dve.tensor_copy(eyg[0:CAP, 512:1024], bank[7][0:CAP, :]).then_inc(e_yg2, 1)
                    for m in range(4):
                        c, half = m // 2, m % 2
                        dve.wait_ge(e_sc, it * 4 + (m + 1))
                        v = x[:, c, 512 * half:512 * (half + 1)]
                        dve.tensor_tensor(v, v, bank[3 - m % 2][:, :], ALU.add).then_inc(e_x, 1)
                    cuts.to(MU0 + UPER + AHEAD - 1, it)
                dve.wait_ge(e_sel, b * NE + (NE + 1))
                dve.tensor_scalar(posm[:, :, :], posm[:, :, :], -float(CAP), None, ALU.add).then_inc(e_own, 1)
                dve.wait_ge(e_own, b + 1)

            dve.wait_ge(sq_sum[6], TC)
            normed(6, TC, 6, D)
            dve.wait_ge(par3_in, 16)
            for c in range(TC):
                dve.scalar_tensor_tensor(out=fout[:, c, :], in0=x[:, c, :], scalar=rs[:, 6, c:c + 1],
                                         in1=fgain[:, :], op0=ALU.mult, op1=ALU.mult).then_inc(fin_ok, 1)

        @block.tensor
        def _(pe):
            mm = pe.matmul

            def ready(u):
                pe.wait_ge(lo_ok, u + 1)

            def three(o, sh, sl, mh, ml, start, stop):
                mm(o, sh, mh, start=start, stop=False, skip_group_check=True)
                mm(o, sh, ml, start=False, stop=False, skip_group_check=True)
                return mm(o, sl, mh, start=False, stop=stop, skip_group_check=True)

            xh = hTr[:, 0, :].rearrange("p (c t) -> p c t", c=DC)
            xl = hTr[:, 1, :].rearrange("p (c t) -> p c t", c=DC)

            def turn(i):
                pe.wait_ge(xn_ok[i], TC)
                for k in range(4):
                    for a in range(2):
                        for c in range(TC):
                            d = 2 * k + a
                            ins = pe.transpose(bank[k][:, a * S + c * P:a * S + (c + 1) * P],
                                               xn[:, c, d * P:(d + 1) * P], ident[:, :])
                    ins.then_inc(tr_ok[i], 1)

            def fresh_part(i, c):
                if i is not None and c % 2 == 0:
                    pe.wait_ge(hT_lo[i], c // 2 + 1)

            def tall(k, at, fresh=None):
                for c in range(DC):
                    u = 2 * k + c // 4
                    if c % 4 == 0:
                        ready(u)
                    fresh_part(fresh, c)
                    wh, wl = unit_view(whi, u % CUT, False)[:, c % 4], unit_view(wlo, u % CUT, False)[:, c % 4]
                    for a in range(4):
                        o = bank[at + a // 2][:, (a % 2) * S:(a % 2 + 1) * S]
                        v = slice(a * P, (a + 1) * P)
                        ins = three(o, wh[:, v], wl[:, v], xh[:, c, :], xl[:, c, :],
                                    start=(c == 0 and a % 2 == 0), stop=(c == DC - 1))
                    if c % 4 == 3:
                        ins.then_inc(unit_used, 1)

            def flat(k, at, fresh=None):
                for c in range(DC):
                    u = 2 * k + c // 4
                    if c % 4 == 0:
                        ready(u)
                    fresh_part(fresh, c)
                    wh, wl = unit_view(whi, u % CUT, False)[:, c % 4], unit_view(wlo, u % CUT, False)[:, c % 4]
                    for t in range(TC):
                        v = slice(t * P, (t + 1) * P)
                        ins = three(bank[at + t][:, :], xh[:, c, v], xl[:, c, v], wh, wl,
                                    start=(c == 0), stop=(c == DC - 1))
                    if c % 4 == 3:
                        ins.then_inc(unit_used, 1)

            pe.wait_ge(consts, 1)
            pe.wait_ge(par_in, 16 * N_PAR)
            pe.transpose(bank[4][:, 0:41], packG[0:41, :], ident[0:41, 0:41]).then_inc(pack_t, 1)

            turn(0)
            pe.wait_ge(pack_e, 1)
            pe.wait_ge(hT_lo[0], 4)
            for t in range(TC):
                for c in range(DC):
                    ins = mm(bank[4][:, 8 * t:8 * t + 8], hT[:, c, t * P:(t + 1) * P], w_if[:, c, :],
                             start=(c == 0), stop=(c == DC - 1))
            ins.then_inc(g0_pe, 1)
            tall(0, 6)
            pe.wait_ge(g0_dve, 3)
            lf = sm[:, 4, :]
            mm(bank[5][:, 0:4], incl[:, :], lf[:, 0:4], start=True, stop=True)
            mm(bank[5][:, 4:8], incl[:, :], lf[:, 4:8], start=True, stop=False)
            mm(bank[5][:, 4:8], ones, lf[:, 0:4], start=False, stop=True).then_inc(g0_pe, 1)
            tall(1, 0)
            pe.wait_ge(g0_dve, 4)
            for c in range(TC):
                ins = pe.transpose(bank[5][0:4, 256 + c * P:256 + (c + 1) * P], sm[:, 5, 4 * c:4 * c + 4], ident[:, :])
            ins.then_inc(g0_pe, 1)
            flat(2, 2)
            pe.wait_ge(g0_dve, 7)
            for c in range(TC):
                ins = pe.transpose(bank[5][:, 16 + 4 * c:20 + 4 * c], mrow[0:4, 1, c * P:(c + 1) * P], ident[0:4, 0:4])
            ins.then_inc(g0_pe, 1)
            pe.wait_ge(g0_dve, 8)
            flat(3, 4)
            pe.wait_ge(ev0, 2)
            flat(4, 6)
            pe.wait_ge(ev0, 4)
            flat(5, 0)

            def weigh(h):
                o = bank[2 + 4 * (h % 2)]
                pick = ident[0:4, h:h + 1].to_broadcast([4, P])
                nmu = mrow[0:4, 2, :]
                if h >= 2:
                    pe.wait_ge(h_w, h - 1)
                mm(o[:, 0:256], pick, nmu, start=True, stop=False)
                mm(o[:, 0:128], ident[:, :], neg[:, 1, :], start=False, stop=True)
                mm(o[:, 256:384], pick, nmu[:, 128:256], start=True, stop=False)
                mm(o[:, 256:384], ident[:, :], neg[:, 1, :], start=False, stop=True).then_inc(h_bc, 1)
                if h >= 2:
                    pe.wait_ge(h_sc, h - 1)
                o = bank[3 + 4 * (h % 2)]
                mm(o[:, 0:256], mk[:, h, 0:128], mq[:, h, :], start=True, stop=True)
                mm(o[:, 256:384], mk[:, h, 128:256], mq[:, h, 128:256], start=True, stop=True).then_inc(h_qk, 1)

            def gather_values(h):
                pe.wait_ge(h_sc, h + 1)
                if h >= 2:
                    pe.wait_ge(h_hs, TC * (h - 1))
                sc = msc[:, h % 2, :]
                at = (0, 4)[h % 2]
                mm(bank[at][:, 0:257], sc[:, 0:128], mv[:, 0, h, :], start=True, stop=True)
                mm(bank[at + 1][:, 0:257], sc[:, 128:256], mv[:, 0, h, :], start=True, stop=False)
                mm(bank[at + 1][:, 0:257], sc[:, 256:384], mv[:, 1, h, :], start=False, stop=True).then_inc(h_num, 1)

            pe.wait_ge(ev0v, 4)
            weigh(0)
            pe.wait_ge(ev0, 8)
            for h in range(ML_H):
                if h + 1 < ML_H:
                    weigh(h + 1)
                gather_values(h)
            turn(1)
            pe.wait_ge(h_hs, TC * ML_H)
            flat(6, 4, 1)
            flat(7, 6)

            def ffn_in(kind, j, at):
                if j >= 1:
                    pe.wait_ge(f_silu if kind == "gate" else f_hh, 2 * j)
                tall(ffn_slab[(kind, j)], at, 2 if j == 0 and kind == "gate" else None)

            fh = hr[:, 0, :].rearrange("p (a t) -> p a t", a=FC)
            fl = hr[:, 1, :].rearrange("p (a t) -> p a t", a=FC)

            def ffn_out(j):
                k = ffn_slab[("down", j)]
                for a in range(FC):
                    u = 2 * k + a // 2
                    if a % 2 == 0:
                        ready(u)
                        pe.wait_ge(f_lo, 2 * j + a // 2 + 1)
                    wh, wl = unit_view(whi, u % CUT, True)[:, a % 2], unit_view(wlo, u % CUT, True)[:, a % 2]
                    for t in range(TC):
                        v = slice(t * P, (t + 1) * P)
                        for half in range(2):
                            n = slice(512 * half, 512 * (half + 1))
                            ins = three(bank[4 + 2 * t + half][:, :], fh[:, a, v], fl[:, a, v], wh[:, n], wl[:, n],
                                        start=(j == 0 and a == 0), stop=(j == FJ - 1 and a == FC - 1))
                    if a % 2 == 1:
                        ins.then_inc(unit_used, 1)

            turn(2)
            pe.wait_ge(res[0], 4)
            for j in range(FJ + 1):
                if j < FJ:
                    ffn_in("gate", j, 0)
                    ffn_in("up", j, 2)
                if j > 0:
                    ffn_out(j - 1)

            pe.wait_ge(par2_in, 16 * N_PAR2)
            pe.wait_ge(f_silu, 2 * FJ)
            pe.transpose(bank[0][:, 0:96], packT[0:96, :], ident[0:96, 0:96]).then_inc(tap_t, 1)
            pe.wait_ge(tap_e, 1)
            turn(3)
            pe.wait_ge(res[1], 4)
            pe.wait_ge(hT_lo[3], 4)
            for t in range(TC):
                for c in range(DC):
                    ins = mm(bank[4][:, 16 * t:16 * t + 16], hT[:, c, t * P:(t + 1) * P], w_ba[:, c, :],
                             start=(c == 0), stop=(c == DC - 1))
            ins.then_inc(g1_pe, 1)

            def gdn_in(s):
                at = 2 * ((s + 3) % 4)
                if s >= 4:
                    pe.wait_ge(ev1, 2 * (s - 3))
                    pe.wait_ge(ssq_ev, 2 * (s - 3))
                (tall if s < 6 else flat)(GDN0 + s, at)

            def lengths(s):
                at = [6, 0, 2, 4][s]
                pe.wait_ge(sqr_ok, s + 1)
                pe.wait_ge(ev1, 2 * ([0, 1, 2, 3][s] + 1))
                for a in range(2):
                    mm(bank[at + a][:, :], ones,
                       sqb[:, s % 2, 2 * a:2 * a + 2, :].rearrange("p a t -> p (a t)"),
                       start=True, stop=True).then_inc(ssq_pe, 1)

            gdn_in(0)
            pe.wait_ge(g1_dve, 4)
            g = sm[:, 4, :]
            mm(bank[5][:, 0:16], incl[:, :], g, start=True, stop=True)
            mm(bank[5][:, 16:24], ones, g[:, 0:8], start=True, stop=True).then_inc(g1_pe, 1)
            gdn_in(1)
            pe.wait_ge(g1_dve, 8)
            for a, r in ((0, 21), (1, 22)):
                for c in range(TC):
                    ins = pe.transpose(bank[4][0:8, a * S + c * P:a * S + (c + 1) * P], sm[:, r, 8 * c:8 * c + 8],
                                       ident[:, :])
            ins.then_inc(g1_pe, 1)
            gdn_in(2)
            pe.wait_ge(g1_dve, 9)
            lengths(0)
            for q in range(1, 4):
                gdn_in(q + 2)
                lengths(q)
            gdn_in(6)
            gdn_in(7)
            pe.wait_ge(ev1, 16)
            pe.wait_ge(qk_ok, 4)
            pe.wait_ge(silu_ok, 2)
            for gi in range(8):
                hg = gi % 2
                src, c = ((gk, 1), (gk, 0), (gv, 0), (gv, 1))[gi // 2]
                for a in range(4):
                    ins = pe.transpose(bank[gi][:, a * P:(a + 1) * P], src[:, 4 * hg + a, c * P:(c + 1) * P],
                                       ident[:, :])
                ins.then_inc(kv_t, 1)

            def decay(h):
                pe.wait_ge(kv_ev, 5 + h % 2 + 1) if h < 2 else pe.wait_ge(gam_ok, h - 1)
                o = bank[4 + h % 2][:, :]
                mm(o, ident[0:8, h:h + 1].to_broadcast([8, P]), rows2[0:8, :, :].rearrange("p a t -> p (a t)"),
                   start=True, stop=False)
                mm(o.rearrange("p (a c t) -> p a c t", a=2, c=TC), ident[:, :],
                   neg[:, :, :].unsqueeze(2).to_broadcast([P, 2, TC, P]), start=False, stop=True).then_inc(bc_ok, 1)

            def scores(h):
                if h >= 2:
                    pe.wait_ge(att_ok, h - 1)
                for a, q in ((0, gk), (1, gq)):
                    for c in range(TC):
                        ins = mm(bank[h % 2][:, (2 * a + c) * P:(2 * a + c + 1) * P], gk[:, h, c * P:(c + 1) * P],
                                 q[:, h, c * P:(c + 1) * P], start=True, stop=True)
                ins.then_inc(kq_ok, 1)

            pe.wait_ge(kv_ev, 2)
            for h in range(GD_H):
                decay(h)
                scores(h)
            pe.wait_ge(att_ok, 8)
            pe.wait_ge(kv_ev, 8)
            for gi in range(4):
                c = gi // 2
                for a in range(4):
                    h = 4 * (gi % 2) + a
                    ins = mm(bank[2 * gi][:, a * P:(a + 1) * P], nAT[:, c, h, :], ident[:, :], start=True, stop=True)
                ins.then_inc(inv_x, 1)
            for l in range(1, 7):
                for gi in range(4):
                    c = gi // 2
                    pe.wait_ge(inv_t, 4 * (l - 1) + gi + 1)
                    for a in range(4):
                        h = 4 * (gi % 2) + a
                        ins = mm(bank[2 * gi][:, a * P:(a + 1) * P], nAT[:, c, h, :], Tn[:, c, h, :],
                                 start=True, stop=True)
                    ins.then_inc(inv_x, 1)
                for gi in range(4):
                    c = gi // 2
                    pe.wait_ge(inv_xs, 4 * (l - 1) + gi + 1)
                    for a in range(4):
                        h = 4 * (gi % 2) + a
                        o = slice(a * P, (a + 1) * P)
                        if l < 6:
                            mm(bank[2 * gi][:, o], Tt[:, c, h, :], xs[:, gi, a, :], start=True, stop=True)
                        ins = mm(bank[2 * gi + 1][:, o], xs[:, gi, a, :], Tt[:, c, h, :], start=True, stop=True)
                    ins.then_inc(inv_d, 1)
            def heads4(gi, at, signal, *products):
                for a in range(4):
                    h = 4 * gi + a
                    for m, (l, r) in enumerate(products):
                        ins = mm(bank[at][:, a * P:(a + 1) * P], l(h), r(h), start=(m == 0),
                                 stop=(m == len(products) - 1))
                ins.then_inc(signal, 1)

            pe.wait_ge(inv_t, 28)
            for gi in range(2):
                heads4(gi, 2 * gi, s_pe, (lambda h: Tt[:, 0, h, :], lambda h: vb[:, 0, h, :]))
                heads4(gi, 2 * gi + 1, s_pe, (lambda h: kbg[:, h, :], lambda h: Tt[:, 1, h, :]))
            for gi in range(2):
                pe.wait_ge(s_act, 2 * gi + 2)
                heads4(gi, 4 + 2 * gi, s_pe, (lambda h: kdec[:, h, :], lambda h: vn[:, 0, h, :]))
                heads4(gi, 5 + 2 * gi, s_pe, (lambda h: attT[:, 0, h, :], lambda h: vn[:, 0, h, :]))
                pe.wait_ge(s_act, 4 + gi + 1)
                heads4(gi, 1 + 2 * gi, s_pe, (lambda h: gq[:, h, P:S], lambda h: st1[:, h, :]))
            for gi in range(2):
                heads4(gi, 2 * gi, s_pe, (lambda h: Tt[:, 1, h, :], lambda h: vb[:, 1, h, :]),
                       (lambda h: nwT[:, h, :], lambda h: st1[:, h, :]))
                pe.wait_ge(s_act, 6 + gi + 1)
                heads4(gi, 4 + 2 * gi, s_pe, (lambda h: attT[:, 1, h, :], lambda h: vn[:, 1, h, :]))
            turn(4)
            flat(GDN0 + 8, 4, 4)
            flat(GDN0 + 9, 6)

            turn(5)
            pe.wait_ge(res[2], 4)
            pe.wait_ge(hT_lo[5], 4)
            for t in range(TC):
                for c in range(DC):
                    ins = mm(bank[4][:, 8 * t:8 * t + 8], hT[:, c, t * P:(t + 1) * P], w_rt[:, c, :],
                             start=(c == 0), stop=(c == DC - 1))
            ins.then_inc(r_pe, 1)
            pe.wait_ge(r_dve, 2)
            sel = rt[:, 10, :]
            mm(bank[5][:, 0:8], incl[:, :], sel[:, 0:8], start=True, stop=True)
            mm(bank[5][:, 8:16], incl[:, :], sel[:, 8:16], start=True, stop=False)
            mm(bank[5][:, 8:16], ones, sel[:, 0:8], start=False, stop=True)
            mm(bank[5][:, 16:24], ones, sel[:, 0:8], start=True, stop=False)
            mm(bank[5][:, 16:24], ones, sel[:, 8:16], start=False, stop=True).then_inc(r_pe, 1)
            pe.wait_ge(routed, 1)
            nr = pe.value_load(nrounds[0:1, 0:1], min_val=1, max_val=ROUNDS)

            with pe.Fori(0, nr) as b:
                with pe.Fori(0, NE) as e:
                    it = pe.snap(b * NE + e)
                    pe.wait_ge(e_sel, it + 1)
                    for a in range(2):
                        for q in range(4):
                            d = 4 * a + q
                            for c in range(TC):
                                ins = mm(bank[4 + a][:, q * CAP:(q + 1) * CAP], xn[:, c, d * P:(d + 1) * P],
                                         eP[:, c, :], start=(c == 0), stop=(c == TC - 1))
                        ins.then_inc(e_gather, 1)
                    for c in range(TC):
                        ins = pe.transpose(bank[0][0:CAP, c * P:(c + 1) * P], ePG[:, c, :], ident[:, :])
                    ins.then_inc(e_gather, 1)
                    pe.wait_ge(e_gt, it + 1)

                    def turn_hidden(j):
                        pe.wait_ge(e_hh, it * FJ + (j + 1))
                        if j == 0:
                            pe.wait_ge(e_x, it * 4 + 1)
                        for a in range(FC):
                            ins = pe.transpose(bank[2][:, a * CAP:(a + 1) * CAP], ehh[0:CAP, a * P:(a + 1) * P],
                                               ident[0:CAP, 0:CAP])
                        ins.then_inc(e_t, 1)

                    th = hr[:, 0, 0:FC * CAP].rearrange("p (a n) -> p a n", a=FC)
                    tl = hr[:, 1, 0:FC * CAP].rearrange("p (a n) -> p a n", a=FC)
                    gh = hTr[:, 0, 0:DC * CAP].rearrange("p (c n) -> p c n", c=DC)
                    gl = hTr[:, 1, 0:DC * CAP].rearrange("p (c n) -> p c n", c=DC)
                    for m, (kind, j) in enumerate(order):
                        k = MOE0 + m
                        down = kind == "down"
                        if down:
                            if j == FJ - 1:
                                turn_hidden(j)
                            pe.wait_ge(e_tlo, it * FJ + (j + 1))
                        if kind == "gate" and j >= 1:
                            pe.wait_ge(e_silu, it * FJ + j)
                        if kind == "up" and j >= 1:
                            pe.wait_ge(e_hh, it * FJ + j)
                        for c in range(FC if down else DC):
                            u = 2 * k + c // (2 if down else 4)
                            if c % (2 if down else 4) == 0:
                                pe.wait_ge(lo_ok, it * UPER + (u + 1))
                            if m == 0 and c % 4 == 0:
                                pe.wait_ge(e_xlo, it * 2 + (c // 4 + 1))
                            wh, wl = unit_view(whi, u % CUT, down), unit_view(wlo, u % CUT, down)
                            if down:
                                for half in range(2):
                                    n = slice(512 * half, 512 * (half + 1))
                                    ins = three(bank[6 + half][0:CAP, :], th[:, c, :], tl[:, c, :],
                                                wh[:, c % 2, n], wl[:, c % 2, n], start=(j == 0 and c == 0),
                                                stop=(j == FJ - 1 and c == FC - 1))
                            else:
                                ins = three(bank[0 if kind == "gate" else 1][0:CAP, :], gh[:, c, :], gl[:, c, :],
                                            wh[:, c % 4, :], wl[:, c % 4, :], start=(c == 0), stop=(c == DC - 1))
                            if c % (2 if down else 4) == (1 if down else 3):
                                ins.then_inc(unit_used, 1)
                        if kind == "gate" and j >= 1:
                            turn_hidden(j - 1)
                    pe.wait_ge(e_yg, it + 1)
                    pe.wait_ge(e_yg2, it + 1)
                    for m in range(4):
                        c, half = m // 2, m % 2
                        if m >= 2:
                            pe.wait_ge(e_x, it * 4 + m)
                        mm(bank[3 - m % 2][:, :], eGT[0:CAP, c * P:(c + 1) * P],
                           eyg[0:CAP, 512 * half:512 * (half + 1)], start=True, stop=True).then_inc(e_sc, 1)


_INS = ['x', 'l0_norm_mix', 'l0_ml_w_in', 'l0_ml_b_if', 'l0_ml_head_gain', 'l0_ml_w_out', 'l0_norm_ffn',
        'l0_ffn_w_gate', 'l0_ffn_w_up', 'l0_ffn_w_down', 'l1_norm_mix', 'l1_gdn_w_in', 'l1_gdn_conv',
        'l1_gdn_a_log', 'l1_gdn_dt_bias', 'l1_gdn_out_gain', 'l1_gdn_w_out', 'l1_norm_ffn', 'l1_moe_router',
        'l1_moe_w_gate', 'l1_moe_w_up', 'l1_moe_w_down', 'final_norm']


def kernel(**inputs):
    import numpy as _np
    import concourse.bacc as _bacc
    from concourse import mybir as _mybir
    from concourse.bass_utils import run_bass_kernel_spmd as _run

    nc = _bacc.Bacc("TRN2", target_bir_lowering=False, num_devices=1,
                     dynamic_dma_scratch_size=512)
    arrays, args = {}, {}
    for name in _INS:
        a = _np.ascontiguousarray(inputs[name])
        arrays[f"in_{name}"] = a
        args[name] = nc.dram_tensor(f"in_{name}", a.shape, _mybir.dt.from_np(a.dtype), kind="ExternalInput").ap()
    out = nc.dram_tensor("out_dram", (1, S, D), _mybir.dt.float32, kind="ExternalOutput").ap()
    bass_hybrid_trunk(nc, out, args)
    r = _run(nc, [arrays], core_ids=[0])
    return r.results[0]["out_dram"]
```

```python
from contextlib import ExitStack

import concourse.bass as bass
from concourse import mybir

P = 128
S = 256
TC = S // P
D = 1024
DC = D // P
EPS = 1e-6

ML_H, ML_DQK, ML_DV = 4, 128, 256
GD_H, GD_DK, GD_DV, GD_K = 8, 128, 128, 4
FF = 3584
NE = 8
CAP = 96
ROUNDS = -(-S // CAP)

SLAB = 512
UNIT = DC * SLAB // 2
RAW = 7
CUT = 3
FJ = FF // SLAB
FC = SLAB // P
NEG = -1e30

F32 = mybir.dt.float32
F32R = mybir.dt.float32r
I32 = mybir.dt.int32
U8 = mybir.dt.uint8
ALU = mybir.AluOpType
ACT = mybir.ActivationFunctionType
AX = mybir.AxisListType


def bass_hybrid_trunk(nc, out, w):
    ctx = ExitStack()
    with ctx:
        def sb(name, shape, dt=F32):
            return ctx.enter_context(nc.sbuf_tensor(name, shape, dt))

        def sem(name):
            return ctx.enter_context(nc.semaphore(name))

        raw = sb("raw", [P, RAW, UNIT])
        whi = sb("whi", [P, CUT, UNIT], F32R)
        wlo = sb("wlo", [P, CUT, UNIT], F32R)
        hTr = sb("hTr", [P, 2, DC * S], F32R)
        xh = hTr[:, 0, :].rearrange("p (c t) -> p c t", c=DC)
        xl = hTr[:, 1, :].rearrange("p (c t) -> p c t", c=DC)
        hr = sb("hr", [P, 2, FC * S], F32R)
        x = sb("x", [P, TC, D])
        xn = sb("xn", [P, TC, D])
        Ttb = sb("Ttb", [P, 2 * D])
        area = sb("area", [P, 15424])

        ident = sb("ident", [P, P])
        one = sb("one", [P, 1])
        ones = one[:, :].to_broadcast([P, P])
        incl = sb("incl", [P, P])
        neg = sb("neg", [P, 2, P])
        low = sb("low", [P, 7, P], U8)
        upp = sb("upp", [P, 7, P], U8)
        iot = sb("iot", [P, CAP])
        mhalf = sb("mhalf", [P, 16])
        gains = sb("gains", [P, 5 * DC + 1])
        taps = sb("taps", [P, GD_K, 24])
        w_if = Ttb[:, 0:64].rearrange("p (c n) -> p c n", c=DC)
        w_ba = Ttb[:, 64:192].rearrange("p (c n) -> p c n", c=DC)
        w_rt = sb("w_rt", [P, DC, NE])
        narrow_r = sb("narrow_r", [P, 2 * DC * 2 * GD_H], F32R)

        def narrow_parts(n):
            return narrow_r[:, 0:2 * DC * n].rearrange("p (a c n) -> p a c n", a=2, c=DC)

        w_if_r, w_ba_r, w_rt_r = narrow_parts(2 * ML_H), narrow_parts(2 * GD_H), narrow_parts(NE)
        bif = sb("bif", [P, 2 * ML_H])
        dtb = sb("dtb", [P, GD_H])
        alog = sb("alog", [P, GD_H])
        ss = sb("ss", [P, 7, 16])
        va = sb("va", [P, 7, 16])
        rs = sb("rs", [P, 7, 16])
        sm = sb("sm", [P, 24, 16])
        den = sb("den", [P, 2, 8])
        nrounds = sb("nrounds", [1, 1], I32)

        def view(at, n, pat=None, **kw):
            v = area[:, at:at + n]
            return v.rearrange(pat, **kw) if pat else v

        packG = view(8872, 128)
        packT = view(9000, 128)
        xorI = view(9200, 3 * 128).bitcast(I32).rearrange("p (a n) -> p a n", a=3)
        xorF = view(9584, 4 * 128, "p (a n) -> p a n", a=4)
        mq = view(0, 1024, "p (h t) -> p h t", h=ML_H)
        mk = view(1024, 1024, "p (h t) -> p h t", h=ML_H)
        mv = view(2048, TC * ML_H * 257, "p (c h n) -> p c h n", c=TC, h=ML_H)
        mog = view(4104, 2048, "p (c n) -> p c n", c=TC)
        mw = view(6152, 2 * 384, "p (b n) -> p b n", b=2)
        msc = view(6920, 2 * 384, "p (b n) -> p b n", b=2)
        mrow = view(7688, 3 * S, "p (a n) -> p a n", a=3)
        msq = view(8456, 256)
        fsg = view(0, 1024, "p (a t) -> p a t", a=FC)
        fhh = view(1024, 1024, "p (a t) -> p a t", a=FC)
        gq = view(0, 2048, "p (h t) -> p h t", h=GD_H)
        gk = view(2048, 2048, "p (h t) -> p h t", h=GD_H)
        gv = view(4096, 2048, "p (h t) -> p h t", h=GD_H)
        gz = view(6144, 2048, "p (c n) -> p c n", c=TC)
        RW = S + GD_K - 1
        graw = view(8192, 8 * RW, "p (b a n) -> p b a n", b=2, a=4)
        kbg = view(8192, 1024, "p (h d) -> p h d", h=GD_H)
        kdec = view(9216, 1024, "p (h d) -> p h d", h=GD_H)
        nAT = view(10304, 2048, "p (c h t) -> p c h t", c=TC, h=GD_H)
        attT = view(12352, 2048, "p (c h t) -> p c h t", c=TC, h=GD_H)
        rsq = view(10304, 4096, "p (h t) -> p h t", h=2 * GD_H)
        gam = view(14400, 1024, "p (b a c t) -> p b a c t", b=2, a=2, c=TC)
        vb = view(4096, 2048, "p (c h d) -> p c h d", c=TC, h=GD_H)
        xs = view(2048, 2048, "p (g h t) -> p g h t", g=4, h=4)
        nwT = view(2048, 1024, "p (h t) -> p h t", h=GD_H)
        st1 = view(3072, 1024, "p (h t) -> p h t", h=GD_H)
        vn = view(10304, 2048, "p (c h d) -> p c h d", c=TC, h=GD_H)
        osq = view(12352, 2048, "p (g d) -> p g d", g=16)
        rows2 = sb("rows2", [GD_H, 2, S])
        sqb = xn[:, :, :].rearrange("p b (h t) -> p b h t", h=4)
        Tn = xn[:, :, :].rearrange("p c (h t) -> p c h t", h=GD_H)
        Tt = Ttb[:, :].rearrange("p (c h t) -> p c h t", c=TC, h=GD_H)
        eP = view(0, TC * CAP, "p (c n) -> p c n", c=TC)
        ePG = view(256, TC * CAP, "p (c n) -> p c n", c=TC)
        eGT = view(512, S)
        exg = view(768, DC * CAP, "p (c n) -> p c n", c=DC)
        esg = view(1792, 512)
        ehh = view(2816, 512)
        eyg = view(4864, D)
        fgain = view(6144, D)
        fout = view(7168, 2 * D, "p (c n) -> p c n", c=TC)
        tok9 = view(9216, 2 * TC * 9, "p (a c n) -> p a c n", a=2, c=TC)
        posm, gate9 = tok9[:, 0], tok9[:, 1]
        rt = view(9280, 16 * 16, "p (a n) -> p a n", a=16)

        bank = [ctx.enter_context(nc.psum_tensor(f"bank{i}", [P, 512], F32)) for i in range(8)]

        def b2(i, n=2):
            return bank[i][:, :].rearrange("p (a t) -> p a t", a=n)

        x_in = [sem(f"x_in{c}") for c in range(TC)]
        par_in, par2_in, par3_in = sem("par_in"), sem("par2_in"), sem("par3_in")
        landed = [sem(f"landed{i}") for i in range(RAW)]
        hi_ok = sem("hi_ok")
        lo_ok = sem("lo_ok")
        unit_used = sem("unit_used")
        pool_step = sem("pool_step")
        consts = sem("consts")
        dve_step = sem("dve_step")
        act_step = sem("act_step")
        masks = sem("masks")
        pack_t = sem("pack_t")
        pack_e = sem("pack_e")
        tap_t, tap_e = sem("tap_t"), sem("tap_e")
        first_chunk = sem("first_chunk")
        sq_sum = [sem(f"sq_sum{i}") for i in range(7)]
        var_ok = [sem(f"var_ok{i}") for i in range(7)]
        rs_ok = [sem(f"rs_ok{i}") for i in range(7)]
        xn_ok = [sem(f"xn_ok{i}") for i in range(6)]
        tr_ok = [sem(f"tr_ok{i}") for i in range(6)]
        hT_hi = [sem(f"hT_hi{i}") for i in range(6)]
        hT_lo = [sem(f"hT_lo{i}") for i in range(6)]
        small_hi, small_lo = sem("small_hi"), sem("small_lo")
        ev0, ev0v = sem("ev0"), sem("ev0v")
        g0_pe, g0_dve, g0_act = sem("g0_pe"), sem("g0_dve"), sem("g0_act")
        h_bc, h_w, h_qk, h_sc, h_num, h_hs = [sem(n) for n in ("h_bc", "h_w", "h_qk", "h_sc", "h_num", "h_hs")]
        res = [sem(f"res{i}") for i in range(3)]
        f_silu, f_hh, f_hi, f_lo = sem("f_silu"), sem("f_hh"), sem("f_hi"), sem("f_lo")
        ev1 = sem("ev1")
        conv_ok, silu_ok, sqr_ok, ssq_pe, ssq_ev, ln_ok, qk_ok = [sem(n) for n in (
            "conv_ok", "silu_ok", "sqr_ok", "ssq_pe", "ssq_ev", "ln_ok", "qk_ok")]
        log_ok = sem("log_ok")
        g1_pe, g1_dve, g1_act = sem("g1_pe"), sem("g1_dve"), sem("g1_act")
        kv_t, kv_ev = sem("kv_t"), sem("kv_ev")
        bc_ok, gam_ok, kq_ok, att_ok = sem("bc_ok"), sem("gam_ok"), sem("kq_ok"), sem("att_ok")
        inv_x, inv_xs, inv_d, inv_t = sem("inv_x"), sem("inv_xs"), sem("inv_d"), sem("inv_t")
        s_pe, s_act, s_dve = sem("s_pe"), sem("s_act"), sem("s_dve")
        r_pe, r_dve, r_act, routed = sem("r_pe"), sem("r_dve"), sem("r_act"), sem("routed")
        e_sel, e_gather, e_xg, e_xhi, e_xlo, e_turn, e_gt, e_silu, e_hh, e_t, e_thi, e_tlo = [sem(n) for n in (
            "e_sel", "e_gather", "e_xg", "e_xhi", "e_xlo", "e_turn", "e_gt", "e_silu", "e_hh", "e_t", "e_thi",
            "e_tlo")]
        e_y0, e_yg, e_yg2, e_sc, e_x = [sem(n) for n in ("e_y0", "e_yg", "e_yg2", "e_sc", "e_x")]
        e_own = sem("e_own")
        fin_ok = sem("fin_ok")
        stored = sem("stored")

        def cols(m, a):
            return m[:, a:a + SLAB].rearrange("(c p) n -> p c n", p=P)

        def rows(m, a):
            return m[a:a + SLAB, :].rearrange("(c p) n -> p c n", p=P)

        slabs = [cols(w["l0_ml_w_in"], SLAB * i) for i in range(6)]
        slabs += [cols(w["l0_ml_w_out"], SLAB * i) for i in range(2)]
        FFN0 = len(slabs)
        for j in range(FJ):
            slabs += [cols(w["l0_ffn_w_gate"], SLAB * j), cols(w["l0_ffn_w_up"], SLAB * j),
                      rows(w["l0_ffn_w_down"], SLAB * j)]
        GDN0 = len(slabs)
        slabs += [cols(w["l1_gdn_w_in"], SLAB * i) for i in range(8)]
        slabs += [cols(w["l1_gdn_w_out"], SLAB * i) for i in range(2)]
        MOE0 = len(slabs)
        PER = 3 * FJ
        order = []
        for j in range(FJ + 1):
            if j < FJ:
                order += [("gate", j), ("up", j)]
            if j > 0:
                order += [("down", j - 1)]
        place = {key: m for m, key in enumerate(order)}

        ffn_slab = {key: FFN0 + m for key, m in place.items()}
        by_kind = {"gate": "l0_ffn_w_gate", "up": "l0_ffn_w_up", "down": "l0_ffn_w_down"}
        for (kind, j), k in ffn_slab.items():
            slabs[k] = (rows if kind == "down" else cols)(w[by_kind[kind]], SLAB * j)

        def unit_view(buf, slot, down):
            return buf[:, slot, :].rearrange("p (c n) -> p c n", c=2 if down else 4)

        MU0 = 2 * MOE0
        UPER = 2 * PER
        AHEAD = CUT

        def products(eng, k, item=0):
            eng.wait_ge(unit_used, item * UPER + (2 * k + 2))

        def cut_hi(act, u, item=0):
            act.wait_ge(landed[u % RAW], item * (16 * UPER // RAW) + 16 * (u // RAW + 1))
            if u >= CUT:
                act.wait_ge(unit_used, item * UPER + (u - CUT + 1))
            act.activation(whi[:, u % CUT, :], raw[:, u % RAW, :], ACT.Copy).then_inc(hi_ok, 1)

        def cut_lo(dve, u, item=0):
            dve.wait_ge(hi_ok, item * UPER + (u + 1))
            dve.tensor_tensor(wlo[:, u % CUT, :], raw[:, u % RAW, :], whi[:, u % CUT, :].bitcast(F32), ALU.subtract) \
               .then_inc(lo_ok, 1)

        class Cuts:

            def __init__(self, eng, cut):
                self.eng, self.cut, self.done = eng, cut, 0

            def to(self, n, item=0):
                while self.done <= n:
                    self.cut(self.eng, self.done, item)
                    self.done += 1

            def through(self, k, item=0):
                self.to(2 * k + CUT, item)

        def hidden(part, j):
            return hr[:, part, 512 * (j % 2):512 * (j % 2) + FC * CAP]

        def gate_bank(j):
            return 4 if j == 0 else 0

        BY_HALF = [(c, half) for half in range(2) for c in range(TC)]
        BY_CHUNK = [(c, half) for c in range(TC) for half in range(2)]

        scatter_banks = (3, 2, 4, 5)

        N_PAR, N_PAR2 = 8, 8

        block = ctx.enter_context(nc.Block())

        @block.sync
        def _(sp):
            xv = w["x"].rearrange("b (c p) d -> p (b c) d", p=P)
            for c in range(TC):
                sp.dma_start(x[:, c, :], xv[:, c, :]).then_inc(x_in[c], 16)
            g = [w["l0_norm_mix"], w["l0_ml_head_gain"], w["l0_norm_ffn"], w["l1_norm_mix"], w["l1_norm_ffn"]]
            for i, a in enumerate(g):
                sp.dma_start(packG[DC * i:DC * (i + 1), :], a.rearrange("(c p) -> c p", p=P)).then_inc(par_in, 16)
            sp.dma_start(packG[5 * DC:5 * DC + 1, :], w["l1_gdn_out_gain"].rearrange("(c p) -> c p", p=P)) \
              .then_inc(par_in, 16)

            def small(dst, name, at, m, s):
                sp.dma_start(dst[:, :, :], w[name][:, at:at + m].rearrange("(c p) n -> p c n", p=P)).then_inc(s, 16)

            small(w_if, "l0_ml_w_in", 3072, 2 * ML_H, par_in)
            sp.dma_start(bif[:, :], w["l0_ml_b_if"].partition_broadcast(P)).then_inc(par_in, 16)
            for k, src in enumerate(slabs):
                down = src.shape[1] == FC
                for half in range(2):
                    u, c = 2 * k + half, src.shape[1] // 2
                    if u >= RAW:
                        sp.wait_ge(lo_ok, u - RAW + 1)
                    sp.dma_start(unit_view(raw, u % RAW, down), src[:, c * half:c * (half + 1), :]) \
                      .then_inc(landed[u % RAW], 16)
                if k == 3:
                    for q in range(GD_K):
                        sp.dma_start(packT[24 * q:24 * (q + 1), :],
                                     w["l1_gdn_conv"][q, :].rearrange("(c p) -> c p", p=P)).then_inc(par2_in, 16)
                    small(w_ba, "l1_gdn_w_in", 4096, 2 * GD_H, par2_in)
                    small(w_rt, "l1_moe_router", 0, NE, par2_in)
                    for dst, name in ((dtb, "l1_gdn_dt_bias"), (alog, "l1_gdn_a_log")):
                        sp.dma_start(dst[:, :], w[name].partition_broadcast(P)).then_inc(par2_in, 16)
            moe = {"gate": "l1_moe_w_gate", "up": "l1_moe_w_up", "down": "l1_moe_w_down"}

            def load(it, e, r):
                kind, j = order[r // 2 % PER]
                u, half, wm = MU0 + r, r % 2, w[moe[kind]]
                sp.wait_ge(lo_ok, it * UPER + (u - RAW + 1))
                if kind == "down":
                    part = slice(SLAB * j + 256 * half, SLAB * j + 256 * (half + 1))
                    src = wm[bass.ds(e, 1), part, :]
                else:
                    src = wm[bass.ds(e, 1), 512 * half:512 * (half + 1), SLAB * j:SLAB * (j + 1)]
                sp.dma_start(unit_view(raw, u % RAW, kind == "down"),
                             src.rearrange("a (c p) n -> p (a c) n", p=P)).then_inc(landed[u % RAW], 16)

            def load_round(b):
                with sp.Fori(0, NE) as e:
                    it = sp.snap(b * NE + e)
                    for r in range(UPER):
                        load(it, e, r)

            load_round(0)
            sp.wait_ge(routed, 1)
            nr = sp.value_load(nrounds[0:1, 0:1], min_val=1, max_val=ROUNDS)
            with sp.If(nr > 1):
                with sp.Fori(1, nr) as b:
                    load_round(b)
            for r in range(AHEAD):
                load(nr * NE, 0, r)
            ov = out.rearrange("b (c p) d -> p (b c) d", p=P)
            for c in range(TC):
                sp.wait_ge(fin_ok, c + 1)
                sp.dma_start(ov[:, c, :], fout[:, c, :]).then_inc(stored, 16)
            sp.wait_ge(stored, 16 * TC)

        @block.gpsimd
        def _(pool):
            n = [0]

            def own(ins):
                n[0] += 1
                ins.then_inc(pool_step, 1)

            def settled():
                pool.wait_ge(pool_step, n[0])

            own(pool.memset(ident[:, :], 0.0))
            own(pool.memset(one[:, :], 1.0))
            own(pool.memset(incl[:, :], 1.0))
            own(pool.memset(neg[:, :, :], 0.0))
            own(pool.memset(mhalf[:, :], -0.5))
            own(pool.iota(xorI[:, 0, :], pattern=[[1, P]], base=0, channel_multiplier=0))
            own(pool.iota(xorI[:, 1, :], pattern=[[0, P]], base=0, channel_multiplier=1))
            own(pool.iota(iot[:, :], pattern=[[1, CAP]], base=0, channel_multiplier=0,
                          allow_small_or_imprecise_dtypes=True))
            settled()
            own(pool.affine_select(out=ident[:, :], in_=ident[:, :], compare_op=ALU.not_equal, fill=1.0, base=0,
                                   pattern=[[-1, P]], channel_multiplier=1))
            own(pool.affine_select(out=incl[:, :], in_=incl[:, :], compare_op=ALU.is_ge, fill=0.0, base=0,
                                   pattern=[[1, P]], channel_multiplier=-1))
            for a, op in ((0, ALU.is_gt), (1, ALU.is_ge)):
                own(pool.affine_select(out=neg[:, a, :], in_=neg[:, a, :], compare_op=op, fill=NEG, base=0,
                                       pattern=[[1, P]], channel_multiplier=-1))
            settled()
            pool.memset(mv[:, :, :, 256:257], 1.0).then_inc(consts, 1)

            def roots(i, steps, m):
                for t in range(steps):
                    v = slice(m * t, m * (t + 1))
                    pool.wait_ge(var_ok[i], t + 1)
                    pool.tensor_tensor(rs[:, i, v], va[:, i, v], mhalf[:, 0:m], ALU.pow).then_inc(rs_ok[i], 1)

            roots(0, TC, 1)
            roots(1, ML_H, TC)
            roots(2, TC, 1)
            roots(3, TC, 1)
            pool.wait_ge(res[1], 4)
            pool.memset(graw[:, :, :, 0:GD_K - 1], 0.0).then_inc(consts, 1)
            roots(4, 4, 4)
            roots(5, TC, 1)
            roots(6, TC, 1)

        @block.scalar
        def _(act):
            n = [0]

            def own(ins):
                n[0] += 1
                ins.then_inc(act_step, 1)
                act.wait_ge(act_step, n[0])

            def square(i, c, half):
                piece = slice(512 * half, 512 * (half + 1))
                act.activation(xn[:, c, piece], x[:, c, piece], ACT.Square, scale=D ** -0.5,
                               accum_out=ss[:, i, 2 * c + half:2 * c + half + 1]).then_inc(sq_sum[i], 1)

            def sum_squares(i, r, pieces):
                for m, (c, half) in enumerate(pieces):
                    act.wait_ge(res[r], m + 1)
                    square(i, c, half)

            def turned(i, gcol):
                for k in range(4):
                    act.wait_ge(tr_ok[i], k + 1)
                    for a in range(2):
                        c = 2 * k + a
                        act.activation(xh[:, c, :], b2(k)[:, a, :], ACT.Copy, scale=gcol(c)) \
                           .then_inc(hT_hi[i], 1)

            cuts = Cuts(act, cut_hi)

            def small_high(src, dst):
                act.activation(dst[:, 0], src[:, :, :], ACT.Copy).then_inc(small_hi, 1)

            act.wait_ge(par_in, 16 * N_PAR)
            small_high(w_if, w_if_r)
            for c, half in BY_CHUNK:
                act.wait_ge(x_in[c], 16)
                square(0, c, half)
            act.wait_ge(pack_e, 1)
            turned(0, lambda c: gains[:, c:c + 1])
            cuts.to(CUT - 1)

            act.wait_ge(g0_dve, 2)
            act.activation(sm[:, 2, 0:8], sm[:, 1, 0:8], ACT.Exp, scale=-1.0).then_inc(g0_act, 1)
            act.wait_ge(g0_act, 1)
            act.activation(sm[:, 3, 0:8], sm[:, 2, 0:8], ACT.Ln, bias=1.0).then_inc(g0_act, 1)

            for s, dst, scale in ((0, mq, 1.0), (1, mk, ML_DQK ** -0.5)):
                cuts.through(s)
                products(act, s)
                for a in range(2):
                    act.activation(dst[:, 2 * a:2 * a + 2, :], b2([6, 0][s] + a), ACT.Copy, scale=scale) \
                       .then_inc(ev0, 1)
            cuts.through(2)
            act.wait_ge(g0_dve, 8)
            act.activation(sm[:, 8, 0:8], sm[:, 7, 0:8], ACT.Exp, scale=-1.0).then_inc(g0_act, 1)
            for s, at in ((4, 6), (5, 0)):
                cuts.through(s)
                products(act, s)
                for c in range(TC):
                    act.activation(mog[:, c, SLAB * (s - 4):SLAB * (s - 3)], bank[at + c][:, :], ACT.Sigmoid) \
                       .then_inc(ev0, 1)
            cuts.to(2 * 5 + 1 + CUT)
            def weights(h):
                act.wait_ge(h_bc, h + 1)
                if h >= 2:
                    act.wait_ge(h_sc, h - 1)
                D0 = bank[2 + 4 * (h % 2)]
                act.activation(mw[:, h % 2, 0:256], D0[:, 0:256], ACT.Exp, bias=sm[:, 5, h:h + 1])
                act.activation(mw[:, h % 2, 256:384], D0[:, 256:384], ACT.Exp,
                               bias=sm[:, 5, 4 + h:5 + h]).then_inc(h_w, 1)

            def head_squares(h):
                for c in range(TC):
                    act.wait_ge(h_hs, TC * h + c + 1)
                    if h or c:
                        act.wait_ge(sq_sum[1], TC * h + c)
                    act.activation(msq[:, :], xn[:, c, ML_DV * h:ML_DV * (h + 1)], ACT.Square,
                                   accum_out=ss[:, 1, 2 * h + c:2 * h + c + 1]).then_inc(sq_sum[1], 1)

            for h in range(3):
                weights(h)
            head_squares(0)
            weights(3)
            for h in range(1, ML_H):
                head_squares(h)
            turned(1, lambda c: gains[:, DC + c:DC + c + 1])

            cuts.through(FFN0 - 1)
            sum_squares(2, 0, BY_HALF)
            turned(2, lambda c: gains[:, 2 * DC + c:2 * DC + c + 1])
            for j in range(FJ):
                cuts.through(ffn_slab[("gate", j)])
                products(act, ffn_slab[("gate", j)])
                if j >= 1:
                    act.wait_ge(f_hh, 2 * j)
                for a in range(2):
                    act.activation(fsg[:, 2 * a:2 * a + 2, :], b2(gate_bank(j) + a), ACT.Silu).then_inc(f_silu, 1)
                if j >= 1:
                    cuts.through(ffn_slab[("up", j)])
                    cuts.through(ffn_slab[("down", j - 1)])
                    products(act, ffn_slab[("down", j - 1)])
                else:
                    cuts.through(ffn_slab[("up", j)])
                for a in range(2):
                    act.wait_ge(f_hh, 2 * j + a + 1)
                    act.activation(hr[:, 0, 512 * a:512 * (a + 1)],
                                   fhh[:, 2 * a:2 * a + 2, :].rearrange("p a t -> p (a t)"), ACT.Copy) \
                       .then_inc(f_hi, 1)
            act.wait_ge(par2_in, 16 * N_PAR2)
            small_high(w_ba, w_ba_r)
            cuts.through(GDN0 - 1)

            sum_squares(3, 1, BY_CHUNK)
            turned(3, lambda c: gains[:, 3 * DC + c:3 * DC + c + 1])
            cuts.to(2 * GDN0 - 1 + CUT)
            act.activation(sm[:, 10, 0:8], alog[:, :], ACT.Exp).then_inc(g1_act, 1)
            act.wait_ge(g1_dve, 3)
            act.activation(sm[:, 14:16, :], sm[:, 12:14, :], ACT.Exp, scale=-1.0).then_inc(g1_act, 1)
            act.wait_ge(g1_act, 2)
            act.activation(sm[:, 16:18, :], sm[:, 14:16, :], ACT.Ln, bias=1.0).then_inc(g1_act, 1)
            cuts.through(GDN0)
            act.wait_ge(g1_dve, 8)
            act.activation(sm[:, 18, :], sm[:, 19, :], ACT.Exp)
            act.activation(sm[:, 20, 0:8], sm[:, 21, 8:16], ACT.Exp)
            act.activation(sm[:, 20, 8:16], sm[:, 22, 8:16], ACT.Exp)
            act.activation(sm[:, 23, 8:16], sm[:, 23, 0:8], ACT.Exp).then_inc(g1_act, 1)
            small_high(w_rt, w_rt_r)
            act.wait_ge(consts, 2)

            def conv_in(s):
                if s >= 2:
                    act.wait_ge(conv_ok, s - 1)
                cuts.through(GDN0 + s)
                products(act, GDN0 + s)
                for a in range(2):
                    act.activation(graw[:, s % 2, 2 * a:2 * a + 2, GD_K - 1:RW], b2(2 * ((s + 3) % 4) + a),
                                   ACT.Copy).then_inc(ev1, 1)

            def conv_act(s):
                dst = (gq, gk, gv)[s // 2][:, 4 * (s % 2):4 * (s % 2) + 4, :]
                act.wait_ge(conv_ok, s + 1)
                ins = act.activation(dst, dst, ACT.Silu)
                if s < 4:
                    own(ins)
                    if s >= 2:
                        act.wait_ge(ssq_pe, 2 * (s - 1))
                    act.activation(sqb[:, s % 2, :, :], dst, ACT.Square).then_inc(sqr_ok, 1)
                else:
                    ins.then_inc(silu_ok, 1)

            conv_in(0)
            for s in range(1, 6):
                conv_in(s)
                conv_act(s - 1)
            conv_act(5)
            cuts.through(GDN0 + 6)
            for s in range(4):
                act.wait_ge(ssq_ev, 2 * s + 2)
                r = rsq[:, 4 * s:4 * s + 4, :]
                act.activation(r, r, ACT.Ln).then_inc(log_ok, 1)
            for s in range(4):
                r = rsq[:, 4 * s:4 * s + 4, :]
                act.wait_ge(log_ok, s + 1)
                act.activation(r, r, ACT.Exp, scale=-0.5).then_inc(ln_ok, 1)
            for s in (6, 7):
                cuts.through(GDN0 + s)
                products(act, GDN0 + s)
                for c in range(TC):
                    act.activation(gz[:, c, SLAB * (s - 6):SLAB * (s - 5)], bank[2 * ((s + 3) % 4) + c][:, :],
                                   ACT.Silu).then_inc(ev1, 1)
            cuts.to(2 * (GDN0 + 8) - 1 + CUT)
            for h in range(GD_H):
                act.wait_ge(bc_ok, h + 1)
                if h >= 2:
                    act.wait_ge(att_ok, h - 1)
                Db = bank[4 + h % 2][:, :].rearrange("p (a c t) -> p a c t", a=2, c=TC)
                for c in range(TC):
                    ins = act.activation(gam[:, h % 2, :, c, :], Db[:, :, c, :], ACT.Exp,
                                         bias=sm[:, 11, 8 * c + h:8 * c + h + 1])
                ins.then_inc(gam_ok, 1)
            for l in range(1, 7):
                for gi in range(4):
                    act.wait_ge(inv_x, 4 * l + gi + 1)
                    act.activation(xs[:, gi, :, :], b2(2 * gi, 4), ACT.Copy).then_inc(inv_xs, 1)
            for gi in range(2):
                hs = slice(4 * gi, 4 * gi + 4)
                act.wait_ge(s_pe, 2 * gi + 1)
                act.activation(vn[:, 0, hs, :], b2(2 * gi, 4), ACT.Copy).then_inc(s_act, 1)
                act.wait_ge(s_pe, 2 * gi + 2)
                act.activation(nwT[:, hs, :], b2(2 * gi + 1, 4), ACT.Copy, scale=-1.0).then_inc(s_act, 1)
            for gi in range(2):
                hs = slice(4 * gi, 4 * gi + 4)
                act.wait_ge(s_pe, 4 + 3 * gi + 1)
                act.activation(st1[:, hs, :], b2(4 + 2 * gi, 4), ACT.Copy).then_inc(s_act, 1)
            for gi in range(2):
                hs = slice(4 * gi, 4 * gi + 4)
                act.wait_ge(s_pe, 10 + 2 * gi + 1)
                act.activation(vn[:, 1, hs, :], b2(2 * gi, 4), ACT.Copy).then_inc(s_act, 1)
            turned(4, lambda c: gains[:, 5 * DC:5 * DC + 1])
            cuts.through(MOE0 - 1)

            sum_squares(5, 2, BY_HALF)
            turned(5, lambda c: gains[:, 4 * DC + c:4 * DC + c + 1])
            cuts.to(MU0 + AHEAD - 1)
            act.dma_start(fgain[:, :], w["final_norm"].partition_broadcast(P)).then_inc(par3_in, 16)
            act.wait_ge(r_dve, 1)
            act.activation(rt[:, 6, 0:TC], rt[:, 5, 0:TC], ACT.Exp).then_inc(r_act, 1)
            act.wait_ge(routed, 1)
            nr = act.value_load(nrounds[0:1, 0:1], min_val=1, max_val=ROUNDS)
            def gathered(it):
                for a in range(2):
                    act.wait_ge(e_xg, it * 2 + (a + 1))
                    act.activation(hTr[:, 0, 4 * CAP * a:4 * CAP * (a + 1)],
                                   exg[:, 4 * a:4 * a + 4, :].rearrange("p a n -> p (a n)"), ACT.Copy) \
                       .then_inc(e_xhi, 1)

            gathered(0)
            with act.Fori(0, nr) as b:
                with act.Fori(0, NE) as e:
                    it = act.snap(b * NE + e)
                    cuts.done = MU0 + AHEAD

                    def high(j):
                        act.wait_ge(e_t, it * FJ + (j + 1))
                        act.activation(hidden(0, j), bank[2][:, 0:FC * CAP], ACT.Copy).then_inc(e_thi, 1)

                    for j in range(FJ):
                        k = MOE0 + place[("gate", j)]
                        cuts.through(k, it)
                        products(act, k, it)
                        if j >= 1:
                            act.wait_ge(e_hh, it * FJ + j)
                        act.activation(esg[0:CAP, :], bank[0][0:CAP, :], ACT.Silu).then_inc(e_silu, 1)
                        if j >= 1:
                            high(j - 1)
                        if j == 1:
                            act.wait_ge(e_turn, it + 1)
                            act.activation(eGT[0:CAP, :], bank[3][0:CAP, 0:S], ACT.Copy).then_inc(e_gt, 1)
                    cuts.through(MOE0 + place[("up", FJ - 1)], it)
                    gathered(it + 1)
                    cuts.through(MOE0 + PER - 2, it)
                    high(FJ - 1)
                    cuts.to(MU0 + UPER, it)
                    act.wait_ge(e_y0, it + 1)
                    act.activation(eyg[0:CAP, 0:512], bank[6][0:CAP, :], ACT.Copy).then_inc(e_yg, 1)
                    cuts.to(MU0 + UPER + AHEAD - 1, it)
            for m, (c, half) in enumerate(BY_HALF):
                act.wait_ge(e_x, nr * (4 * NE) + (m + 1))
                square(6, c, half)

        @block.vector
        def _(dve):
            n = [0]

            def own(ins):
                n[0] += 1
                ins.then_inc(dve_step, 1)

            def settled():
                dve.wait_ge(dve_step, n[0])

            def step(ins):
                own(ins)
                settled()

            cuts = Cuts(dve, cut_lo)

            def level_masks(l):
                if l == 0:
                    step(dve.tensor_tensor(xorI[:, 2, :], xorI[:, 0, :], xorI[:, 1, :], ALU.bitwise_xor))
                    step(dve.tensor_copy(xorF[:, 0, :], xorI[:, 2, :]))
                    step(dve.tensor_tensor(xorF[:, 2, :], xorF[:, 0, :], incl[:, :], ALU.mult))
                    step(dve.tensor_tensor(xorF[:, 1, :], xorF[:, 0, :], xorF[:, 2, :], ALU.subtract))
                for dst, src in ((low, xorF[:, 1, :]), (upp, xorF[:, 2, :])):
                    step(dve.tensor_scalar(xorF[:, 0, :], src, float(2 ** l), None, ALU.is_ge))
                    step(dve.scalar_tensor_tensor(out=dst[:, l, :], in0=src, scalar=float(2 ** (l + 1)),
                                                  in1=xorF[:, 0, :], op0=ALU.is_lt, op1=ALU.mult))

            dve.wait_ge(consts, 1)
            dve.wait_ge(pack_t, 1)
            dve.tensor_copy(gains[:, :], bank[4][:, 0:5 * DC + 1]).then_inc(pack_e, 1)

            def norm_root(i, c, seen):
                dve.wait_ge(sq_sum[i], seen)
                dve.tensor_scalar(va[:, i, c:c + 1], ss[:, i, 2 * c:2 * c + 1], ss[:, i, 2 * c + 1:2 * c + 2], EPS,
                                  ALU.add, ALU.add).then_inc(var_ok[i], 1)
                dve.wait_ge(rs_ok[i], c + 1)

            def norm(i, c, seen):
                norm_root(i, c, seen)
                dve.tensor_scalar(xn[:, c, :], x[:, c, :], rs[:, i, c:c + 1], None, ALU.mult).then_inc(xn_ok[i], 1)

            def turned(i, gcol):
                for c in range(DC):
                    dve.wait_ge(hT_hi[i], 2 * (c // 2) + 2)
                    dve.scalar_tensor_tensor(out=xl[:, c, :], in0=b2(c // 2)[:, c % 2, :], scalar=gcol(c),
                                             in1=xh[:, c, :].bitcast(F32), op0=ALU.mult, op1=ALU.subtract) \
                       .then_inc(hT_lo[i], 1)

            def gcol(i):
                return lambda c: gains[:, DC * i + c:DC * i + c + 1]

            def small_low(m, src, dst):
                dve.wait_ge(small_hi, m)
                dve.tensor_tensor(dst[:, 1], src[:, :, :], dst[:, 0].bitcast(F32), ALU.subtract).then_inc(small_lo, 1)

            small_low(1, w_if, w_if_r)
            dve.wait_ge(pack_e, 1)
            for c in range(TC):
                dve.wait_ge(x_in[c], 16)
                norm(0, c, 2 * c + 2)
            turned(0, gcol(0))
            cuts.to(CUT - 1)
            G = sm[:, 0, :].rearrange("p (c n) -> p c n", c=TC)
            dve.wait_ge(g0_pe, 1)
            dve.wait_ge(par_in, 16 * N_PAR)
            dve.tensor_tensor(G, bank[4][:, 0:16].rearrange("p (c n) -> p c n", c=TC),
                              bif[:, :].unsqueeze(1).to_broadcast([P, TC, 8]), ALU.add).then_inc(g0_dve, 1)
            dve.wait_ge(g0_dve, 1)
            four = "p (c n) -> p c n"
            dve.scalar_tensor_tensor(out=sm[:, 1, 0:8].rearrange(four, c=TC), in0=G[:, :, 4:8], scalar=-1.0,
                                     in1=G[:, :, 4:8], op0=ALU.mult, op1=ALU.max).then_inc(g0_dve, 1)
            dve.wait_ge(g0_act, 2)
            dve.scalar_tensor_tensor(out=sm[:, 4, 0:8].rearrange(four, c=TC), in0=G[:, :, 4:8], scalar=0.0,
                                     in1=sm[:, 3, 0:8].rearrange(four, c=TC), op0=ALU.min,
                                     op1=ALU.subtract).then_inc(g0_dve, 1)
            cuts.through(0)
            dve.wait_ge(g0_pe, 2)
            own(dve.tensor_copy(sm[:, 6, 0:8], bank[5][:, 0:8]))
            dve.tensor_tensor(sm[:, 5, 0:8].rearrange(four, c=TC), G[:, :, 0:4],
                              bank[5][:, 0:8].rearrange(four, c=TC), ALU.subtract).then_inc(g0_dve, 1)
            cuts.through(1)
            dve.wait_ge(g0_pe, 3)
            dve.tensor_copy(mrow[0:4, 0, :], bank[5][0:4, 256:512]).then_inc(g0_dve, 1)
            dve.wait_ge(g0_dve, 5)
            dve.tensor_tensor_scan(mrow[0:4, 1, :], mrow[0:4, 0, :], mrow[0:4, 0, :], 0.0, ALU.max, ALU.max) \
               .then_inc(g0_dve, 1)
            dve.wait_ge(g0_dve, 6)
            dve.tensor_scalar(mrow[0:4, 2, :], mrow[0:4, 1, :], -1.0, None, ALU.mult).then_inc(g0_dve, 1)
            cuts.through(2)
            dve.wait_ge(g0_pe, 4)
            dve.tensor_tensor(sm[:, 7, 0:8], sm[:, 6, 0:8], bank[5][:, 16:24], ALU.add).then_inc(g0_dve, 1)
            for s, at in ((2, 2), (3, 4)):
                cuts.through(s)
                products(dve, s)
                for c in range(TC):
                    dve.tensor_copy(mv[:, c, 2 * (s - 2):2 * (s - 2) + 2, 0:256], b2(at + c)).then_inc(ev0v, 1)

            def head_scores(h):
                dve.wait_ge(h_w, h + 1)
                dve.wait_ge(h_qk, h + 1)
                dve.tensor_tensor(msc[:, h % 2, :], bank[3 + 4 * (h % 2)][:, 0:384], mw[:, h % 2, :], ALU.mult) \
                   .then_inc(h_sc, 1)

            def head_out(h):
                dve.wait_ge(h_num, h + 1)
                nb = [bank[(0, 4)[h % 2] + c] for c in range(TC)]
                for c in range(TC):
                    own(dve.tensor_tensor(den[:, 0, c:c + 1], nb[c][:, 256:257], sm[:, 8, 4 * c + h:4 * c + h + 1],
                                          ALU.max))
                settled()
                for c in range(TC):
                    own(dve.scalar_tensor_tensor(out=den[:, 0, c:c + 1], in0=nb[c][:, 256:257], scalar=-1.0,
                                                 in1=den[:, 0, c:c + 1], op0=ALU.mult, op1=ALU.max))
                settled()
                step(dve.reciprocal(den[:, 1, 0:TC], den[:, 0, 0:TC]))
                for c in range(TC):
                    dve.tensor_scalar(xn[:, c, ML_DV * h:ML_DV * (h + 1)], nb[c][:, 0:256], den[:, 1, c:c + 1], None,
                                      ALU.mult).then_inc(h_hs, 1)

            def head_var(h):
                dve.wait_ge(sq_sum[1], TC * (h + 1))
                dve.tensor_scalar(va[:, 1, 2 * h:2 * h + 2], ss[:, 1, 2 * h:2 * h + 2], 1.0 / ML_DV, EPS, ALU.mult,
                                  ALU.add).then_inc(var_ok[1], 1)

            def head_gate(h):
                dve.wait_ge(rs_ok[1], h + 1)
                for c in range(TC):
                    v = xn[:, c, ML_DV * h:ML_DV * (h + 1)]
                    ins = dve.scalar_tensor_tensor(out=v, in0=v, scalar=rs[:, 1, 2 * h + c:2 * h + c + 1],
                                                   in1=mog[:, c, ML_DV * h:ML_DV * (h + 1)],
                                                   op0=ALU.mult, op1=ALU.mult)
                ins.then_inc(xn_ok[1], 1)

            cuts.to(2 * 5 + 1 + CUT)
            dve.wait_ge(g0_act, 3)
            head_scores(0)
            for h in range(1, ML_H + 1):
                if h < ML_H:
                    head_scores(h)
                if h >= 2:
                    head_var(h - 2)
                head_out(h - 1)
                if h >= 2:
                    head_gate(h - 2)
            head_var(ML_H - 1)
            head_gate(ML_H - 1)
            turned(1, gcol(1))

            def add(r, c, half, at):
                v = x[:, c, 512 * half:512 * (half + 1)]
                dve.tensor_tensor(v, v, bank[at][:, :], ALU.add).then_inc(res[r], 1)

            def project_out(r, k, i):
                cuts.through(k)
                products(dve, k)
                for c in range(TC):
                    add(r, c, 0, 4 + c)
                cuts.through(k + 1)
                dve.wait_ge(first_chunk, r + 1)
                add(r, 0, 1, 6)
                norm(i, 0, 3)
                products(dve, k + 1)
                add(r, 1, 1, 7)
                norm(i, 1, 4)

            project_out(0, 6, 2)

            turned(2, gcol(2))
            for j in range(FJ):
                cuts.through(ffn_slab[("gate", j)])
                cuts.through(ffn_slab[("up", j)])
                products(dve, ffn_slab[("up", j)])
                for a in range(2):
                    dve.wait_ge(f_silu, 2 * j + a + 1)
                    dve.tensor_tensor(fhh[:, 2 * a:2 * a + 2, :], b2(2 + a), fsg[:, 2 * a:2 * a + 2, :],
                                      ALU.mult).then_inc(f_hh, 1)
                if j >= 1:
                    cuts.through(ffn_slab[("down", j - 1)])
                for a in range(2):
                    part = slice(512 * a, 512 * (a + 1))
                    dve.wait_ge(f_hi, 2 * j + a + 1)
                    dve.tensor_tensor(hr[:, 1, part], fhh[:, 2 * a:2 * a + 2, :].rearrange("p a t -> p (a t)"),
                                      hr[:, 0, part].bitcast(F32), ALU.subtract).then_inc(f_lo, 1)
                level_masks(j)
            small_low(2, w_ba, w_ba_r)
            dve.wait_ge(tap_t, 1)
            dve.tensor_copy(taps[:, :, :].rearrange("p a b -> p (a b)"), bank[0][:, 0:96]).then_inc(tap_e, 1)
            cuts.through(ffn_slab[("down", FJ - 1)])
            for c in range(TC):
                if c == 0:
                    dve.wait_ge(first_chunk, 2)
                else:
                    products(dve, ffn_slab[("down", FJ - 1)])
                for half in range(2):
                    add(1, c, half, 4 + 2 * c + half)
                norm(3, c, 2 * c + 2)

            turned(3, gcol(3))
            cuts.to(2 * GDN0 - 1 + CUT)
            SB = sm[:, 0:2, :]
            dve.wait_ge(g1_pe, 1)
            bk = bank[4][:, 0:32].rearrange("p (c n) -> p c n", c=TC)
            own(dve.tensor_copy(SB[:, :, 0:8], bk[:, :, 0:8]))
            own(dve.tensor_tensor(SB[:, :, 8:16], bk[:, :, 8:16], dtb[:, :].unsqueeze(1).to_broadcast([P, TC, 8]),
                                  ALU.add))
            settled()
            dve.scalar_tensor_tensor(out=sm[:, 12:14, :], in0=SB, scalar=-1.0, in1=SB, op0=ALU.mult,
                                     op1=ALU.max).then_inc(g1_dve, 3)
            dve.wait_ge(g1_act, 3)
            lnb = sm[:, 19, :].rearrange("p (c n) -> p c n", c=TC)
            gg = sm[:, 4, :].rearrange("p (c n) -> p c n", c=TC)
            own(dve.scalar_tensor_tensor(out=lnb, in0=SB[:, :, 0:8], scalar=0.0, in1=sm[:, 16:18, 0:8], op0=ALU.min,
                                         op1=ALU.subtract))
            step(dve.scalar_tensor_tensor(out=sm[:, 2:4, 0:8], in0=SB[:, :, 8:16], scalar=0.0,
                                          in1=sm[:, 16:18, 8:16], op0=ALU.max, op1=ALU.add))
            dve.scalar_tensor_tensor(out=gg, in0=sm[:, 2:4, 0:8], scalar=-1.0,
                                     in1=sm[:, 10, 0:8].unsqueeze(1).to_broadcast([P, TC, 8]),
                                     op0=ALU.mult, op1=ALU.mult).then_inc(g1_dve, 1)
            cuts.through(GDN0)
            dve.wait_ge(g1_pe, 2)
            own(dve.tensor_scalar(sm[:, 11, :], bank[5][:, 0:16], -1.0, None, ALU.mult))
            own(dve.tensor_copy(sm[:, 22, :], bank[5][:, 0:16]))
            settled()
            own(dve.tensor_tensor(sm[:, 23, 0:8], sm[:, 11, 0:8], bank[5][:, 16:24], ALU.add))
            own(dve.tensor_tensor(sm[:, 21, :], sm[:, 19, :], sm[:, 22, :], ALU.add))
            settled()
            dve.tensor_copy(sm[:, 9, :], sm[:, 22, :]).then_inc(g1_dve, 4)
            cuts.through(GDN0 + 1)
            dve.wait_ge(g1_pe, 3)
            dve.tensor_copy(rows2[0:8, :, :].rearrange("p a t -> p (a t)"), bank[4][0:8, :]).then_inc(g1_dve, 1)

            small_low(3, w_rt, w_rt_r)

            def conv(s):
                dst = (gq, gk, gv)[s // 2]
                cuts.through(GDN0 + s)
                dve.wait_ge(ev1, 2 * s + 2)
                if s == 0:
                    dve.wait_ge(tap_e, 1)
                for k in range(GD_K):
                    for a in range(4):
                        o = dst[:, 4 * (s % 2) + a, :]
                        i = graw[:, s % 2, a, k:k + S]
                        t = taps[:, k, 4 * s + a:4 * s + a + 1]
                        if k == 0:
                            ins = dve.tensor_scalar(o, i, t, None, ALU.mult)
                        else:
                            ins = dve.scalar_tensor_tensor(out=o, in0=i, scalar=t, in1=o, op0=ALU.mult, op1=ALU.add)
                        if k < GD_K - 1:
                            own(ins)
                    if k < GD_K - 1:
                        settled()
                ins.then_inc(conv_ok, 1)

            def squares(s):
                for a in range(2):
                    dve.wait_ge(ssq_pe, 2 * s + a + 1)
                    dve.tensor_scalar(rsq[:, 4 * s + 2 * a:4 * s + 2 * a + 2, :], b2([6, 0, 2, 4][s] + a), EPS, None,
                                      ALU.add).then_inc(ssq_ev, 1)

            for s in range(6):
                conv(s)
                if 2 <= s < 6:
                    squares(s - 2)
            cuts.through(GDN0 + 6)
            for s in range(4):
                dst = (gq, gk)[s // 2][:, 4 * (s % 2):4 * (s % 2) + 4, :]
                dve.wait_ge(ln_ok, s + 1)
                dve.scalar_tensor_tensor(out=dst, in0=rsq[:, 4 * s:4 * s + 4, :],
                                         scalar=GD_DK ** -0.5 if s < 2 else 1.0, in1=dst,
                                         op0=ALU.mult, op1=ALU.mult).then_inc(qk_ok, 1)
            cuts.to(2 * (GDN0 + 8) - 1 + CUT)
            dve.wait_ge(g1_act, 4)
            for gi in range(8):
                hg = gi % 2
                hs = slice(4 * hg, 4 * hg + 4)
                dve.wait_ge(kv_t, 8 if gi >= 4 else gi + 1)
                if gi < 2:
                    dst, sc = kbg[:, hs, :], sm[:, 20, 4 * hg:4 * hg + 4]
                elif gi < 4:
                    dst, sc = kdec[:, hs, :], sm[:, 23, 8 + 4 * hg:12 + 4 * hg]
                else:
                    c = (gi - 4) // 2
                    dst, sc = vb[:, c, hs, :], sm[:, 18, 8 * c + 4 * hg:8 * c + 4 * hg + 4]
                dve.tensor_tensor(dst, b2([0, 1, 2, 3, 4, 5, 6, 7][gi], 4), sc.unsqueeze(2).to_broadcast([P, 4, P]),
                                  ALU.mult).then_inc(kv_ev, 1)
            for h in range(GD_H):
                dve.wait_ge(gam_ok, h + 1)
                dve.wait_ge(kq_ok, h + 1)
                kq = bank[h % 2][:, :].rearrange("p (a c t) -> p a c t", a=2, c=TC)
                own(dve.scalar_tensor_tensor(out=nAT[:, :, h, :], in0=kq[:, 0], scalar=-1.0, in1=gam[:, h % 2, 0],
                                             op0=ALU.mult, op1=ALU.mult))
                dve.tensor_tensor(attT[:, :, h, :], kq[:, 1], gam[:, h % 2, 1], ALU.mult).then_inc(att_ok, 1)
            settled()
            for gi in range(4):
                c, hs = gi // 2, slice(4 * (gi % 2), 4 * (gi % 2) + 4)
                eye = ident[:, :].unsqueeze(1).to_broadcast([P, 4, P])
                own(dve.tensor_copy(Tn[:, c, hs, :], eye))
                own(dve.tensor_copy(Tt[:, c, hs, :], eye))
            settled()
            for l in range(7):
                lo = low[:, l, :].unsqueeze(1).to_broadcast([P, 4, P])
                up = upp[:, l, :].unsqueeze(1).to_broadcast([P, 4, P])
                for gi in range(4):
                    c, hs = gi // 2, slice(4 * (gi % 2), 4 * (gi % 2) + 4)
                    if l == 0:
                        dve.wait_ge(inv_x, gi + 1)
                        own(dve.copy_predicated(Tn[:, c, hs, :], lo, b2(2 * gi, 4)))
                        dve.copy_predicated(Tt[:, c, hs, :], up, nAT[:, c, hs, :]).then_inc(inv_t, 1)
                        continue
                    dve.wait_ge(inv_d, 4 * (l - 1) + gi + 1)
                    if l < 6:
                        own(dve.copy_predicated(Tn[:, c, hs, :], lo, b2(2 * gi, 4)))
                    dve.copy_predicated(Tt[:, c, hs, :], up, b2(2 * gi + 1, 4)).then_inc(inv_t, 1)
            og = xn[:, :, :].rearrange("p c (h d) -> p c h d", h=GD_H)
            for gi in range(2):
                hs = slice(4 * gi, 4 * gi + 4)
                dve.wait_ge(s_pe, 4 + 3 * gi + 2)
                step(dve.tensor_copy(og[:, 0, hs, :], b2(5 + 2 * gi, 4)))
                dve.wait_ge(s_pe, 4 + 3 * gi + 3)
                dve.tensor_tensor(og[:, 1, hs, :], b2(1 + 2 * gi, 4),
                                  sm[:, 20, 8 + 4 * gi:12 + 4 * gi].unsqueeze(2).to_broadcast([P, 4, P]),
                                  ALU.mult).then_inc(s_dve, 1)

            def head_norm(c, gi):
                t, hs = 2 * c + gi, slice(4 * gi, 4 * gi + 4)
                o, z = og[:, c, hs, :], gz[:, c, 512 * gi:512 * (gi + 1)].rearrange("p (h d) -> p h d", h=4)
                step(dve.tensor_tensor(osq[:, 4 * t:4 * t + 4, :], o, o, ALU.mult))
                step(dve.tensor_reduce(ss[:, 4, 4 * t:4 * t + 4], osq[:, 4 * t:4 * t + 4, :], AX.X, ALU.add))
                dve.tensor_scalar(va[:, 4, 4 * t:4 * t + 4], ss[:, 4, 4 * t:4 * t + 4], 1.0 / GD_DV, EPS, ALU.mult,
                                  ALU.add).then_inc(var_ok[4], 1)
                step(dve.tensor_tensor(o, o, z, ALU.mult))
                dve.wait_ge(rs_ok[4], t + 1)
                dve.tensor_tensor(o, o, rs[:, 4, 4 * t:4 * t + 4].unsqueeze(2).to_broadcast([P, 4, P]), ALU.mult) \
                   .then_inc(xn_ok[4], 1)

            for gi in range(2):
                head_norm(0, gi)
            for gi in range(2):
                hs = slice(4 * gi, 4 * gi + 4)
                dve.wait_ge(s_pe, 10 + 2 * gi + 2)
                dve.wait_ge(s_dve, gi + 1)
                step(dve.tensor_tensor(og[:, 1, hs, :], og[:, 1, hs, :], b2(4 + 2 * gi, 4), ALU.add))
                head_norm(1, gi)
            turned(4, lambda c: gains[:, 5 * DC:5 * DC + 1])
            project_out(2, GDN0 + 8, 5)

            turned(5, gcol(4))
            cuts.to(MU0 + AHEAD - 1)
            r16 = "p (c n) -> p c n"

            def t8(i):
                return rt[:, i, :].rearrange(r16, c=TC)

            ramp = iot[:, 0:NE].unsqueeze(1).to_broadcast([P, TC, NE])

            def col(i):
                return rt[:, i, 0:TC]

            def wide(i):
                return col(i).unsqueeze(2).to_broadcast([P, TC, NE])

            dve.wait_ge(r_pe, 1)
            step(dve.tensor_copy(t8(0), bank[4][:, 0:16].rearrange(r16, c=TC)))

            def top(src, m, hot):
                step(dve.tensor_reduce(col(m), t8(src), AX.X, ALU.max))
                step(dve.tensor_tensor(t8(8), t8(src), wide(m), ALU.is_equal))
                step(dve.scalar_tensor_tensor(out=t8(8), in0=t8(8), scalar=-100.0, in1=ramp, op0=ALU.mult,
                                              op1=ALU.add))
                step(dve.tensor_reduce(col(9), t8(8), AX.X, ALU.min))
                step(dve.tensor_tensor(t8(hot), t8(8), wide(9), ALU.is_equal))

            top(0, 3, 1)
            step(dve.scalar_tensor_tensor(out=t8(7), in0=t8(1), scalar=NEG, in1=t8(0), op0=ALU.mult, op1=ALU.add))
            top(7, 4, 2)
            dve.tensor_tensor(col(5), col(4), col(3), ALU.subtract).then_inc(r_dve, 1)
            dve.tensor_tensor(t8(10), t8(1), t8(2), ALU.add).then_inc(r_dve, 1)
            dve.wait_ge(r_act, 1)
            step(dve.tensor_scalar(col(11), col(6), 1.0, None, ALU.add))
            step(dve.reciprocal(col(12), col(11)))
            step(dve.tensor_tensor(col(13), col(6), col(12), ALU.mult))
            own(dve.tensor_tensor(t8(1), t8(1), wide(12), ALU.mult))
            step(dve.tensor_tensor(t8(2), t8(2), wide(13), ALU.mult))
            step(dve.tensor_tensor(gate9[:, :, 0:NE], t8(1), t8(2), ALU.add))
            own(dve.tensor_copy(gate9[:, :, NE:NE + 1], gate9[:, :, 0:1]))
            dve.wait_ge(r_pe, 2)
            rk = bank[5][:, 0:16].rearrange(r16, c=TC)
            step(dve.tensor_tensor(t8(14), rk, t8(10), ALU.mult))
            step(dve.tensor_scalar(posm[:, :, 0:NE], t8(14), -1.0, None, ALU.add))
            dve.tensor_scalar(posm[:, :, NE:NE + 1], posm[:, :, 0:1], -float(CAP), None, ALU.add).then_inc(e_x, 4)
            dve.wait_ge(e_x, 4)
            step(dve.tensor_reduce(rt[0:1, 15, 0:1], bank[5][0:1, 16:24], AX.X, ALU.max))
            step(dve.tensor_scalar(rt[0:1, 15, 1:2], rt[0:1, 15, 0:1], -0.5, None, ALU.is_gt))
            for b in range(1, ROUNDS):
                step(dve.scalar_tensor_tensor(out=rt[0:1, 15, b + 1:b + 2], in0=rt[0:1, 15, 0:1],
                                              scalar=float(b * CAP), in1=rt[0:1, 15, b:b + 1], op0=ALU.is_gt,
                                              op1=ALU.add))
            dve.tensor_copy(nrounds[0:1, 0:1], rt[0:1, 15, ROUNDS:ROUNDS + 1]).then_inc(routed, 1)
            settled()
            dve.wait_ge(routed, 1)

            def select(e):
                for c in range(TC):
                    dve.tensor_scalar(eP[:, c, :], iot[:, 0:CAP], posm[:, c, bass.ds(e, 1)], None, ALU.is_equal)
                for c in range(TC):
                    ins = dve.tensor_scalar(ePG[:, c, :], iot[:, 0:CAP], posm[:, c, bass.ds(e, 1)],
                                            gate9[:, c, bass.ds(e, 1)], ALU.is_equal, ALU.mult)
                ins.then_inc(e_sel, 1)

            def gathered(it):
                for a in range(2):
                    dve.wait_ge(e_gather, it * 2 + (a + 1))
                    gh = gains[:, 4 * DC + 4 * a:4 * DC + 4 * a + 4].unsqueeze(2).to_broadcast([P, 4, CAP])
                    dve.tensor_tensor(exg[:, 4 * a:4 * a + 4, :],
                                      bank[4 + a][:, 0:4 * CAP].rearrange("p (a n) -> p a n", a=4), gh,
                                      ALU.mult).then_inc(e_xg, 1)
                for a in range(2):
                    part = slice(4 * CAP * a, 4 * CAP * (a + 1))
                    dve.wait_ge(e_xhi, it * 2 + (a + 1))
                    dve.tensor_tensor(hTr[:, 1, part], exg[:, 4 * a:4 * a + 4, :].rearrange("p a n -> p (a n)"),
                                      hTr[:, 0, part].bitcast(F32), ALU.subtract).then_inc(e_xlo, 1)

            select(0)
            gathered(0)
            nr = dve.value_load(nrounds[0:1, 0:1], min_val=1, max_val=ROUNDS)
            with dve.Fori(0, nr) as b:
                with dve.Fori(0, NE) as e:
                    it = dve.snap(b * NE + e)
                    cuts.done = MU0 + AHEAD

                    def low_part(j):
                        dve.wait_ge(e_thi, it * FJ + (j + 1))
                        dve.tensor_tensor(hidden(1, j), bank[2][:, 0:FC * CAP], hidden(0, j).bitcast(F32),
                                          ALU.subtract).then_inc(e_tlo, 1)

                    for j in range(FJ):
                        cuts.through(MOE0 + place[("gate", j)], it)
                        if j >= 1:
                            low_part(j - 1)
                        k = MOE0 + place[("up", j)]
                        cuts.through(k, it)
                        products(dve, k, it)
                        dve.wait_ge(e_silu, it * FJ + (j + 1))
                        if j >= 1:
                            dve.wait_ge(e_t, it * FJ + j)
                        dve.tensor_tensor(ehh[0:CAP, :], bank[1][0:CAP, :], esg[0:CAP, :], ALU.mult) \
                           .then_inc(e_hh, 1)
                        if j == 3:
                            dve.wait_ge(e_turn, it + 1)
                            select(e + 1)
                    gathered(it + 1)
                    cuts.through(MOE0 + PER - 2, it)
                    low_part(FJ - 1)
                    cuts.to(MU0 + UPER, it)
                    products(dve, MOE0 + PER - 1, it)
                    dve.tensor_copy(eyg[0:CAP, 512:1024], bank[7][0:CAP, :]).then_inc(e_yg2, 1)
                    for m in range(4):
                        c, half = m % 2, m // 2
                        dve.wait_ge(e_sc, it * 4 + (m + 1))
                        v = x[:, c, 512 * half:512 * (half + 1)]
                        dve.tensor_tensor(v, v, bank[scatter_banks[m]][:, :], ALU.add).then_inc(e_x, 1)
                        if m == 1:
                            cuts.to(MU0 + UPER + 1, it)
                    cuts.to(MU0 + UPER + AHEAD - 1, it)
                dve.wait_ge(e_sel, b * NE + (NE + 1))
                dve.tensor_scalar(posm[:, :, :], posm[:, :, :], -float(CAP), None, ALU.add).then_inc(e_own, 1)
                dve.wait_ge(e_own, b + 1)

            dve.wait_ge(par3_in, 16)
            for c in range(TC):
                norm_root(6, c, 3 + c)
                dve.scalar_tensor_tensor(out=fout[:, c, :], in0=x[:, c, :], scalar=rs[:, 6, c:c + 1],
                                         in1=fgain[:, :], op0=ALU.mult, op1=ALU.mult).then_inc(fin_ok, 1)

        @block.tensor
        def _(pe):
            mm = pe.matmul

            def ready(u):
                pe.wait_ge(lo_ok, u + 1)

            def three(o, sh, sl, mh, ml, start, stop):
                mm(o, sh, mh, start=start, stop=False, skip_group_check=True)
                mm(o, sh, ml, start=False, stop=False, skip_group_check=True)
                return mm(o, sl, mh, start=False, stop=stop, skip_group_check=True)

            def turn_one(k, a, c):
                d = 2 * k + a
                return pe.transpose(bank[k][:, a * S + c * P:a * S + (c + 1) * P], xn[:, c, d * P:(d + 1) * P],
                                    ident[:, :])

            def turn(i):
                for c in range(TC):
                    pe.wait_ge(xn_ok[i], c + 1)
                    for k in range(4):
                        for a in range(2):
                            ins = turn_one(k, a, c)
                        if c == TC - 1:
                            ins.then_inc(tr_ok[i], 1)

            def turn_heads(i, steps):
                for k in range(4):
                    pe.wait_ge(xn_ok[i], steps[k])
                    for a in range(2):
                        for c in range(TC):
                            ins = turn_one(k, a, c)
                    ins.then_inc(tr_ok[i], 1)

            def fresh_part(i, c):
                if i is not None:
                    pe.wait_ge(hT_lo[i], c + 1)

            def tall(k, at, fresh=None):
                for c in range(DC):
                    u = 2 * k + c // 4
                    if c % 4 == 0:
                        ready(u)
                    fresh_part(fresh, c)
                    wh, wl = unit_view(whi, u % CUT, False)[:, c % 4], unit_view(wlo, u % CUT, False)[:, c % 4]
                    for a in range(4):
                        o = bank[at + a // 2][:, (a % 2) * S:(a % 2 + 1) * S]
                        v = slice(a * P, (a + 1) * P)
                        ins = three(o, wh[:, v], wl[:, v], xh[:, c, :], xl[:, c, :],
                                    start=(c == 0 and a % 2 == 0), stop=(c == DC - 1))
                    if c % 4 == 3:
                        ins.then_inc(unit_used, 1)

            def flat(k, at, fresh=None, chunk_first=False):
                for half in range(2):
                    u = 2 * k + half
                    ready(u)
                    wh, wl = unit_view(whi, u % CUT, False), unit_view(wlo, u % CUT, False)
                    steps = [(q, t) for q in range(4) for t in range(TC)]
                    if chunk_first and half == 1:
                        steps.sort(key=lambda step: step[1])
                    for q, t in steps:
                        c, v = 4 * half + q, slice(t * P, (t + 1) * P)
                        fresh_part(fresh, c)
                        ins = three(bank[at + t][:, :], xh[:, c, v], xl[:, c, v], wh[:, q], wl[:, q],
                                    start=(c == 0), stop=(c == DC - 1))
                        if chunk_first and (c, t) == (DC - 1, 0):
                            ins.then_inc(first_chunk, 1)
                    ins.then_inc(unit_used, 1)

            def narrow(wr, n):
                for t in range(TC):
                    v = slice(t * P, (t + 1) * P)
                    for c in range(DC):
                        ins = three(bank[4][:, n * t:n * (t + 1)], xh[:, c, v], xl[:, c, v], wr[:, 0, c, :],
                                    wr[:, 1, c, :], start=(c == 0), stop=(c == DC - 1))
                return ins

            pe.wait_ge(consts, 1)
            pe.wait_ge(par_in, 16 * N_PAR)
            pe.transpose(bank[4][:, 0:41], packG[0:41, :], ident[0:41, 0:41]).then_inc(pack_t, 1)

            turn(0)
            pe.wait_ge(pack_e, 1)
            pe.wait_ge(hT_lo[0], DC)
            pe.wait_ge(small_lo, 1)
            narrow(w_if_r, 2 * ML_H).then_inc(g0_pe, 1)
            tall(0, 6)
            pe.wait_ge(g0_dve, 3)
            lf = sm[:, 4, :]
            mm(bank[5][:, 0:4], incl[:, :], lf[:, 0:4], start=True, stop=True)
            mm(bank[5][:, 4:8], incl[:, :], lf[:, 4:8], start=True, stop=False)
            mm(bank[5][:, 4:8], ones, lf[:, 0:4], start=False, stop=True).then_inc(g0_pe, 1)
            tall(1, 0)
            pe.wait_ge(g0_dve, 4)
            for c in range(TC):
                ins = pe.transpose(bank[5][0:4, 256 + c * P:256 + (c + 1) * P], sm[:, 5, 4 * c:4 * c + 4], ident[:, :])
            ins.then_inc(g0_pe, 1)
            flat(2, 2)
            pe.wait_ge(g0_dve, 7)
            for c in range(TC):
                ins = pe.transpose(bank[5][:, 16 + 4 * c:20 + 4 * c], mrow[0:4, 1, c * P:(c + 1) * P], ident[0:4, 0:4])
            ins.then_inc(g0_pe, 1)
            pe.wait_ge(g0_dve, 8)
            flat(3, 4)
            pe.wait_ge(ev0, 2)
            flat(4, 6)
            pe.wait_ge(ev0, 4)
            flat(5, 0)

            def weigh(h):
                o = bank[2 + 4 * (h % 2)]
                pick = ident[0:4, h:h + 1].to_broadcast([4, P])
                nmu = mrow[0:4, 2, :]
                if h >= 2:
                    pe.wait_ge(h_w, h - 1)
                mm(o[:, 0:256], pick, nmu, start=True, stop=False)
                mm(o[:, 0:128], ident[:, :], neg[:, 1, :], start=False, stop=True)
                mm(o[:, 256:384], pick, nmu[:, 128:256], start=True, stop=False)
                mm(o[:, 256:384], ident[:, :], neg[:, 1, :], start=False, stop=True).then_inc(h_bc, 1)
                if h >= 2:
                    pe.wait_ge(h_sc, h - 1)
                o = bank[3 + 4 * (h % 2)]
                mm(o[:, 0:256], mk[:, h, 0:128], mq[:, h, :], start=True, stop=True)
                mm(o[:, 256:384], mk[:, h, 128:256], mq[:, h, 128:256], start=True, stop=True).then_inc(h_qk, 1)

            def gather_values(h):
                pe.wait_ge(h_sc, h + 1)
                if h >= 2:
                    pe.wait_ge(h_hs, TC * (h - 1))
                sc = msc[:, h % 2, :]
                at = (0, 4)[h % 2]
                mm(bank[at][:, 0:257], sc[:, 0:128], mv[:, 0, h, :], start=True, stop=True)
                mm(bank[at + 1][:, 0:257], sc[:, 128:256], mv[:, 0, h, :], start=True, stop=False)
                mm(bank[at + 1][:, 0:257], sc[:, 256:384], mv[:, 1, h, :], start=False, stop=True).then_inc(h_num, 1)

            pe.wait_ge(ev0v, 4)
            weigh(0)
            pe.wait_ge(ev0, 8)
            for h in range(ML_H):
                if h + 1 < ML_H:
                    weigh(h + 1)
                gather_values(h)
            pe.wait_ge(h_hs, TC * (ML_H - 1))
            turn_heads(1, (1, 2, 3, 4))
            flat(6, 4, 1)
            flat(7, 6, chunk_first=True)

            def ffn_in(kind, j, at):
                if j >= 1:
                    pe.wait_ge(f_silu if kind == "gate" else f_hh, 2 * j)
                tall(ffn_slab[(kind, j)], at, 2 if j == 0 and kind == "gate" else None)

            fh = hr[:, 0, :].rearrange("p (a t) -> p a t", a=FC)
            fl = hr[:, 1, :].rearrange("p (a t) -> p a t", a=FC)

            def ffn_out(j):
                k = ffn_slab[("down", j)]
                for part in range(2):
                    u = 2 * k + part
                    ready(u)
                    pe.wait_ge(f_lo, 2 * j + part + 1)
                    wh, wl = unit_view(whi, u % CUT, True), unit_view(wlo, u % CUT, True)
                    last = j == FJ - 1 and part == 1
                    steps = [(q, t) for q in range(2) for t in range(TC)]
                    if last:
                        steps.sort(key=lambda step: step[1])
                    for q, t in steps:
                        a, v = 2 * part + q, slice(t * P, (t + 1) * P)
                        for half in range(2):
                            n = slice(512 * half, 512 * (half + 1))
                            ins = three(bank[4 + 2 * t + half][:, :], fh[:, a, v], fl[:, a, v], wh[:, q, n],
                                        wl[:, q, n], start=(j == 0 and a == 0), stop=(j == FJ - 1 and a == FC - 1))
                        if last and (q, t) == (1, 0):
                            ins.then_inc(first_chunk, 1)
                    ins.then_inc(unit_used, 1)

            turn(2)
            pe.wait_ge(res[0], 4)
            for j in range(FJ + 1):
                if j < FJ:
                    ffn_in("gate", j, gate_bank(j))
                    ffn_in("up", j, 2)
                if j == FJ:
                    pe.wait_ge(par2_in, 16 * N_PAR2)
                    pe.wait_ge(f_silu, 2 * FJ)
                    pe.transpose(bank[0][:, 0:96], packT[0:96, :], ident[0:96, 0:96]).then_inc(tap_t, 1)
                if j > 0:
                    ffn_out(j - 1)

            pe.wait_ge(tap_e, 1)
            turn(3)
            pe.wait_ge(res[1], 4)
            pe.wait_ge(hT_lo[3], DC)
            pe.wait_ge(small_lo, 2)
            narrow(w_ba_r, 2 * GD_H).then_inc(g1_pe, 1)

            def gdn_in(s):
                at = 2 * ((s + 3) % 4)
                if s >= 4:
                    pe.wait_ge(ev1, 2 * (s - 3))
                    pe.wait_ge(ssq_ev, 2 * (s - 3))
                (tall if s < 6 else flat)(GDN0 + s, at)

            def lengths(s):
                at = [6, 0, 2, 4][s]
                pe.wait_ge(sqr_ok, s + 1)
                pe.wait_ge(ev1, 2 * ([0, 1, 2, 3][s] + 1))
                for a in range(2):
                    mm(bank[at + a][:, :], ones,
                       sqb[:, s % 2, 2 * a:2 * a + 2, :].rearrange("p a t -> p (a t)"),
                       start=True, stop=True).then_inc(ssq_pe, 1)

            gdn_in(0)
            pe.wait_ge(g1_dve, 4)
            g = sm[:, 4, :]
            mm(bank[5][:, 0:16], incl[:, :], g, start=True, stop=True)
            mm(bank[5][:, 16:24], ones, g[:, 0:8], start=True, stop=True).then_inc(g1_pe, 1)
            gdn_in(1)
            pe.wait_ge(g1_dve, 8)
            for a, r in ((0, 21), (1, 22)):
                for c in range(TC):
                    ins = pe.transpose(bank[4][0:8, a * S + c * P:a * S + (c + 1) * P], sm[:, r, 8 * c:8 * c + 8],
                                       ident[:, :])
            ins.then_inc(g1_pe, 1)
            gdn_in(2)
            pe.wait_ge(g1_dve, 9)
            lengths(0)
            for q in range(1, 4):
                gdn_in(q + 2)
                lengths(q)
            gdn_in(6)
            gdn_in(7)
            pe.wait_ge(ev1, 16)
            pe.wait_ge(qk_ok, 4)
            pe.wait_ge(silu_ok, 2)
            for gi in range(8):
                hg = gi % 2
                src, c = ((gk, 1), (gk, 0), (gv, 0), (gv, 1))[gi // 2]
                for a in range(4):
                    ins = pe.transpose(bank[gi][:, a * P:(a + 1) * P], src[:, 4 * hg + a, c * P:(c + 1) * P],
                                       ident[:, :])
                ins.then_inc(kv_t, 1)

            def decay(h):
                pe.wait_ge(kv_ev, 5 + h % 2 + 1) if h < 2 else pe.wait_ge(gam_ok, h - 1)
                o = bank[4 + h % 2][:, :]
                mm(o, ident[0:8, h:h + 1].to_broadcast([8, P]), rows2[0:8, :, :].rearrange("p a t -> p (a t)"),
                   start=True, stop=False)
                mm(o.rearrange("p (a c t) -> p a c t", a=2, c=TC), ident[:, :],
                   neg[:, :, :].unsqueeze(2).to_broadcast([P, 2, TC, P]), start=False, stop=True).then_inc(bc_ok, 1)

            def scores(h):
                if h >= 2:
                    pe.wait_ge(att_ok, h - 1)
                for a, q in ((0, gk), (1, gq)):
                    for c in range(TC):
                        ins = mm(bank[h % 2][:, (2 * a + c) * P:(2 * a + c + 1) * P], gk[:, h, c * P:(c + 1) * P],
                                 q[:, h, c * P:(c + 1) * P], start=True, stop=True)
                ins.then_inc(kq_ok, 1)

            pe.wait_ge(kv_ev, 2)
            for h in range(GD_H):
                decay(h)
                scores(h)
            pe.wait_ge(att_ok, 8)
            pe.wait_ge(kv_ev, 8)
            for gi in range(4):
                c = gi // 2
                for a in range(4):
                    h = 4 * (gi % 2) + a
                    ins = mm(bank[2 * gi][:, a * P:(a + 1) * P], nAT[:, c, h, :], ident[:, :], start=True, stop=True)
                ins.then_inc(inv_x, 1)
            for l in range(1, 7):
                for gi in range(4):
                    c = gi // 2
                    pe.wait_ge(inv_t, 4 * (l - 1) + gi + 1)
                    for a in range(4):
                        h = 4 * (gi % 2) + a
                        ins = mm(bank[2 * gi][:, a * P:(a + 1) * P], nAT[:, c, h, :], Tn[:, c, h, :],
                                 start=True, stop=True)
                    ins.then_inc(inv_x, 1)
                for gi in range(4):
                    c = gi // 2
                    pe.wait_ge(inv_xs, 4 * (l - 1) + gi + 1)
                    for a in range(4):
                        h = 4 * (gi % 2) + a
                        o = slice(a * P, (a + 1) * P)
                        if l < 6:
                            mm(bank[2 * gi][:, o], Tt[:, c, h, :], xs[:, gi, a, :], start=True, stop=True)
                        ins = mm(bank[2 * gi + 1][:, o], xs[:, gi, a, :], Tt[:, c, h, :], start=True, stop=True)
                    ins.then_inc(inv_d, 1)
            def heads4(gi, at, signal, *products):
                for a in range(4):
                    h = 4 * gi + a
                    for m, (l, r) in enumerate(products):
                        ins = mm(bank[at][:, a * P:(a + 1) * P], l(h), r(h), start=(m == 0),
                                 stop=(m == len(products) - 1))
                ins.then_inc(signal, 1)

            pe.wait_ge(inv_t, 28)
            for gi in range(2):
                heads4(gi, 2 * gi, s_pe, (lambda h: Tt[:, 0, h, :], lambda h: vb[:, 0, h, :]))
                heads4(gi, 2 * gi + 1, s_pe, (lambda h: kbg[:, h, :], lambda h: Tt[:, 1, h, :]))
            for gi in range(2):
                pe.wait_ge(s_act, 2 * gi + 2)
                heads4(gi, 4 + 2 * gi, s_pe, (lambda h: kdec[:, h, :], lambda h: vn[:, 0, h, :]))
                heads4(gi, 5 + 2 * gi, s_pe, (lambda h: attT[:, 0, h, :], lambda h: vn[:, 0, h, :]))
                pe.wait_ge(s_act, 4 + gi + 1)
                heads4(gi, 1 + 2 * gi, s_pe, (lambda h: gq[:, h, P:S], lambda h: st1[:, h, :]))
            for gi in range(2):
                heads4(gi, 2 * gi, s_pe, (lambda h: Tt[:, 1, h, :], lambda h: vb[:, 1, h, :]),
                       (lambda h: nwT[:, h, :], lambda h: st1[:, h, :]))
                pe.wait_ge(s_act, 6 + gi + 1)
                heads4(gi, 4 + 2 * gi, s_pe, (lambda h: attT[:, 1, h, :], lambda h: vn[:, 1, h, :]))
            turn_heads(4, (3, 3, 4, 4))
            flat(GDN0 + 8, 4, 4)
            flat(GDN0 + 9, 6, chunk_first=True)

            turn(5)
            pe.wait_ge(res[2], 4)
            pe.wait_ge(hT_lo[5], DC)
            pe.wait_ge(small_lo, 3)
            narrow(w_rt_r, NE).then_inc(r_pe, 1)
            pe.wait_ge(r_dve, 2)
            sel = rt[:, 10, :]
            mm(bank[5][:, 0:8], incl[:, :], sel[:, 0:8], start=True, stop=True)
            mm(bank[5][:, 8:16], incl[:, :], sel[:, 8:16], start=True, stop=False)
            mm(bank[5][:, 8:16], ones, sel[:, 0:8], start=False, stop=True)
            mm(bank[5][:, 16:24], ones, sel[:, 0:8], start=True, stop=False)
            mm(bank[5][:, 16:24], ones, sel[:, 8:16], start=False, stop=True).then_inc(r_pe, 1)
            pe.wait_ge(routed, 1)
            nr = pe.value_load(nrounds[0:1, 0:1], min_val=1, max_val=ROUNDS)

            def gather(it):
                pe.wait_ge(e_sel, it + 1)
                for a in range(2):
                    for q in range(4):
                        d = 4 * a + q
                        for c in range(TC):
                            ins = mm(bank[4 + a][:, q * CAP:(q + 1) * CAP], xn[:, c, d * P:(d + 1) * P],
                                     eP[:, c, :], start=(c == 0), stop=(c == TC - 1))
                    ins.then_inc(e_gather, 1)

            gather(0)
            with pe.Fori(0, nr) as b:
                with pe.Fori(0, NE) as e:
                    it = pe.snap(b * NE + e)

                    def turn_hidden(j):
                        pe.wait_ge(e_hh, it * FJ + (j + 1))
                        for a in range(FC):
                            ins = pe.transpose(bank[2][:, a * CAP:(a + 1) * CAP], ehh[0:CAP, a * P:(a + 1) * P],
                                               ident[0:CAP, 0:CAP])
                        ins.then_inc(e_t, 1)

                    def turn_gates():
                        for c in range(TC):
                            ins = pe.transpose(bank[3][0:CAP, c * P:(c + 1) * P], ePG[:, c, :], ident[:, :])
                        ins.then_inc(e_turn, 1)

                    gh = hTr[:, 0, 0:DC * CAP].rearrange("p (c n) -> p c n", c=DC)
                    gl = hTr[:, 1, 0:DC * CAP].rearrange("p (c n) -> p c n", c=DC)
                    for m, (kind, j) in enumerate(order):
                        k = MOE0 + m
                        if kind == "down":
                            pe.wait_ge(e_tlo, it * FJ + (j + 1))
                            th = hidden(0, j).rearrange("p (a n) -> p a n", a=FC)
                            tl = hidden(1, j).rearrange("p (a n) -> p a n", a=FC)
                            for half_unit in range(2):
                                u = 2 * k + half_unit
                                pe.wait_ge(lo_ok, it * UPER + (u + 1))
                                wh, wl = unit_view(whi, u % CUT, True), unit_view(wlo, u % CUT, True)
                                for half in range(2):
                                    n = slice(512 * half, 512 * (half + 1))
                                    for q in range(2):
                                        c = 2 * half_unit + q
                                        ins = three(bank[6 + half][0:CAP, :], th[:, c, :], tl[:, c, :],
                                                    wh[:, q, n], wl[:, q, n], start=(j == 0 and c == 0),
                                                    stop=(j == FJ - 1 and c == FC - 1))
                                    if j == FJ - 1 and half_unit == 1 and half == 0:
                                        ins.then_inc(e_y0, 1)
                                ins.then_inc(unit_used, 1)
                                if j == FJ - 2 and half_unit == 0:
                                    turn_hidden(FJ - 1)
                            continue
                        if j >= 1:
                            pe.wait_ge(e_silu if kind == "gate" else e_hh, it * FJ + j)
                        for c in range(DC):
                            u = 2 * k + c // 4
                            if c % 4 == 0:
                                pe.wait_ge(lo_ok, it * UPER + (u + 1))
                                if m == 0:
                                    pe.wait_ge(e_xlo, it * 2 + (c // 4 + 1))
                            wh, wl = unit_view(whi, u % CUT, False), unit_view(wlo, u % CUT, False)
                            ins = three(bank[0 if kind == "gate" else 1][0:CAP, :], gh[:, c, :], gl[:, c, :],
                                        wh[:, c % 4, :], wl[:, c % 4, :], start=(c == 0), stop=(c == DC - 1))
                            if c % 4 == 3:
                                ins.then_inc(unit_used, 1)
                        if kind == "gate" and j >= 1:
                            if j == 1:
                                pe.wait_ge(e_x, it * 4 + 4)
                            turn_hidden(j - 1)
                            if j == 1:
                                turn_gates()
                        if kind == "up" and j == FJ - 1:
                            gather(it + 1)
                    pe.wait_ge(e_gt, it + 1)
                    pe.wait_ge(e_yg, it + 1)
                    for m in range(4):
                        c, half = m % 2, m // 2
                        if m == 2:
                            pe.wait_ge(e_yg2, it + 1)
                        mm(bank[scatter_banks[m]][:, :], eGT[0:CAP, c * P:(c + 1) * P],
                           eyg[0:CAP, 512 * half:512 * (half + 1)], start=True, stop=True).then_inc(e_sc, 1)


_INS = ['x', 'l0_norm_mix', 'l0_ml_w_in', 'l0_ml_b_if', 'l0_ml_head_gain', 'l0_ml_w_out', 'l0_norm_ffn',
        'l0_ffn_w_gate', 'l0_ffn_w_up', 'l0_ffn_w_down', 'l1_norm_mix', 'l1_gdn_w_in', 'l1_gdn_conv',
        'l1_gdn_a_log', 'l1_gdn_dt_bias', 'l1_gdn_out_gain', 'l1_gdn_w_out', 'l1_norm_ffn', 'l1_moe_router',
        'l1_moe_w_gate', 'l1_moe_w_up', 'l1_moe_w_down', 'final_norm']


def kernel(**inputs):
    import numpy as _np
    import concourse.bacc as _bacc
    from concourse import mybir as _mybir
    from concourse.bass_utils import run_bass_kernel_spmd as _run

    nc = _bacc.Bacc("TRN2", target_bir_lowering=False, num_devices=1,
                     dynamic_dma_scratch_size=512)
    arrays, args = {}, {}
    for name in _INS:
        a = _np.ascontiguousarray(inputs[name])
        arrays[f"in_{name}"] = a
        args[name] = nc.dram_tensor(f"in_{name}", a.shape, _mybir.dt.from_np(a.dtype), kind="ExternalInput").ap()
    out = nc.dram_tensor("out_dram", (1, S, D), _mybir.dt.float32, kind="ExternalOutput").ap()
    bass_hybrid_trunk(nc, out, args)
    r = _run(nc, [arrays], core_ids=[0])
    return r.results[0]["out_dram"]
```
